# Optimizing a Trainium2 kernel written in Bass

```python
import math
import jax, jax.numpy as jnp
from jax import lax
import numpy as np

D_MODEL = 2048
BATCH = 1
SEQ = 512
DEPTH = 1
DEC_BATCH = 8
DEC_SEQ = 4
PAST_LEN = 2048
PAGE_SIZE = 128

N_HEADS = 8
N_KV_HEADS = 4
Q_PER_KV = N_HEADS // N_KV_HEADS
HEAD_DIM = 64
ROT_DIM = HEAD_DIM // 4
ROPE_THETA = 500000.0
Q_BLOCK = 128
ATT_WIDTH = N_HEADS * 2 * HEAD_DIM
KV_WIDTH = N_KV_HEADS * 2 * HEAD_DIM
LRU_WIDTH = 1024
LRU_BLOCKS = 8
LRU_BLOCK_W = LRU_WIDTH // LRU_BLOCKS
CONV_W = 4
LRU_C = 8.0
N_KEYS = 128
N_EXPERTS = N_KEYS * N_KEYS
PEER_HEADS = 8
PEER_TOPK = 16
PEER_KEY_DIM = 256
PEER_HALF = PEER_KEY_DIM // 2
PEER_POS_BLOCK = 128
RMS_EPS = 1e-6
OFF_Q = ATT_WIDTH
OFF_K = OFF_Q + KV_WIDTH
OFF_V = OFF_K + KV_WIDTH
OFF_L = OFF_V + LRU_WIDTH
OFF_GA = OFF_L + D_MODEL
IN_WIDTH = OFF_GA + D_MODEL

kernel_name = 'hybrid_diffattn_rglru_peer_step'

F32 = jnp.float32

def rms_norm(x, g):
    xf = x.astype(F32)
    var = jnp.mean(xf * xf, axis=-1, keepdims=True)
    return (xf * lax.rsqrt(var + RMS_EPS) * g.astype(F32)).astype(x.dtype)

def partial_rope(t, pos):
    half = ROT_DIM // 2
    inv_freq = jnp.float32(ROPE_THETA) ** (-jnp.arange(half, dtype=F32) * 2.0 / ROT_DIM)
    ang = pos.astype(F32)[:, None] * inv_freq[None, :]
    cos = jnp.cos(ang)[None, :, None, None, :]
    sin = jnp.sin(ang)[None, :, None, None, :]
    tr = t[..., :ROT_DIM].astype(F32)
    t1, t2 = tr[..., :half], tr[..., half:]
    rot = jnp.concatenate([t1 * cos - t2 * sin, t2 * cos + t1 * sin], axis=-1).astype(t.dtype)
    return jnp.concatenate([rot, t[..., ROT_DIM:]], axis=-1)

def _project(xn, pos, w_in):
    b, t, _ = xn.shape
    proj = xn @ w_in
    q, k, v, xl, ga, gl = jnp.split(proj, [OFF_Q, OFF_K, OFF_V, OFF_L, OFF_GA], axis=-1)
    q = partial_rope(q.reshape(b, t, N_HEADS, 2, HEAD_DIM), pos)
    q = q.reshape(b, t, N_KV_HEADS, Q_PER_KV, 2, HEAD_DIM)
    k = partial_rope(k.reshape(b, t, N_KV_HEADS, 2, HEAD_DIM), pos)
    v = v.reshape(b, t, N_KV_HEADS, 2 * HEAD_DIM)
    return q, k, v, xl, ga, gl

def _diff_attend(q, k, v, mask, lam):
    s = jnp.einsum('bqgrcd,bkgcd->bgrcqk', q.astype(F32), k.astype(F32)) * (HEAD_DIM ** -0.5)
    s = jnp.where(mask, s, -jnp.inf)
    p = jax.nn.softmax(s, axis=-1)
    w = p[:, :, :, 0] - lam * p[:, :, :, 1]
    return jnp.einsum('bgrqk,bkgv->bqgrv', w, v.astype(F32))

def _attn_out(att, p, lam_init, dtype):
    b, t = att.shape[0], att.shape[1]
    att = rms_norm(att, p['subln_g']).astype(F32) * (1.0 - lam_init)
    return att.reshape(b, t, ATT_WIDTH).astype(dtype)

def _causal_conv(x_ext, w, b):
    t = x_ext.shape[1] - (CONV_W - 1)
    out = x_ext[:, 0:t] * w[0]
    for j in range(1, CONV_W):
        out = out + x_ext[:, j:j + t] * w[j]
    return out + b

def _lru_branch(xl_ext, h0, p):
    xc = _causal_conv(xl_ext, p['conv_w'], p['conv_b'])
    b, t, c = xc.shape
    xb = xc.reshape(b, t, LRU_BLOCKS, LRU_BLOCK_W)
    r = jax.nn.sigmoid(jnp.einsum('btni,nij->btnj', xb, p['lru_wa']).reshape(b, t, c) + p['lru_ba'])
    i = jax.nn.sigmoid(jnp.einsum('btni,nij->btnj', xb, p['lru_wx']).reshape(b, t, c) + p['lru_bx'])
    log_a = -LRU_C * r.astype(F32) * jax.nn.softplus(-p['lru_lambda'].astype(F32))
    a = jnp.exp(log_a)
    u = jnp.sqrt(-jnp.expm1(2.0 * log_a)) * (i * xc).astype(F32)

    def step(h, au):
        a_t, u_t = au
        h = a_t * h + u_t
        return h, h

    h_t, hs = lax.scan(step, h0.astype(F32), (jnp.swapaxes(a, 0, 1), jnp.swapaxes(u, 0, 1)))
    conv_state = xl_ext[:, -(CONV_W - 1):]
    return jnp.swapaxes(hs, 0, 1).astype(xc.dtype), conv_state, h_t.astype(h0.dtype)

def _merge(att, lru, ga, gl, p):
    m = jax.nn.sigmoid(ga) * (att @ p['w_att_up']) + jax.nn.sigmoid(gl) * (lru @ p['w_lru_up'])
    return m @ p['w_out']

def _peer(xt, p):
    t = xt.shape[0]
    q = (xt @ p['peer_wq']).astype(F32).reshape(t, PEER_HEADS, 2, PEER_HALF)
    s1 = jnp.einsum('thd,nd->thn', q[:, :, 0], p['peer_k1'].astype(F32))
    s2 = jnp.einsum('thd,nd->thn', q[:, :, 1], p['peer_k2'].astype(F32))
    v1, i1 = lax.top_k(s1, PEER_TOPK)
    v2, i2 = lax.top_k(s2, PEER_TOPK)
    cand = (v1[..., :, None] + v2[..., None, :]).reshape(t, PEER_HEADS, PEER_TOPK * PEER_TOPK)
    cid = (i1[..., :, None] * N_KEYS + i2[..., None, :]).reshape(t, PEER_HEADS, PEER_TOPK * PEER_TOPK)
    best, sel = lax.top_k(cand, PEER_TOPK)
    eid = jnp.take_along_axis(cid, sel, axis=-1).reshape(t, PEER_HEADS * PEER_TOPK)
    gate = jax.nn.softmax(best, axis=-1).reshape(t, PEER_HEADS * PEER_TOPK)
    u = p['peer_u'][eid]
    act = jax.nn.gelu(jnp.einsum('tkd,td->tk', u, xt).astype(F32), approximate=False)
    coef = (gate * act).astype(xt.dtype)
    return jnp.einsum('tk,tkd->td', coef, p['peer_v'][eid])

def _layer_prompt(x, p, lam, lam_init):
    b, t, _ = x.shape
    xn = rms_norm(x, p['norm1_g'])
    pos = jnp.arange(t, dtype=jnp.int32)
    q, k, v, xl, ga, gl = _project(xn, pos, p['w_in'])
    nb = t // Q_BLOCK
    qb = jnp.moveaxis(q.reshape(b, nb, Q_BLOCK, N_KV_HEADS, Q_PER_KV, 2, HEAD_DIM), 1, 0)
    kpos = jnp.arange(t, dtype=jnp.int32)

    def block(args):
        q_blk, bi = args
        qpos = bi * Q_BLOCK + jnp.arange(Q_BLOCK, dtype=jnp.int32)
        return _diff_attend(q_blk, k, v, kpos[None, :] <= qpos[:, None], lam)

    att = lax.map(block, (qb, jnp.arange(nb, dtype=jnp.int32)))
    att = jnp.moveaxis(att, 0, 1).reshape(b, t, N_HEADS, 2 * HEAD_DIM)
    att = _attn_out(att, p, lam_init, x.dtype)
    xl_ext = jnp.concatenate([jnp.zeros((b, CONV_W - 1, LRU_WIDTH), xl.dtype), xl], axis=1)
    h0 = jnp.zeros((b, LRU_WIDTH), x.dtype)
    lru, conv_state, h_t = _lru_branch(xl_ext, h0, p)
    h = x + _merge(att, lru, ga, gl, p)
    xn2 = rms_norm(h, p['norm2_g'])
    nbp = t // PEER_POS_BLOCK
    xb = xn2.reshape(b, nbp, PEER_POS_BLOCK, D_MODEL).transpose(1, 0, 2, 3).reshape(nbp, b * PEER_POS_BLOCK, D_MODEL)
    ffn = lax.map(lambda z: _peer(z, p), xb)
    ffn = ffn.reshape(nbp, b, PEER_POS_BLOCK, D_MODEL).transpose(1, 0, 2, 3).reshape(b, t, D_MODEL)
    k_rows = k.reshape(b, t, N_KV_HEADS, 2 * HEAD_DIM)
    return h + ffn, k_rows, v, conv_state, h_t

def _layer_sample(x, k_past, v_past, conv_buf, h0, p, lam, lam_init):
    b, t, _ = x.shape
    xn = rms_norm(x, p['norm1_g'])
    pos = PAST_LEN + jnp.arange(t, dtype=jnp.int32)
    q, k, v, xl, ga, gl = _project(xn, pos, p['w_in'])
    k_all = jnp.concatenate([k_past.reshape(b, PAST_LEN, N_KV_HEADS, 2, HEAD_DIM).astype(k.dtype), k], axis=1)
    v_all = jnp.concatenate([v_past.astype(v.dtype), v], axis=1)
    kpos = jnp.arange(PAST_LEN + t, dtype=jnp.int32)
    att = _diff_attend(q, k_all, v_all, kpos[None, :] <= pos[:, None], lam)
    att = _attn_out(att.reshape(b, t, N_HEADS, 2 * HEAD_DIM), p, lam_init, x.dtype)
    xl_ext = jnp.concatenate([conv_buf.astype(xl.dtype), xl], axis=1)
    lru, conv_state, h_t = _lru_branch(xl_ext, h0, p)
    h = x + _merge(att, lru, ga, gl, p)
    xn2 = rms_norm(h, p['norm2_g'])
    ffn = _peer(xn2.reshape(b * t, D_MODEL), p).reshape(b, t, D_MODEL)
    k_rows = k.reshape(b, t, N_KV_HEADS, 2 * HEAD_DIM)
    return h + ffn, k_rows, v, conv_state, h_t

def setup_inputs(seed: int = 0) -> dict:
    key = jax.random.key(seed)
    ks = jax.random.split(key, 32)
    n_pages = PAST_LEN // PAGE_SIZE
    n_used = DEC_BATCH * n_pages
    n_pool = (n_used * 5 + 3) // 4
    nrm = lambda k, shape, s: jax.random.normal(k, shape, F32) * s
    a0 = jax.random.uniform(ks[13], (DEPTH, LRU_WIDTH), F32, minval=0.9, maxval=0.999)
    s0 = a0 ** (1.0 / LRU_C)
    page_table = jax.random.permutation(ks[6], n_pool)[:n_used].reshape(DEC_BATCH, n_pages).astype(jnp.int32)
    return {
        'x_prompt': nrm(ks[0], (BATCH, SEQ, D_MODEL), 1.0),
        'x_sample': nrm(ks[1], (DEC_BATCH, DEC_SEQ, D_MODEL), 1.0),
        'cache_k': nrm(ks[2], (DEPTH, n_pool, PAGE_SIZE, N_KV_HEADS, 2 * HEAD_DIM), 1.0),
        'cache_v': nrm(ks[3], (DEPTH, n_pool, PAGE_SIZE, N_KV_HEADS, 2 * HEAD_DIM), 1.0),
        'state_conv': nrm(ks[4], (DEPTH, DEC_BATCH, CONV_W - 1, LRU_WIDTH), 1.0),
        'state_h': nrm(ks[5], (DEPTH, DEC_BATCH, LRU_WIDTH), 0.5),
        'page_table': page_table,
        'norm1_g': 1.0 + nrm(ks[7], (DEPTH, D_MODEL), 0.02),
        'w_in': nrm(ks[8], (DEPTH, D_MODEL, IN_WIDTH), D_MODEL ** -0.5),
        'lambda_q1': nrm(ks[9], (DEPTH, HEAD_DIM), 0.1),
        'lambda_k1': nrm(ks[10], (DEPTH, HEAD_DIM), 0.1),
        'lambda_q2': nrm(ks[11], (DEPTH, HEAD_DIM), 0.1),
        'lambda_k2': nrm(ks[12], (DEPTH, HEAD_DIM), 0.1),
        'subln_g': 1.0 + nrm(ks[14], (DEPTH, 2 * HEAD_DIM), 0.02),
        'conv_w': nrm(ks[15], (DEPTH, CONV_W, LRU_WIDTH), CONV_W ** -0.5),
        'conv_b': nrm(ks[16], (DEPTH, LRU_WIDTH), 0.01),
        'lru_wa': nrm(ks[17], (DEPTH, LRU_BLOCKS, LRU_BLOCK_W, LRU_BLOCK_W), LRU_BLOCK_W ** -0.5),
        'lru_ba': nrm(ks[18], (DEPTH, LRU_WIDTH), 0.01),
        'lru_wx': nrm(ks[19], (DEPTH, LRU_BLOCKS, LRU_BLOCK_W, LRU_BLOCK_W), LRU_BLOCK_W ** -0.5),
        'lru_bx': nrm(ks[20], (DEPTH, LRU_WIDTH), 0.01),
        'lru_lambda': jnp.log(s0) - jnp.log1p(-s0),
        'w_att_up': nrm(ks[21], (DEPTH, ATT_WIDTH, D_MODEL), ATT_WIDTH ** -0.5),
        'w_lru_up': nrm(ks[22], (DEPTH, LRU_WIDTH, D_MODEL), LRU_WIDTH ** -0.5),
        'w_out': nrm(ks[23], (DEPTH, D_MODEL, D_MODEL), D_MODEL ** -0.5),
        'norm2_g': 1.0 + nrm(ks[24], (DEPTH, D_MODEL), 0.02),
        'peer_wq': nrm(ks[25], (DEPTH, D_MODEL, PEER_HEADS * PEER_KEY_DIM), D_MODEL ** -0.5),
        'peer_k1': nrm(ks[26], (DEPTH, N_KEYS, PEER_HALF), PEER_HALF ** -0.5),
        'peer_k2': nrm(ks[27], (DEPTH, N_KEYS, PEER_HALF), PEER_HALF ** -0.5),
        'peer_u': nrm(ks[28], (DEPTH, N_EXPERTS, D_MODEL), D_MODEL ** -0.5),
        'peer_v': nrm(ks[29], (DEPTH, N_EXPERTS, D_MODEL), PEER_HEADS ** -0.5),
        'final_g': 1.0 + nrm(ks[30], (D_MODEL,), 0.02),
    }

def reference(x_prompt, x_sample, cache_k, cache_v, state_conv, state_h, page_table,
              norm1_g, w_in, lambda_q1, lambda_k1, lambda_q2, lambda_k2, subln_g,
              conv_w, conv_b, lru_wa, lru_ba, lru_wx, lru_bx, lru_lambda,
              w_att_up, w_lru_up, w_out, norm2_g, peer_wq, peer_k1, peer_k2, peer_u, peer_v, final_g):
    hp, hs = x_prompt, x_sample
    kp_l, vp_l, cp_l, hp_l, ks_l, vs_l, cs_l, hs_l = [], [], [], [], [], [], [], []
    for l in range(DEPTH):
        p = {
            'norm1_g': norm1_g[l], 'w_in': w_in[l], 'subln_g': subln_g[l],
            'conv_w': conv_w[l], 'conv_b': conv_b[l], 'lru_wa': lru_wa[l], 'lru_ba': lru_ba[l],
            'lru_wx': lru_wx[l], 'lru_bx': lru_bx[l], 'lru_lambda': lru_lambda[l],
            'w_att_up': w_att_up[l], 'w_lru_up': w_lru_up[l], 'w_out': w_out[l], 'norm2_g': norm2_g[l],
            'peer_wq': peer_wq[l], 'peer_k1': peer_k1[l], 'peer_k2': peer_k2[l],
            'peer_u': peer_u[l], 'peer_v': peer_v[l],
        }
        lam_init = 0.8 - 0.6 * math.exp(-0.3 * l)
        lam = (jnp.exp(jnp.sum(lambda_q1[l].astype(F32) * lambda_k1[l].astype(F32)))
               - jnp.exp(jnp.sum(lambda_q2[l].astype(F32) * lambda_k2[l].astype(F32))) + lam_init)
        hp, kp, vp, cp, hpt = _layer_prompt(hp, p, lam, lam_init)
        k_past = cache_k[l, page_table]
        v_past = cache_v[l, page_table]
        b = x_sample.shape[0]
        k_past = k_past.reshape(b, PAST_LEN, N_KV_HEADS, 2 * HEAD_DIM)
        v_past = v_past.reshape(b, PAST_LEN, N_KV_HEADS, 2 * HEAD_DIM)
        hs, kn, vn, cn, hst = _layer_sample(hs, k_past, v_past, state_conv[l], state_h[l], p, lam, lam_init)
        kp_l.append(kp); vp_l.append(vp); cp_l.append(cp); hp_l.append(hpt)
        ks_l.append(kn); vs_l.append(vn); cs_l.append(cn); hs_l.append(hst)
    y_prompt = rms_norm(hp, final_g)
    y_sample = rms_norm(hs, final_g)
    return (y_prompt, y_sample,
            jnp.stack(kp_l), jnp.stack(vp_l), jnp.stack(cp_l), jnp.stack(hp_l),
            jnp.stack(ks_l), jnp.stack(vs_l), jnp.stack(cs_l), jnp.stack(hs_l))


_drawn_inputs = setup_inputs


def setup_inputs(seed=0):
    import zlib

    import numpy as np

    out = dict(_drawn_inputs(seed))
    spreads = {}
    factors = {'lambda_q1': 3.768,
     'lambda_k1': 5.401,
     'subln_g': 7.709,
     'lru_ba': 25.713,
     'lru_bx': 8.0,
     'final_g': 7.602,
     'lambda_k2': 3.091,
     'norm2_g': 3.387}
    for name, (base, spread) in spreads.items():
        noise = np.random.default_rng([zlib.crc32(name.encode()), seed]).standard_normal(out[name].shape)
        drawn = base * np.exp(spread * noise) if base else spread * noise
        out[name] = __import__('jax').numpy.asarray(drawn.astype(out[name].dtype))
    for name, factor in factors.items():
        out[name] = (out[name] * factor).astype(out[name].dtype)
    return out
```

```python
from contextlib import ExitStack, contextmanager

import numpy as np

import concourse.bass as bass
from concourse import mybir

F32 = mybir.dt.float32
I32 = mybir.dt.int32
U32 = mybir.dt.uint32
ALU = mybir.AluOpType
ACT = mybir.ActivationFunctionType
AX = mybir.AxisListType

P = 128
D = 2048
DC = D // P
SEQ, NB, NT = 512, 8, 4
TB = SEQ // P
NS = NB * NT
T = SEQ + NS
HALF = T // 2
NH, NG, HD = 8, 4, 64
AC = NH
LW, LB = 1024, 8
CW = 4
PAST, PAGE = 2048, 128
NK, PH, TOPK = 128, 8, 16
SLOTS = PH * TOPK
EPS = 1e-6
LAM_INIT = 0.8 - 0.6 * float(np.exp(-0.3 * 0))
HC = 256
COL_Q, COL_K, COL_V, COL_L, COL_GA, COL_GL = 0, 1024, 1536, 2048, 3072, 5120
NEG = -1e30

C_ID, C_CAUSAL, C_NEW, C_COMB, C_CS, C_ISC, C_REP, C_IOTA, C_ONE, C_PAGE, C_SEL = (
    0, 128, 256, 384, 448, 528, 530, 562, 578, 706, 707)
C_END = 723


def shape_constants():
    c = np.zeros((P, C_END), np.float32)
    p = np.arange(P)
    c[:, C_ID:C_ID + P] = np.eye(P)
    c[:, C_CAUSAL:C_CAUSAL + P] = np.where(p[None, :] <= p[:, None], 0.0, NEG)
    bb, g, comp, r, t = p // 64, p // 16 % 4, p // 8 % 2, p // 4 % 2, p % 4
    key = np.arange(NS)
    for pair in range(NB // 2):
        seen = (key[None, :] // NT == (2 * pair + bb)[:, None]) & (key[None, :] % NT <= t[:, None])
        c[:, C_NEW + NS * pair:C_NEW + NS * (pair + 1)] = np.where(seen, 0.0, NEG)
    c[p, C_COMB + bb * 32 + g * 8 + r * 4 + t] = 1.0
    inv = np.float32(500000.0) ** (-np.arange(8, dtype=np.float32) * np.float32(2.0) / np.float32(16))
    for tb in range(TB + 1):
        pos = (tb * P + p if tb < TB else PAST + p % NT).astype(np.float32)
        ang = (pos[:, None] * inv[None, :]).astype(np.float32)
        c[:, C_CS + 16 * tb:C_CS + 16 * tb + 8] = np.cos(ang)
        c[:, C_CS + 16 * tb + 8:C_CS + 16 * tb + 16] = np.sin(ang)
    c[:, C_ISC] = comp == 0
    c[:, C_ISC + 1] = comp == 1
    c[p, C_REP + p % NS] = 1.0
    c[:, C_IOTA:C_IOTA + 16] = np.arange(16)
    c[:, C_ONE:C_ONE + P] = 1.0
    c[:, C_PAGE] = 2 * (p % 8)
    c[p, C_SEL + p // 8] = 1.0
    return c


class Steps:

    def __init__(self, eng, sem):
        self.eng, self.sem, self.base, self.n = eng, sem, 0, 0

    def did(self, ins):
        ins.then_inc(self.sem, 1)
        self.n += 1
        return ins

    def settle(self):
        self.eng.wait_ge(self.sem, self.base + self.n)

    @contextmanager
    def loop(self, trips, per):
        start = self.base + self.n
        with self.eng.Fori(0, trips) as i:
            self.base, self.n = start + i * per, 0
            yield i
            assert self.n == per, (self.n, per)
        self.base, self.n = start + trips * per, 0


def build_trunk(nc, io, upto=99):
    with ExitStack() as ctx:
        def sem(name):
            return ctx.enter_context(nc.semaphore(name))

        AREA = 53100
        area = ctx.enter_context(nc.sbuf_tensor("area", [P, AREA], F32))
        PS = ctx.enter_context(nc.psum_tensor("PS", [P, 8, 512], F32))

        def at(off, words, spec=None, **dims):
            assert off + words <= AREA
            v = area[:, off:off + words]
            return v.rearrange(spec, **dims) if spec else v

        W_AT, X_AT, A_AT, L_AT, M_AT = 0, 16384, 25088, 29440, 33792
        R_AT = M_AT + 8704
        K_AT = AREA - 1500
        W = at(W_AT, 16384, "p (s k n) -> p s k n", s=4, k=DC)
        xnT = at(X_AT, DC * T, "p (k t) -> p k t", k=DC)
        attT = at(A_AT, AC * T, "p (h t) -> p h t", h=AC)
        lruT = at(L_AT, LB * T, "p (n t) -> p n t", n=LB)
        mT = at(M_AT, DC * T, "p (k t) -> p k t", k=DC)

        const = at(K_AT, C_END)
        ident, causal = const[:, C_ID:C_ID + P], const[:, C_CAUSAL:C_CAUSAL + P]
        ones = const[:, C_ONE:C_ONE + P]
        small_at = [K_AT + C_END]

        def small(words, spec=None, **dims):
            small_at[0] += words
            return at(small_at[0] - words, words, spec, **dims)

        prmT = small(LB * 40, "p (n c) -> p n c", n=LB)
        gT = small(33)
        ssq = small(5)
        rstd = small(5)
        lam2 = small(2)
        neglam = small(1)
        csel = small(1)
        sp8 = small(LB)
        rowidx = small(2 * NB).bitcast(I32)
        stats = small(64)

        xs = at(M_AT, 5 * D, "p (b n) -> p b n", b=5)
        junk = at(L_AT, 2 * D, "p (b n) -> p b n", b=2)
        prm = at(44100, LW)
        gains = at(45200, P)
        lamq = at(45400, 4 * HD, "p (a d) -> p a d", a=4)
        lamp = at(45700, 2 * HD, "p (a d) -> p a d", a=2)
        pt = at(45900, 16 * NB).bitcast(I32)
        ptm = at(46130, 16 * NB)
        sp = at(46000, 8 * LB, "p (a n) -> p a n", a=8)
        ptf = at(46300, 3 * NB, "p (a n) -> p a n", a=3)

        def rows(tb):
            return P if tb < TB else NS

        steps_v = Steps(nc.vector, sem("vector_steps"))
        steps_g = Steps(nc.gpsimd, sem("pool_steps"))
        held = {e.engine: sem(f"held_{n}") for n, e in enumerate((nc.vector, nc.scalar, nc.gpsimd, nc.tensor, nc.sync))}

        def settle_apart(steps):
            wait_apart(steps.eng, steps.sem, steps.base + steps.n)

        def wait_apart(eng, s, value):
            eng.wait_ge(s, value)
            eng.sem_inc(held[eng.engine], 1)

        out_done = sem("out_done")
        outs = [0]

        def store(eng, dst, src):
            eng.dma_start(dst, src).then_inc(out_done, 16)
            outs[0] += 1

        w_in = io["w_in"][0].rearrange("(k p) n -> p k n", p=P)

        s_const, s_prm, s_lamq, s_pt = sem("const_in"), sem("prm_in"), sem("lamq_in"), sem("pages_in")
        s_x = [sem(f"x_in{tb}") for tb in range(5)]
        s_sq, s_ms, s_root = sem("squares"), sem("mean_squares"), sem("root")
        s_xs, s_tr, s_ev_a, s_ev_v = sem("x_scaled"), sem("x_transposed"), sem("evac_scalar"), sem("evac_vector")
        s_gT, s_gTe, s_pT, s_pTe = sem("gains_tr"), sem("gains_ready"), sem("prm_tr"), sem("prm_ready")
        w_in_sem = [sem(f"w_slot{s}_in") for s in range(4)]
        s_lamw = sem("lam_parts")
        s_lame = sem("lam_exp")
        s_spl = [sem(f"softplus_{k}") for k in range(4)]

        def transposed_norm(k, src, dstT, gcol):
            nbank = 4 * 5

            def squares(act):
                if k == 0:
                    act.wait_ge(s_spl[3], 1)
                for tb in range(5):
                    if k == 0:
                        act.wait_ge(s_x[tb], 16)
                    if tb >= 2:
                        act.wait_ge(s_sq, 5 * k + tb - 1)
                    act.activation(junk[:rows(tb), tb % 2, :], src[:rows(tb), tb, :], ACT.Square,
                                   accum_out=ssq[:rows(tb), tb:tb + 1]).then_inc(s_sq, 1)
                act.wait_ge(s_ms, k + 1)
                act.activation(rstd, rstd, ACT.Sqrt).then_inc(s_root, 1)

            def evac_scalar(act):
                act.wait_ge(s_gTe, 1)
                for n in range(0, nbank, 2):
                    tb, q, np_ = n // 4, n % 4, rows(n // 4)
                    act.wait_ge(s_tr, nbank * k + n + 1)
                    for j in range(4):
                        d = 4 * q + j
                        ins = act.activation(dstT[:, d, tb * P:tb * P + np_], PS[:, n % 4, j * P:j * P + np_],
                                             ACT.Copy, scale=gT[:, gcol + d:gcol + d + 1])
                    ins.then_inc(s_ev_a, 1)

            def scale(v):
                v.wait_ge(s_sq, 5 * (k + 1))
                v.tensor_scalar(rstd, ssq, 1.0 / D, EPS, ALU.mult, ALU.add).then_inc(s_ms, 1)
                v.wait_ge(s_root, k + 1)
                steps_v.did(v.reciprocal(rstd, rstd))
                steps_v.settle()

            def scale_block(v, tb, dst):
                v.tensor_scalar(dst, src[:rows(tb), tb, :], rstd[:rows(tb), tb:tb + 1], None,
                                ALU.mult).then_inc(s_xs, 1)

            def evac_vector(v, tb):
                for n in (4 * tb + 1, 4 * tb + 3):
                    q, np_ = n % 4, rows(tb)
                    v.wait_ge(s_tr, nbank * k + n + 1)
                    for j in range(4):
                        d = 4 * q + j
                        ins = v.tensor_scalar(dstT[:, d, tb * P:tb * P + np_], PS[:, n % 4, j * P:j * P + np_],
                                              gT[:, gcol + d:gcol + d + 1], None, ALU.mult)
                    ins.then_inc(s_ev_v, 1)

            def turn(pe, tb, block):
                pe.wait_ge(s_xs, 5 * k + tb + 1)
                for q in range(4):
                    n = 4 * tb + q
                    if n >= 4:
                        pe.wait_ge((s_ev_a, s_ev_v)[n % 2], (nbank // 2) * k + (n - 4) // 2 + 1)
                    for j in range(4):
                        d = 4 * q + j
                        ins = pe.transpose(PS[:, n % 4, j * P:j * P + rows(tb)], block[:, d * P:(d + 1) * P],
                                           ident[:rows(tb), :rows(tb)])
                    ins.then_inc(s_tr, 1)

            return squares, evac_scalar, scale, scale_block, evac_vector, turn

        wab = at(A_AT + 1088, 2 * 256, "p (a m j) -> p a m j", a=2, m=2)
        s_wab = [sem(f"lru_w{a}_in") for a in range(2)]
        landed = [0, 0, 0, 0]

        def load_w(sp_, a, src):
            sp_.dma_start(W[:, a], src).then_inc(w_in_sem[a], 16)

        def load_gates(sp_, a, n):
            for m, name in enumerate(("lru_wa", "lru_wx")):
                sp_.dma_start(wab[:, a, m, :], io[name].rearrange("l n i j -> (l n) i j")[n]).then_inc(s_wab[a], 16)

        squares, evac_scalar, scale, scale_block, evac_vector, turn = transposed_norm(0, xs, xnT, 0)
        xp = io["x_prompt"][0].rearrange("(b p) d -> b p d", p=P)
        xsm = io["x_sample"].rearrange("b t d -> (b t) d")

        with nc.Block() as block:
            @block.sync
            def _(sp_):
                for tb in range(5):
                    sp_.dma_start(xs[:rows(tb), tb, :], xp[tb] if tb < TB else xsm).then_inc(s_x[tb], 16)
                    if tb == 0:
                        sp_.dma_start(const, io["const"]).then_inc(s_const, 16)
                        sp_.dma_start(gains[0:16, :], io["norm1_g"][0].rearrange("(k p) -> k p", p=P)).then_inc(s_prm, 16)
                        sp_.dma_start(gains[16:32, :], io["norm2_g"][0].rearrange("(k p) -> k p", p=P)).then_inc(s_prm, 16)
                        sp_.dma_start(gains[32:33, :], io["subln_g"]).then_inc(s_prm, 16)
                for a in range(2):
                    load_w(sp_, a, w_in[:, :, COL_L + HC * a:COL_L + HC * (a + 1)])
                for a in range(2):
                    load_gates(sp_, a, a)

            @block.scalar
            def _(act):
                act.dma_start(prm[0:24, :], io["state_conv"][0].rearrange("b j c -> (b j) c")).then_inc(s_prm, 16)
                act.dma_start(prm[24:32, :], io["state_h"][0]).then_inc(s_prm, 16)
                act.dma_start(prm[32:36, :], io["conv_w"][0]).then_inc(s_prm, 16)
                for r, name in enumerate(("conv_b", "lru_ba", "lru_bx", "lru_lambda")):
                    act.dma_start(prm[36 + r:37 + r, :], io[name]).then_inc(s_prm, 16)
                for r, name in enumerate(("lambda_q1", "lambda_k1", "lambda_q2", "lambda_k2")):
                    act.dma_start(lamq[:, r, :], io[name][0].partition_broadcast(P)).then_inc(s_lamq, 16)
                pages = io["page_table"]
                act.dma_start(pt, pages.rearrange("b g -> (b g)").partition_broadcast(P)).then_inc(s_pt, 16)
                squares(act)
                act.wait_ge(s_lamw, 1)
                act.activation(lam2, stats[:, 0:2], ACT.Exp).then_inc(s_lame, 1)
                evac_scalar(act)
                act.wait_ge(s_spl[0], 1)
                act.activation(sp[:, 1, :], sp[:, 0, :], ACT.Exp, scale=-1.0).then_inc(s_spl[1], 1)

            @block.vector
            def _(v):
                v.memset(ssq, 1.0).then_inc(s_spl[3], 1)
                scale(v)
                v.wait_ge(s_lamq, 64)
                for a in range(2):
                    ins = v.tensor_tensor_reduce(lamp[:, a, :], lamq[:, 2 * a, :], lamq[:, 2 * a + 1, :], 1.0, 0.0,
                                                 ALU.mult, ALU.add, stats[:, a:a + 1])
                ins.then_inc(s_lamw, 1)
                for tb in range(5):
                    scale_block(v, tb, xs[:rows(tb), tb, :])
                v.wait_ge(s_gT, 1)
                v.tensor_copy(gT, PS[:, 7, 0:33]).then_inc(s_gTe, 1)
                v.wait_ge(s_pT, 1)
                v.tensor_copy(prmT, PS[:, 6, 0:320].rearrange("p (n c) -> p n c", n=LB)).then_inc(s_pTe, 1)
                v.wait_ge(s_pTe, 1)
                for tb in range(5):
                    evac_vector(v, tb)
                v.wait_ge(s_lame, 1)
                steps_v.did(v.tensor_tensor(neglam, lam2[:, 1:2], lam2[:, 0:1], ALU.subtract))
                steps_v.settle()
                steps_v.did(v.tensor_scalar(neglam, neglam, -LAM_INIT, None, ALU.add))
                steps_v.settle()
                steps_v.did(v.scalar_tensor_tensor(csel, const[:, C_ISC + 1:C_ISC + 2], neglam,
                                                   const[:, C_ISC:C_ISC + 1], ALU.mult, ALU.add))
                v.wait_ge(s_pt, 16)
                steps_v.did(v.tensor_tensor(ptm.rearrange("p (b g) -> p b g", b=NB), pt.rearrange("p (b g) -> p b g", b=NB),
                                            const[:, C_SEL:C_SEL + 16].unsqueeze(1).broadcast_to([P, NB, 16]), ALU.mult))
                steps_v.settle()
                steps_v.did(v.tensor_reduce(ptf[:, 0, :], ptm.rearrange("p (b g) -> p b g", b=NB), AX.X, ALU.add))
                steps_v.settle()
                steps_v.did(v.tensor_scalar(ptf[:, 1, :], ptf[:, 0, :], 16.0, const[:, C_PAGE:C_PAGE + 1],
                                            ALU.mult, ALU.add))
                steps_v.settle()
                steps_v.did(v.tensor_scalar(ptf[:, 2, :], ptf[:, 1, :], 1.0, None, ALU.add))
                steps_v.settle()
                steps_v.did(v.tensor_copy(rowidx[:, 0:NB], ptf[:, 1, :]))
                steps_v.did(v.tensor_copy(rowidx[:, NB:2 * NB], ptf[:, 2, :]))
                lam = prmT[:, :, 39]
                steps_v.did(v.tensor_scalar(sp[:, 0, :], lam, -1.0, None, ALU.mult))
                steps_v.settle()
                v.tensor_tensor(sp[:, 0, :], sp[:, 0, :], lam, ALU.max).then_inc(s_spl[0], 1)
                steps_v.did(v.tensor_scalar(sp[:, 7, :], lam, -1.0, 0.0, ALU.mult, ALU.max))
                v.wait_ge(s_spl[1], 1)
                steps_v.did(v.tensor_scalar(sp[:, 2, :], sp[:, 1, :], 2.0, None, ALU.add))
                steps_v.settle()
                steps_v.did(v.reciprocal(sp[:, 2, :], sp[:, 2, :]))
                steps_v.settle()
                steps_v.did(v.tensor_tensor(sp[:, 2, :], sp[:, 2, :], sp[:, 1, :], ALU.mult))
                steps_v.settle()
                steps_v.did(v.tensor_tensor(sp[:, 3, :], sp[:, 2, :], sp[:, 2, :], ALU.mult))
                steps_v.settle()
                steps_v.did(v.tensor_scalar(sp[:, 4, :], sp[:, 3, :], 1.0 / 17, 1.0 / 15, ALU.mult, ALU.add))
                for k in range(13, 0, -2):
                    steps_v.settle()
                    steps_v.did(v.tensor_tensor(sp[:, 4, :], sp[:, 4, :], sp[:, 3, :], ALU.mult))
                    steps_v.settle()
                    steps_v.did(v.tensor_scalar(sp[:, 4, :], sp[:, 4, :], 1.0 / k, None, ALU.add))
                steps_v.settle()
                steps_v.did(v.scalar_tensor_tensor(sp[:, 5, :], sp[:, 4, :], 2.0, sp[:, 2, :], ALU.mult, ALU.mult))
                steps_v.settle()
                steps_v.did(v.tensor_tensor(sp[:, 6, :], sp[:, 5, :], sp[:, 7, :], ALU.add))
                steps_v.settle()
                steps_v.did(v.tensor_scalar(sp8, sp[:, 6, :], -8.0, None, ALU.mult))

            @block.tensor
            def _(pe):
                pe.wait_ge(s_const, 16)
                pe.wait_ge(s_prm, 16 * 10)
                pe.transpose(PS[:, 7, 0:33], gains[0:33, :], ident[0:33, 0:33]).then_inc(s_gT, 1)
                for n in range(LB):
                    ins = pe.transpose(PS[:, 6, 40 * n:40 * n + 40], prm[0:40, n * P:(n + 1) * P], ident[0:40, 0:40])
                ins.then_inc(s_pT, 1)
                for tb in range(5):
                    turn(pe, tb, xs[:rows(tb), tb, :])

        qk = at(M_AT, 5 * 1536, "p (b n) -> p b n", b=5)
        vn = at(41472, 5 * 512, "p (b n) -> p b n", b=5)
        xlP = at(44032, LB * 515, "p (n t) -> p n t", n=LB)
        xlS = at(48152, LB * NB * 7, "p (n b j) -> p n b j", n=LB, b=NB)
        xc = at(A_AT, 2 * T, "p (a t) -> p a t", a=2)
        pnb = at(A_AT + 1600, 2 * 8, "p (a c) -> p a c", a=2)
        rg = at(48600, 2 * T, "p (a t) -> p a t", a=2)
        ig = at(49688, 2 * T, "p (a t) -> p a t", a=2)
        av = at(A_AT + 1616, T)
        th = at(A_AT + 2160, T)
        uu = at(A_AT + 2704, T)
        hx = at(A_AT + 3248, NB)
        s_xl, s_xle, s_pad = sem("xl_tile"), sem("xl_evac"), sem("conv_rows")
        s_xc, s_gate, s_sig, s_la = sem("xc_ready"), sem("gates_psum"), sem("gates"), sem("log_a")
        s_ab, s_tm, s_sr, s_lru = sem("a_and_tanh"), sem("one_minus_a2"), sem("root_u"), sem("lru_block")
        s_qkv, s_qkve = sem("qkv_tile"), sem("qkv_evac")
        XL0 = landed[0]

        def b_t(ap):
            return ap.rearrange("p (b t) -> p b t", b=NB)

        with nc.Block() as block:
            @block.sync
            def _(sp_):
                for a in range(2):
                    sp_.wait_ge(s_xl, 4 * (a + 1))
                    load_w(sp_, a, w_in[:, :, COL_L + HC * (2 + a):COL_L + HC * (3 + a)])
                for a in range(2):
                    sp_.wait_ge(s_xl, 4 * (a + 3))
                    load_w(sp_, a, w_in[:, :, HC * a:HC * (a + 1)])
                with sp_.Fori(1, 4) as i:
                    for a in range(2):
                        wait_apart(sp_, s_qkv, i * 10 + 5 * a - 5)
                        load_w(sp_, a, w_in[:, :, bass.ds(i * 512 + HC * a, HC)])
                        wait_apart(sp_, s_gate, i * 2 + a - 1)
                        for m, name in enumerate(("lru_wa", "lru_wx")):
                            sp_.dma_start(wab[:, a, m, :].unsqueeze(1),
                                          io[name][0].rearrange("n i j -> i n j")[:, bass.ds(i * 2 + a, 1), :]
                                          ).then_inc(s_wab[a], 16)

            @block.tensor
            def _(pe):
                for n in range(LB):
                    c, j = n // 2, n % 2
                    if j == 0:
                        pe.wait_ge(w_in_sem[c % 2], 16 * (c // 2 + 1))
                    for half in range(2):
                        k = 2 * n + half
                        if k >= 4:
                            pe.wait_ge(s_xle, k - 3)
                        for d in range(DC):
                            ins = pe.matmul(PS[:, k % 4, 0:HALF], W[:, c % 2, d, j * P:(j + 1) * P],
                                            xnT[:, d, half * HALF:(half + 1) * HALF], start=d == 0, stop=d == DC - 1)
                        ins.then_inc(s_xl, 1)
                pe.wait_ge(s_xle, 16)
                pe.sem_inc(s_qkve, 2)
                pe.sem_inc(s_sig, 1)
                with pe.Fori(0, 4) as i:
                    for a in range(2):
                        pe.wait_ge(w_in_sem[a], i * 16 + 48)
                        for tb in range(5):
                            k = 5 * a + tb
                            pe.wait_ge(s_qkve, i * 10 + k + 1)
                            for d in range(DC):
                                ins = pe.matmul(PS[:rows(tb), 4 + k % 2, 0:HC], xnT[:, d, tb * P:tb * P + rows(tb)],
                                                W[:, a, d, :], start=d == 0, stop=d == DC - 1)
                            ins.then_inc(s_qkv, 1)
                        pe.wait_ge(s_wab[a], i * 32 + 32)
                        pe.wait_ge(s_xc, i * 2 + a + 1)
                        pe.wait_ge(s_sig, i * 2 + a + 1)
                        for m in range(2):
                            pe.matmul(PS[:, 6 + m, :], wab[:, a, m, :], xc[:, a, 0:SEQ], start=True, stop=True)
                            ins = pe.matmul(PS[:, m, 0:NS], wab[:, a, m, :], xc[:, a, SEQ:T], start=True, stop=True)
                        ins.then_inc(s_gate, 1)

            @block.scalar
            def _(act):
                for n in range(LB):
                    act.wait_ge(s_xl, 2 * n + 1)
                    act.activation(xlP[:, n, 3:3 + HALF], PS[:, (2 * n) % 4, 0:HALF], ACT.Copy).then_inc(s_xle, 1)
                    act.wait_ge(s_xl, 2 * n + 2)
                    act.activation(xlP[:, n, 3 + HALF:515], PS[:, (2 * n + 1) % 4, 0:SEQ - HALF], ACT.Copy)
                    act.activation(xlS[:, n, :, 3:7], b_t(PS[:, (2 * n + 1) % 4, SEQ - HALF:HALF]),
                                   ACT.Copy).then_inc(s_xle, 1)

                def turn2(i, v_part):
                    for a in range(2):
                        for tb in range(5):
                            k = 5 * a + tb
                            wait_apart(act, s_qkv, i * 10 + k + 1)
                            if v_part:
                                dst = vn[:rows(tb), tb, HC * a:HC * (a + 1)]
                            else:
                                dst = qk[:rows(tb), tb, bass.ds(i * 512 + HC * a, HC)]
                            act.activation(dst, PS[:rows(tb), 4 + k % 2, 0:HC], ACT.Copy).then_inc(s_qkve, 1)
                        act.wait_ge(s_gate, i * 2 + a + 1)
                        for m, dst in ((0, rg), (1, ig)):
                            act.activation(dst[:, a, 0:SEQ], PS[:, 6 + m, :], ACT.Sigmoid, bias=pnb[:, a, 5 + m:6 + m])
                            ins = act.activation(dst[:, a, SEQ:T], PS[:, m, 0:NS], ACT.Sigmoid,
                                                 bias=pnb[:, a, 5 + m:6 + m])
                        ins.then_inc(s_sig, 1)
                        act.wait_ge(s_la, i * 2 + a + 1)
                        act.activation(av, rg[:, a, :], ACT.Exp)
                        act.activation(th, rg[:, a, :], ACT.Tanh, scale=-1.0).then_inc(s_ab, 1)
                        act.wait_ge(s_tm, i * 2 + a + 1)
                        act.activation(uu, th, ACT.Sqrt).then_inc(s_sr, 1)

                with act.Fori(0, 3) as i:
                    turn2(i, False)
                turn2(3, True)

            @block.vector
            def _(v):
                v.memset(xlP[:, :, 0:3], 0.0)
                v.tensor_copy(xlS[:, :, :, 0:3], prmT[:, :, 0:24].rearrange("p n (b j) -> p n b j", b=NB)).then_inc(s_pad, 1)
                v.wait_ge(s_pad, 1)
                v.wait_ge(s_xle, 16)
                with steps_v.loop(4, 2 * 19) as i:
                    for a in range(2):
                        n = i * 2 + a
                        steps_v.did(v.tensor_copy(pnb[:, a, 0:7].unsqueeze(1), prmT[:, bass.ds(n, 1), 32:39]))
                        steps_v.did(v.tensor_copy(pnb[:, a, 7:8], sp8[:, bass.ds(n, 1)]))
                        steps_v.settle()
                        xs_in = [xlP[:, bass.ds(n, 1), j:j + SEQ] for j in range(CW)]
                        xs_smp = [xlS[:, bass.ds(n, 1), :, j:j + NT].rearrange("p a b t -> p (a b) t") for j in range(CW)]
                        oP, oS = xc[:, a, 0:SEQ].unsqueeze(1), b_t(xc[:, a, SEQ:T])
                        steps_v.did(v.tensor_scalar(oP, xs_in[0], pnb[:, a, 0:1], pnb[:, a, 4:5], ALU.mult, ALU.add))
                        steps_v.did(v.tensor_scalar(oS, xs_smp[0], pnb[:, a, 0:1], pnb[:, a, 4:5], ALU.mult, ALU.add))
                        for j in range(1, CW):
                            steps_v.settle()
                            if j < CW - 1:
                                steps_v.did(v.scalar_tensor_tensor(oP, xs_in[j], pnb[:, a, j:j + 1], oP, ALU.mult, ALU.add))
                                steps_v.did(v.scalar_tensor_tensor(oS, xs_smp[j], pnb[:, a, j:j + 1], oS, ALU.mult, ALU.add))
                            else:
                                v.scalar_tensor_tensor(oP, xs_in[j], pnb[:, a, j:j + 1], oP, ALU.mult, ALU.add)
                                v.scalar_tensor_tensor(oS, xs_smp[j], pnb[:, a, j:j + 1], oS, ALU.mult,
                                                       ALU.add).then_inc(s_xc, 1)
                        v.wait_ge(s_sig, i * 2 + a + 2)
                        v.tensor_scalar(rg[:, a, :], rg[:, a, :], pnb[:, a, 7:8], None, ALU.mult).then_inc(s_la, 1)
                        steps_v.did(v.tensor_tensor(ig[:, a, :], ig[:, a, :], xc[:, a, :], ALU.mult))
                        v.wait_ge(s_ab, i * 2 + a + 1)
                        steps_v.did(v.tensor_tensor(uu, av, av, ALU.mult))
                        steps_v.settle()
                        v.scalar_tensor_tensor(th, uu, 1.0, th, ALU.add, ALU.mult).then_inc(s_tm, 1)
                        v.wait_ge(s_sr, i * 2 + a + 1)
                        steps_v.did(v.tensor_tensor(uu, uu, ig[:, a, :], ALU.mult))
                        steps_v.settle()
                        steps_v.did(v.tensor_tensor_scan(lruT[:, bass.ds(n, 1), 0:SEQ].rearrange("p a t -> p (a t)"),
                                                         av[:, 0:SEQ], uu[:, 0:SEQ], 0.0, ALU.mult, ALU.add))
                        hs = lruT[:, bass.ds(n, 1), SEQ:T].rearrange("p a (b t) -> p (a b) t", b=NB)
                        aS, uS = b_t(av[:, SEQ:T]), b_t(uu[:, SEQ:T])
                        prev = prmT[:, bass.ds(n, 1), 24:32].rearrange("p a b -> p (a b)").unsqueeze(2)
                        for t in range(NT):
                            steps_v.did(v.tensor_tensor(hx.unsqueeze(2), aS[:, :, t:t + 1], prev, ALU.mult))
                            steps_v.settle()
                            ins = v.tensor_tensor(hs[:, :, t:t + 1], hx.unsqueeze(2), uS[:, :, t:t + 1], ALU.add)
                            if t < NT - 1:
                                steps_v.did(ins)
                                steps_v.settle()
                            else:
                                ins.then_inc(s_lru, 1)
                            prev = hs[:, :, t:t + 1]
                        v.wait_ge(s_lru, i * 2 + a + 1)

        qT = at(0, NH * T, "p (h t) -> p h t", h=NH)
        kT = at(4352, NG * T, "p (g t) -> p g t", g=NG)
        rtmp = at(6528, 2 * 4 * 192, "p (b a g e) -> p b a g e", b=2, a=4, g=24)
        last = at(8064, LB * 36, "p (n c) -> p n c", n=LB)
        lastrows = at(8400, LW)
        s_rope, s_qkt, s_qke, s_last, s_lastT, s_lrow = (sem("rotated"), sem("qk_transposed"), sem("qk_evac"),
                                                        sem("last_cols"), sem("last_rows"), sem("last_rows_sbuf"))

        with nc.Block() as block:
            @block.vector
            def _(v):
                v.tensor_copy(last[:, :, 0:24].rearrange("p n (b j) -> p n b j", b=NB), xlS[:, :, :, 4:7])
                v.tensor_copy(last[:, :, 24:32], lruT[:, :, SEQ + NT - 1:T:NT])
                v.tensor_copy(last[:, :, 32:35], xlP[:, :, 512:515])
                v.tensor_copy(last[:, :, 35:36], lruT[:, :, SEQ - 1:SEQ]).then_inc(s_last, 1)
                for tb in range(5):
                    np_ = rows(tb)
                    t1 = qk[:np_, tb, :].rearrange("p (g e) -> p g e", g=24)[:, :, 0:8]
                    t2 = qk[:np_, tb, :].rearrange("p (g e) -> p g e", g=24)[:, :, 8:16]
                    cs = const[:np_, C_CS + 16 * tb:C_CS + 16 * tb + 8].unsqueeze(1).broadcast_to([np_, 24, 8])
                    sn = const[:np_, C_CS + 16 * tb + 8:C_CS + 16 * tb + 16].unsqueeze(1).broadcast_to([np_, 24, 8])
                    tmp = rtmp[:np_, tb % 2]
                    if tb >= 2:
                        v.wait_ge(s_rope, tb - 1)
                    for m, (x, y) in enumerate(((t1, cs), (t2, sn), (t2, cs), (t1, sn))):
                        steps_v.did(v.tensor_tensor(tmp[:, m], x, y, ALU.mult))
                    steps_v.settle()
                    v.tensor_tensor(t1, tmp[:, 0], tmp[:, 1], ALU.subtract)
                    v.tensor_tensor(t2, tmp[:, 2], tmp[:, 3], ALU.add).then_inc(s_rope, 1)
                v.wait_ge(s_lastT, 1)
                v.tensor_copy(lastrows[0:36, :].rearrange("p (a n) -> p a n", a=2), PS[0:36, 4:6, :]).then_inc(s_lrow, 1)

            @block.tensor
            def _(pe):
                pe.wait_ge(s_last, 1)
                for n in range(LB):
                    ins = pe.transpose(PS[0:36, 4 + n // 4, (n % 4) * P:(n % 4 + 1) * P], last[:, n, :], ident)
                ins.then_inc(s_lastT, 1)
                for tb in range(5):
                    pe.wait_ge(s_rope, tb + 1)
                    for q in range(3):
                        n = 3 * tb + q
                        if n >= 4:
                            pe.wait_ge(s_qke, n - 3)
                        for j in range(4):
                            ins = pe.transpose(PS[:, n % 4, j * P:j * P + rows(tb)],
                                               qk[:rows(tb), tb, (4 * q + j) * P:(4 * q + j + 1) * P], ident[:rows(tb), :rows(tb)])
                        ins.then_inc(s_qkt, 1)

            @block.scalar
            def _(act):
                for tb in range(5):
                    for q in range(3):
                        n = 3 * tb + q
                        dst = qT[:, 4 * q:4 * q + 4, tb * P:tb * P + rows(tb)] if q < 2 else kT[:, :, tb * P:tb * P + rows(tb)]
                        act.wait_ge(s_qkt, n + 1)
                        act.activation(dst, PS[:, n % 4, :].rearrange("p (j t) -> p j t", j=4)[:, :, 0:rows(tb)],
                                       ACT.Copy).then_inc(s_qke, 1)

            @block.sync
            def _(sp_):
                kp = io["k_prompt"][0, 0].rearrange("(b p) g c -> b p (g c)", p=P)
                vp = io["v_prompt"][0, 0].rearrange("(b p) g c -> b p (g c)", p=P)
                ks = io["k_sample"][0].rearrange("b t g c -> (b t) (g c)")
                vs = io["v_sample"][0].rearrange("b t g c -> (b t) (g c)")
                for tb in range(5):
                    store(sp_, vp[tb] if tb < TB else vs, vn[:rows(tb), tb, :])
                for tb in range(5):
                    sp_.wait_ge(s_rope, tb + 1)
                    store(sp_, kp[tb] if tb < TB else ks, qk[:rows(tb), tb, 1024:1536])
                sp_.wait_ge(s_lrow, 1)
                store(sp_, io["conv_sample"][0].rearrange("b j c -> (b j) c"), lastrows[0:24, :])
                store(sp_, io["h_sample"][0], lastrows[24:32, :])
                store(sp_, io["conv_prompt"][0, 0], lastrows[32:35, :])
                store(sp_, io["h_prompt"][0], lastrows[35:36, :])
                sp_.wait_ge(out_done, 16 * outs[0])

        pb = at(8064, 2 * 2 * SEQ, "p (b c k) -> p b c k", b=2, c=2)
        wTb = at(10112, 2 * SEQ, "p (b k) -> p b k", b=2)
        dg = at(11136, 2 * 2 * P, "p (b c k) -> p b c k", b=2, c=2)
        st = at(11648, 2 * 8, "p (b c) -> p b c", b=2)
        qbd = at(39008, NB * NG * 64, "p (b g c) -> p b g c", b=NB, g=NG)
        kTn = at(44032, NG * NS, "p (g t) -> p g t", g=NG)
        s_qbd = sem("q_blockdiag")
        s_S, s_nb, s_p, s_dg = sem("scores"), sem("neg_max"), sem("exp"), sem("diagonals")
        s_wt, s_wte, s_pv, s_att = sem("weights_T"), sem("weights_T_sbuf"), sem("values"), sem("att_sbuf")
        s_mk = sem("masked")
        its = [(h, qb) for h in range(NH) for qb in range(TB)]
        SC = HD ** -0.5

        with nc.Block() as block:
            @block.gpsimd
            def _(g_):
                steps_g.did(g_.memset(qbd, 0.0))
                for c in range(2):
                    for g in range(NG):
                        for r in range(2):
                            col = 16 * g + 8 * c + 4 * r
                            steps_g.settle()
                            steps_g.did(g_.tensor_copy(qbd[64 * c:64 * c + 64, :, g, col:col + 4],
                                           qT[64 * c:64 * c + 64, 2 * g + r, SEQ:T].rearrange("p (b t) -> p b t", b=NB)))
                steps_g.settle()
                g_.tensor_copy(kTn, kT[:, :, SEQ:T]).then_inc(s_qbd, 1)

            @block.tensor
            def _(pe):
                def scores(it):
                    h, qb = its[it]
                    if it >= 2:
                        pe.wait_ge(s_p, it - 1)
                    for c in range(2):
                        ins = pe.matmul(PS[:, c + 2 * (it % 2), 0:(qb + 1) * P], qT[64 * c:64 * c + 64, h, qb * P:(qb + 1) * P],
                                        kT[64 * c:64 * c + 64, h // 2, 0:(qb + 1) * P], start=True, stop=True)
                    ins.then_inc(s_S, 1)

                def weights(it):
                    h, qb = its[it]
                    pe.wait_ge(s_dg, it + 1)
                    if it >= 2:
                        pe.wait_ge(s_wte, it - 1)
                    for kb in range(qb + 1):
                        for c in range(2):
                            ins = pe.matmul(PS[:, 4 + it % 2, kb * P:(kb + 1) * P], pb[:, it % 2, c, kb * P:(kb + 1) * P],
                                            dg[:, it % 2, c, :], start=c == 0, stop=c == 1)
                    ins.then_inc(s_wt, 1)

                def values(it):
                    h, qb = its[it]
                    pe.wait_ge(s_wte, it + 1)
                    if it >= 2:
                        pe.wait_ge(s_att, it - 1)
                    for kb in range(qb + 1):
                        ins = pe.matmul(PS[:, 6 + it % 2, 0:P], vn[:, kb, (h // 2) * P:(h // 2 + 1) * P],
                                        wTb[:, it % 2, kb * P:(kb + 1) * P], start=kb == 0, stop=kb == qb)
                    ins.then_inc(s_pv, 1)

                scores(0)
                for it in range(len(its) + 1):
                    if it + 1 < len(its):
                        scores(it + 1)
                    if it < len(its):
                        weights(it)
                    if it >= 1:
                        values(it - 1)

            @block.vector
            def _(v):
                def front(it):
                    h, qb = its[it]
                    b0 = 2 * (it % 2)
                    v.wait_ge(s_S, it + 1)
                    dgl = PS[:, b0:b0 + 2, qb * P:(qb + 1) * P]
                    steps_v.did(v.tensor_tensor(dgl, dgl, causal.unsqueeze(1).broadcast_to([P, 2, P]), ALU.add))
                    steps_v.settle()
                    steps_v.did(v.tensor_reduce(st[:, it % 2, 0:2], PS[:, b0:b0 + 2, 0:(qb + 1) * P], AX.X, ALU.max))
                    steps_v.settle()
                    v.tensor_scalar(st[:, it % 2, 2:4], st[:, it % 2, 0:2], -SC, None, ALU.mult).then_inc(s_nb, 1)

                def back(it):
                    v.wait_ge(s_p, it + 1)
                    if it >= 2:
                        v.wait_ge(s_wt, it - 1)
                    steps_v.did(v.reciprocal(st[:, it % 2, 6:8], st[:, it % 2, 4:6]))
                    steps_v.settle()
                    steps_v.did(v.tensor_scalar(st[:, it % 2, 7:8], st[:, it % 2, 7:8], neglam, None, ALU.mult))
                    steps_v.settle()
                    for c in range(2):
                        ins = v.tensor_scalar(dg[:, it % 2, c, :], ident, st[:, it % 2, 6 + c:7 + c], None, ALU.mult)
                    ins.then_inc(s_dg, 1)

                def take(it):
                    h, qb = its[it]
                    v.wait_ge(s_pv, it + 1)
                    v.tensor_copy(attT[:, h, qb * P:(qb + 1) * P], PS[:, 6 + it % 2, 0:P]).then_inc(s_att, 1)

                front(0)
                for it in range(len(its) + 1):
                    if it + 1 < len(its):
                        front(it + 1)
                    if it < len(its):
                        back(it)
                    if it >= 1:
                        take(it - 1)

            @block.scalar
            def _(act):
                def exps(it):
                    h, qb = its[it]
                    act.wait_ge(s_nb, it + 1)
                    if it >= 2:
                        act.wait_ge(s_wt, it - 1)
                    for c in range(2):
                        ins = act.activation(pb[:, it % 2, c, 0:(qb + 1) * P], PS[:, c + 2 * (it % 2), 0:(qb + 1) * P],
                                             ACT.Exp, bias=st[:, it % 2, 2 + c:3 + c], scale=SC,
                                             accum_out=st[:, it % 2, 4 + c:5 + c])
                    ins.then_inc(s_p, 1)

                def take_weights(it):
                    h, qb = its[it]
                    act.wait_ge(s_wt, it + 1)
                    if it >= 2:
                        act.wait_ge(s_pv, it - 1)
                    act.activation(wTb[:, it % 2, 0:(qb + 1) * P], PS[:, 4 + it % 2, 0:(qb + 1) * P],
                                   ACT.Copy).then_inc(s_wte, 1)

                exps(0)
                for it in range(len(its)):
                    if it + 1 < len(its):
                        exps(it + 1)
                    take_weights(it)

        KTs = at(33792, 4 * 512, "p (s k) -> p s k", s=4)
        pS = at(35840, PAST + NS)
        wTs = at(37920, 17 * 64, "p (j c) -> p j c", j=17)
        snew = at(44160, NS)
        comb = at(44192, 64)
        sst = at(44256, 16)
        cache = [io[n].rearrange("l n (r k) g c -> (l n r) (k g c)", k=8) for n in ("cache_k", "cache_v")]
        slots = at(W_AT, 16384, "p (s m) -> p s m", s=4)
        kv = at(W_AT, 16384, "p (s j n) -> p s j n", s=4, j=8)
        s_cache = [sem(f"cache_slot{s}_in") for s in range(4)]
        s_T, s_evA, s_evB, s_sc = sem("k_transposed"), sem("kT_scalar"), sem("kT_vector"), sem("sample_scores")
        s_new, s_nbs, s_ps, s_c64 = sem("new_scores"), sem("sample_neg_max"), sem("sample_exp"), sem("sample_diag")
        s_w, s_wA, s_wB, s_v, s_pve = (sem("sample_weights_T"), sem("weights_T_scalar"), sem("weights_T_vector"),
                                      sem("sample_values"), sem("sample_att_sbuf"))
        PAIRS = NB // 2

        with nc.Block() as block:
            @block.gpsimd
            def _(g_):
                for pr in range(PAIRS):
                    for what in range(2):
                        for bb in range(2):
                            for hf in range(2):
                                b, slot = 2 * pr + bb, 2 * bb + hf
                                if what == 0 and pr >= 1:
                                    g_.wait_ge(s_v, 2 * (pr - 1) + bb + 1)
                                if what == 1:
                                    g_.wait_ge(s_T, 16 * b + 8 * (hf + 1))
                                g_.indirect_dma_start(
                                    slots[:, slot, :], None, cache[what],
                                    bass.IndirectOffsetOnAxis(ap=rowidx[:, hf * NB + b:hf * NB + b + 1], axis=0)
                                ).then_inc(s_cache[slot], 16)

            @block.tensor
            def _(pe):
                def turn_keys(pr, n):
                    bb, u = n // 16, n % 16
                    qd, g = u // 4, u % 4
                    U = 32 * pr + n
                    slot = 2 * bb + u // 8
                    if u % 8 == 0:
                        pe.wait_ge(s_cache[slot], 16 * (2 * pr + 1))
                    if n < 3 and pr:
                        pe.wait_ge(s_wA, pr)
                        pe.wait_ge(s_wB, 2 * pr)
                    elif U >= 3:
                        pe.wait_ge((s_evA, s_evB)[(U - 3) % 2], (U - 3) // 2 + 1)
                    for j in range(4):
                        ins = pe.transpose(PS[:, 5 + U % 3, j * P:(j + 1) * P],
                                           kv[:, slot, (qd % 2) * 4 + j, g * P:(g + 1) * P], ident)
                    ins.then_inc(s_T, 1)

                def score(pr, n):
                    bb, u = n // 16, n % 16
                    qd, g = u // 4, u % 4
                    U = 32 * pr + n
                    pe.wait_ge((s_evA, s_evB)[U % 2], U // 2 + 1)
                    if n == 0 and pr:
                        pe.wait_ge(s_ps, pr)
                    pe.matmul(PS[64 * bb:64 * bb + 64, qd, :], qbd[:, 2 * pr + bb, g, :], KTs[:, U % 4, :],
                              start=g == 0, stop=g == 3).then_inc(s_sc, 1)

                for pr in range(PAIRS):
                    for n in range(33):
                        if n < 32:
                            turn_keys(pr, n)
                        if n:
                            score(pr, n - 1)
                    if pr:
                        pe.wait_ge(s_pve, pr)
                    for bb in range(2):
                        for g in range(NG):
                            ins = pe.matmul(PS[64 * bb:64 * bb + 64, 4, 0:NS], qbd[:, 2 * pr + bb, g, :], kTn[:, g, :],
                                            start=g == 0, stop=g == 3)
                    ins.then_inc(s_new, 1)
                    pe.wait_ge(s_c64, pr + 1)
                    pe.wait_ge(s_evA, 16 * (pr + 1))
                    pe.wait_ge(s_evB, 16 * (pr + 1))
                    for j in range(16):
                        ins = pe.matmul(PS[:, 5 + j // 8, (j % 8) * 64:(j % 8 + 1) * 64], pS[:, j * P:(j + 1) * P], comb,
                                        start=True, stop=True)
                        if j % 8 == 7:
                            ins.then_inc(s_w, 1)
                    pe.matmul(PS[0:NS, 7, 0:64], pS[:, PAST:PAST + NS], comb, start=True, stop=True).then_inc(s_w, 1)
                    pe.wait_ge(s_wA, pr + 1)
                    pe.wait_ge(s_wB, 2 * (pr + 1))
                    for bb in range(2):
                        for hf in range(2):
                            pe.wait_ge(s_cache[2 * bb + hf], 16 * (2 * pr + 2))
                        for g in range(NG):
                            o = 32 * bb + 8 * g
                            dst = PS[:, 4, 64 + o:64 + o + 8]
                            for j in range(16):
                                pe.matmul(dst, kv[:, 2 * bb + j // 8, j % 8, g * P:(g + 1) * P], wTs[:, j, o:o + 8],
                                          start=j == 0, stop=False)
                            ins = pe.matmul(dst, vn[0:NS, TB, g * P:(g + 1) * P], wTs[0:NS, 16, o:o + 8],
                                            start=False, stop=True)
                        ins.then_inc(s_v, 1)

            def take_keys(eng, copy, pr, parity, s):
                for n in range(parity, 32, 2):
                    U = 32 * pr + n
                    eng.wait_ge(s_T, U + 1)
                    if U >= 4:
                        eng.wait_ge(s_sc, U - 3)
                    copy(KTs[:, U % 4, :], PS[:, 5 + U % 3, :]).then_inc(s, 1)

            @block.scalar
            def _(act):
                def copy(dst, src):
                    return act.activation(dst, src, ACT.Copy)
                for pr in range(PAIRS):
                    take_keys(act, copy, pr, 0, s_evA)
                    act.wait_ge(s_nbs, pr + 1)
                    act.activation(pS[:, 0:PAST].rearrange("p (a k) -> p a k", a=4), PS[:, 0:4, :], ACT.Exp, bias=sst[:, 3:4],
                                   scale=SC, accum_out=sst[:, 4:5])
                    act.activation(pS[:, PAST:PAST + NS], snew, ACT.Exp, bias=sst[:, 3:4], scale=SC,
                                   accum_out=sst[:, 5:6]).then_inc(s_ps, 1)
                    act.wait_ge(s_w, 3 * pr + 1)
                    copy(wTs[:, 0:8, :].rearrange("p j c -> p (j c)"), PS[:, 5, :]).then_inc(s_wA, 1)

            @block.vector
            def _(v):
                for pr in range(PAIRS):
                    take_keys(v, v.tensor_copy, pr, 1, s_evB)
                    v.wait_ge(s_new, pr + 1)
                    steps_v.did(v.tensor_tensor(snew, PS[:, 4, 0:NS], const[:, C_NEW + NS * pr:C_NEW + NS * (pr + 1)], ALU.add))
                    steps_v.did(v.tensor_reduce(sst[:, 0:1], PS[:, 0:4, :], AX.XY, ALU.max))
                    steps_v.settle()
                    steps_v.did(v.tensor_reduce(sst[:, 1:2], snew, AX.X, ALU.max))
                    steps_v.settle()
                    steps_v.did(v.tensor_tensor(sst[:, 2:3], sst[:, 0:1], sst[:, 1:2], ALU.max))
                    steps_v.settle()
                    v.tensor_scalar(sst[:, 3:4], sst[:, 2:3], -SC, None, ALU.mult).then_inc(s_nbs, 1)
                    v.wait_ge(s_ps, pr + 1)
                    steps_v.did(v.tensor_tensor(sst[:, 6:7], sst[:, 4:5], sst[:, 5:6], ALU.add))
                    steps_v.settle()
                    steps_v.did(v.reciprocal(sst[:, 7:8], sst[:, 6:7]))
                    steps_v.settle()
                    v.tensor_scalar(comb, const[:, C_COMB:C_COMB + 64], sst[:, 7:8], csel, ALU.mult,
                                    ALU.mult).then_inc(s_c64, 1)
                    v.wait_ge(s_w, 3 * pr + 2)
                    v.tensor_copy(wTs[:, 8:16, :].rearrange("p j c -> p (j c)"), PS[:, 6, :]).then_inc(s_wB, 1)
                    v.wait_ge(s_w, 3 * pr + 3)
                    v.tensor_copy(wTs[0:NS, 16, :], PS[0:NS, 7, 0:64]).then_inc(s_wB, 1)
                    v.wait_ge(s_v, 2 * (pr + 1))
                    cols = slice(SEQ + 2 * NT * pr, SEQ + 2 * NT * (pr + 1))
                    v.tensor_copy(attT[:, :, cols].rearrange("p h (b t) -> p h b t", b=2),
                                  PS[:, 4, 64:128].rearrange("p (b h t) -> p h b t", b=2, h=NH)).then_inc(s_pve, 1)

        w_att_up = io["w_att_up"][0].rearrange("(k p) n -> p k n", p=P)
        w_lru_up = io["w_lru_up"][0].rearrange("(k p) n -> p k n", p=P)
        w_out = io["w_out"][0].rearrange("(k p) n -> p k n", p=P)
        w_q = io["peer_wq"][0].rearrange("(k p) n -> p k n", p=P)

        def load_up(sp_, cols):
            sp_.dma_start(W[:, 2, 0:AC, :], w_att_up[:, :, cols]).then_inc(w_in_sem[2], 16)
            sp_.dma_start(W[:, 2, AC:DC, :], w_lru_up[:, :, cols]).then_inc(w_in_sem[2], 16)

        def stage7_first_loads(sp_):
            load_w(sp_, 0, w_in[:, :, COL_GA:COL_GA + HC])
            load_w(sp_, 1, w_in[:, :, COL_GL:COL_GL + HC])
            load_up(sp_, slice(0, HC))

        SQW = AC * T // 2
        asq = at(33792, AC * T)
        ars = at(38144, AC * T)
        af = at(A_AT, AC * T)
        g08 = at(44300, 1)
        s_asq, s_ams, s_art, s_aps = sem("att_squares"), sem("att_mean_squares"), sem("att_root"), sem("att_sums")

        with nc.Block() as block:
            @block.sync
            def _(sp_):
                stage7_first_loads(sp_)

            @block.vector
            def _(v):
                for r in range(2):
                    sl = slice(SQW * r, SQW * (r + 1))
                    v.tensor_tensor(asq[:, sl], af[:, sl], af[:, sl], ALU.mult).then_inc(s_asq, 1)
                steps_v.did(v.tensor_scalar(g08, gT[:, 32:33], 1.0 - LAM_INIT, None, ALU.mult))
                for r in range(2):
                    v.wait_ge(s_aps, 8 * (r + 1))
                    v.tensor_scalar(ars[:, SQW * r:SQW * (r + 1)].rearrange("p (k t) -> p k t", k=8), PS[:, :, 0:HALF],
                                    1.0 / P, EPS, ALU.mult, ALU.add).then_inc(s_ams, 1)
                for r in range(2):
                    sl = slice(SQW * r, SQW * (r + 1))
                    v.wait_ge(s_art, r + 1)
                    steps_v.did(v.reciprocal(ars[:, sl], ars[:, sl]))
                    steps_v.settle()
                    steps_v.did(v.scalar_tensor_tensor(af[:, sl], af[:, sl], g08, ars[:, sl], ALU.mult, ALU.mult))

            @block.scalar
            def _(act):
                for r in range(2):
                    sl = slice(SQW * r, SQW * (r + 1))
                    act.wait_ge(s_ams, r + 1)
                    act.activation(ars[:, sl], ars[:, sl], ACT.Sqrt).then_inc(s_art, 1)

            @block.tensor
            def _(pe):
                for r in range(2):
                    pe.wait_ge(s_asq, r + 1)
                    if r:
                        pe.wait_ge(s_ams, r)
                    for k in range(8):
                        o = SQW * r + HALF * k
                        pe.matmul(PS[:, k, 0:HALF], ones, asq[:, o:o + HALF], start=True, stop=True).then_inc(s_aps, 1)

        sga = at(44400, 4 * HALF, "p (x t) -> p x t", x=4)
        sgl = at(45500, 4 * HALF, "p (x t) -> p x t", x=4)
        s_ga, s_gl, s_up = sem("ga_tile"), sem("gl_tile"), sem("up_tiles")
        s_sga, s_sgl, s_mA, s_mB = sem("ga_sigmoid"), sem("gl_sigmoid"), sem("att_merged"), sem("lru_merged")
        NCH = D // HC
        L7 = 96

        with nc.Block() as block:
            @block.sync
            def _(sp_):
                with sp_.Fori(1, NCH) as i:
                    wait_apart(sp_, s_ga, i * 4)
                    load_w(sp_, 0, w_in[:, :, bass.ds(i * HC + COL_GA, HC)])
                    wait_apart(sp_, s_gl, i * 4)
                    load_w(sp_, 1, w_in[:, :, bass.ds(i * HC + COL_GL, HC)])
                    wait_apart(sp_, s_up, i * 4)
                    load_up(sp_, bass.ds(i * HC, HC))
                sp_.wait_ge(s_ga, 4 * NCH)
                load_w(sp_, 0, w_out[:, :, 0:HC])
                sp_.wait_ge(s_gl, 4 * NCH)
                load_w(sp_, 1, w_out[:, :, HC:2 * HC])

            @block.tensor
            def _(pe):
                with pe.Fori(0, NCH) as i:
                    for part, tile_done, merged in ((0, s_ga, s_mA), (1, s_gl, s_mB)):
                        pe.wait_ge(w_in_sem[part], i * 16 + (L7 + 16))
                        for x in range(4):
                            pe.wait_ge(merged, i * 4 + x + 1)
                            for d in range(DC):
                                ins = pe.matmul(PS[:, 4 * part + x, 0:HALF], W[:, part, d, (x // 2) * P:(x // 2 + 1) * P],
                                                xnT[:, d, (x % 2) * HALF:(x % 2 + 1) * HALF], start=d == 0, stop=d == DC - 1)
                            ins.then_inc(tile_done, 1)
                    pe.wait_ge(w_in_sem[2], i * 32 + 32)
                    for x in range(4):
                        for part, src, free in ((0, attT, s_sga), (1, lruT, s_sgl)):
                            pe.wait_ge(free, i * 4 + x + 1)
                            for d in range(AC):
                                ins = pe.matmul(PS[:, 4 * part + x, 0:HALF],
                                                W[:, 2, AC * part + d, (x // 2) * P:(x // 2 + 1) * P],
                                                src[:, d, (x % 2) * HALF:(x % 2 + 1) * HALF], start=d == 0, stop=d == AC - 1)
                        ins.then_inc(s_up, 1)

            @block.scalar
            def _(act):
                with act.Fori(0, NCH) as i:
                    for part, dst, tile_done, s, merged in ((0, sga, s_ga, s_sga, s_mA), (1, sgl, s_gl, s_sgl, s_mB)):
                        for x in range(4):
                            act.wait_ge(tile_done, i * 4 + x + 1)
                            act.wait_ge(merged, i * 4 + x + 1)
                            act.activation(dst[:, x, :], PS[:, 4 * part + x, 0:HALF], ACT.Sigmoid).then_inc(s, 1)

            @block.vector
            def _(v):
                v.sem_inc(s_mA, 4)
                v.sem_inc(s_mB, 4)
                with steps_v.loop(NCH, 4) as i:
                    for x in range(4):
                        dst = mT[:, bass.ds(i * 2 + x // 2, 1), (x % 2) * HALF:(x % 2 + 1) * HALF].rearrange("p a t -> p (a t)")
                        v.wait_ge(s_up, i * 4 + x + 1)
                        v.tensor_tensor(dst, sga[:, x, :], PS[:, x, 0:HALF], ALU.mult).then_inc(s_mA, 1)
                        steps_v.did(v.tensor_tensor(sgl[:, x, :], sgl[:, x, :], PS[:, 4 + x, 0:HALF], ALU.mult))
                        steps_v.settle()
                        v.tensor_tensor(dst, dst, sgl[:, x, :], ALU.add).then_inc(s_mB, 1)

        h = at(X_AT, 5 * D, "p (b n) -> p b n", b=5)
        s_xr, s_o, s_hadd = sem("x_again"), sem("out_tile"), sem("h_tile")
        L8 = L7 + 16 * NCH

        def stream_pairs(sp_, src, tile_done, per, upto=NCH):
            with sp_.Fori(1, upto // 2) as i:
                for a in range(2):
                    wait_apart(sp_, tile_done, i * (2 * per) + per * (a - 1))
                    load_w(sp_, a, src[:, :, bass.ds(i * (2 * HC) + HC * a, HC)])

        with nc.Block() as block:
            @block.sync
            def _(sp_):
                for tb in range(5):
                    sp_.dma_start(h[:rows(tb), tb, :], xp[tb] if tb < TB else xsm).then_inc(s_xr, 16)
                stream_pairs(sp_, w_out, s_o, 5)
                for a in range(2):
                    sp_.wait_ge(s_o, 5 * (NCH - 1 + a))
                    load_w(sp_, a, w_q[:, :, HC * a:HC * (a + 1)])

            @block.tensor
            def _(pe):
                with pe.Fori(0, NCH // 2) as i:
                    for a in range(2):
                        pe.wait_ge(w_in_sem[a], i * 16 + (L8 + 16))
                        for tb in range(5):
                            pe.wait_ge(s_hadd, i * 10 + 5 * a + tb + 1)
                            for d in range(DC):
                                ins = pe.matmul(PS[:rows(tb), tb, 0:HC], mT[:, d, tb * P:tb * P + rows(tb)], W[:, a, d, :],
                                                start=d == 0, stop=d == DC - 1)
                            ins.then_inc(s_o, 1)

            @block.vector
            def _(v):
                v.sem_inc(s_hadd, 5)
                v.wait_ge(s_xr, 16 * 5)
                with v.Fori(0, NCH // 2) as i:
                    for a in range(2):
                        for tb in range(5):
                            v.wait_ge(s_o, i * 10 + 5 * a + tb + 1)
                            dst = h[:rows(tb), tb, bass.ds(i * (2 * HC) + HC * a, HC)]
                            v.tensor_tensor(dst, dst, PS[:rows(tb), tb, 0:HC], ALU.add).then_inc(s_hadd, 1)

        xn2T = mT
        xsc = at(R_AT, 2 * D, "p (b n) -> p b n", b=2)
        kkT = at(26624, 2 * NK, "p (a n) -> p a n", a=2)
        kk = at(26880, 2 * P, "p (a n) -> p a n", a=2)
        s_kk, s_kkt, s_kke = sem("peer_keys_in"), sem("peer_keys_T"), sem("peer_keys_sbuf")
        squares, evac_scalar, scale, scale_block, evac_vector, turn = transposed_norm(1, h, xn2T, 16)

        with nc.Block() as block:
            @block.sync
            def _(sp_):
                for a in range(2):
                    sp_.dma_start(kk[:, a, :], io[f"peer_k{a + 1}"][0]).then_inc(s_kk, 16)

            @block.scalar
            def _(act):
                squares(act)
                act.wait_ge(s_kkt, 1)
                act.activation(kkT, PS[:, 4, 0:2 * NK].rearrange("p (a n) -> p a n", a=2), ACT.Copy).then_inc(s_kke, 1)
                evac_scalar(act)

            @block.vector
            def _(v):
                scale(v)
                scale_block(v, 0, xsc[:, 0, :])
                scale_block(v, 1, xsc[:, 1, :])
                for tb in range(5):
                    evac_vector(v, tb)
                    if tb + 2 < 5:
                        v.wait_ge(s_tr, 20 + 4 * (tb + 1))
                        scale_block(v, tb + 2, xsc[:rows(tb + 2), tb % 2, :])

            @block.tensor
            def _(pe):
                pe.wait_ge(s_kk, 32)
                for a in range(2):
                    ins = pe.transpose(PS[:, 4, a * NK:(a + 1) * NK], kk[:, a, :], ident)
                ins.then_inc(s_kkt, 1)
                for tb in range(5):
                    turn(pe, tb, xsc[:rows(tb), tb % 2, :])

        qpT = at(R_AT, DC * T, "p (k t) -> p k t", k=DC)
        s_qp, s_qpe = sem("query_tile"), sem("query_evac")
        L10 = L8 + 16 * NCH // 2

        with nc.Block() as block:
            @block.sync
            def _(sp_):
                stream_pairs(sp_, w_q, s_qp, 4)

            @block.tensor
            def _(pe):
                with pe.Fori(0, NCH // 2) as i:
                    for a in range(2):
                        pe.wait_ge(w_in_sem[a], i * 16 + (L10 + 16))
                        for x in range(4):
                            pe.wait_ge(s_qpe, i * 8 + 4 * a + x + 1)
                            for d in range(DC):
                                ins = pe.matmul(PS[:, 4 * a + x, 0:HALF], W[:, a, d, (x // 2) * P:(x // 2 + 1) * P],
                                                xn2T[:, d, (x % 2) * HALF:(x % 2 + 1) * HALF], start=d == 0, stop=d == DC - 1)
                            ins.then_inc(s_qp, 1)

            @block.scalar
            def _(act):
                act.sem_inc(s_qpe, 8)
                with act.Fori(0, NCH // 2) as i:
                    for a in range(2):
                        for x in range(4):
                            wait_apart(act, s_qp, i * 8 + 4 * a + x + 1)
                            dst = qpT[:, bass.ds(i * 4 + 2 * a + x // 2, 1), (x % 2) * HALF:(x % 2 + 1) * HALF]
                            act.activation(dst, PS[:, 4 * a + x, 0:HALF].unsqueeze(1), ACT.Copy).then_inc(s_qpe, 1)

        eid = at(26880, (TB + 1) * P - 96).bitcast(I32)
        gate = at(27424, (TB + 1) * P - 96)
        S2 = at(0, 2048)
        cand = at(2048, 2048, "p (h m) -> p h m", h=PH)
        cand2 = at(4096, 2048, "p (h m) -> p h m", h=PH)
        eq = at(6144, 2048, "p (m i) -> p m i", i=16)
        picked = at(8192, 2048, "p (m i) -> p m i", i=16)
        vals = at(10240, 256, "p (u k) -> p u k", u=16)
        idx = at(10496, 256, "p (u k) -> p u k", u=16).bitcast(U32)
        idxf = at(10752, 256, "p (h a k) -> p h a k", h=PH, a=2)
        best = at(11008, P, "p (h k) -> p h k", h=PH)
        sel = at(11136, P, "p (h k) -> p h k", h=PH).bitcast(U32)
        selp = at(11264, 2 * P, "p (a m) -> p a m", a=2).bitcast(U32)
        selpf = at(11520, 2 * P, "p (a m) -> p a m", a=2)
        pick = at(11776, 2 * P, "p (a m) -> p a m", a=2)
        rel = at(12032, P, "p (h k) -> p h k", h=PH)
        gexp = at(12160, P, "p (h k) -> p h k", h=PH)
        gsum = at(12288, PH)
        eidS = at(12296, P).bitcast(I32)
        gateS = at(12424, P)
        s_ks, s_l1, s_rel, s_gexp = sem("key_scores"), sem("key_scores_read"), sem("gate_logits"), sem("gate_exp")

        with nc.Block() as block:
            @block.tensor
            def _(pe):
                for tb in range(5):
                    if tb:
                        pe.wait_ge(s_l1, tb)
                    for u in range(2 * PH):
                        ins = pe.matmul(PS[:rows(tb), u // 4, (u % 4) * NK:(u % 4 + 1) * NK], qpT[:, u, tb * P:tb * P + rows(tb)],
                                        kkT[:, u % 2, :], start=True, stop=True)
                    ins.then_inc(s_ks, 1)

            @block.scalar
            def _(act):
                for tb in range(5):
                    act.wait_ge(s_rel, tb + 1)
                    act.activation(gexp[:rows(tb)], rel[:rows(tb)], ACT.Exp).then_inc(s_gexp, 1)

            @block.vector
            def _(v):
                def choose(np_, turn_, eid_to, gate_to):
                    did, settle = steps_v.did, lambda: settle_apart(steps_v)
                    wait_apart(v, s_ks, turn_ + 1)
                    R = slice(0, np_)

                    def key_row(u):
                        return PS[R, u // 4, (u % 4) * NK:(u % 4 + 1) * NK]

                    for u in range(16):
                        did(v.max(vals[R, u, 0:8], key_row(u)))
                    settle()
                    for u in range(16):
                        did(v.max_index(idx[R, u, 0:8], vals[R, u, 0:8], key_row(u)))
                    for u in range(16):
                        ins = v.match_replace(S2[R, u * NK:(u + 1) * NK], vals[R, u, 0:8], key_row(u), -3e38)
                    ins.then_inc(s_l1, 1)
                    wait_apart(v, s_l1, turn_ + 1)
                    for u in range(16):
                        did(v.max(vals[R, u, 8:16], S2[R, u * NK:(u + 1) * NK]))
                    settle()
                    for u in range(16):
                        did(v.max_index(idx[R, u, 8:16], vals[R, u, 8:16], S2[R, u * NK:(u + 1) * NK]))
                    pair = vals[R].rearrange("p (h a) k -> p h a k", a=2)
                    did(v.tensor_tensor(cand[R].rearrange("p h (i j) -> p h i j", i=16),
                                        pair[:, :, 0, :].unsqueeze(3).broadcast_to([np_, PH, 16, 16]),
                                        pair[:, :, 1, :].unsqueeze(2).broadcast_to([np_, PH, 16, 16]), ALU.add))
                    settle()
                    did(v.tensor_copy(idxf[R], idx[R].rearrange("p (h a) k -> p h a k", a=2)))
                    for u in range(PH):
                        did(v.max(best[R, u, 0:8], cand[R, u]))
                    settle()
                    for u in range(PH):
                        did(v.max_index(sel[R, u, 0:8], best[R, u, 0:8], cand[R, u]))
                    for u in range(PH):
                        did(v.match_replace(cand2[R, u], best[R, u, 0:8], cand[R, u], -3e38))
                    settle()
                    for u in range(PH):
                        did(v.max(best[R, u, 8:16], cand2[R, u]))
                    settle()
                    for u in range(PH):
                        did(v.max_index(sel[R, u, 8:16], best[R, u, 8:16], cand2[R, u]))
                    v.tensor_tensor(rel[R], best[R], best[R, :, 0:1].broadcast_to([np_, PH, 16]), ALU.subtract).then_inc(s_rel, 1)
                    settle()
                    flat = sel[R].rearrange("p h k -> p (h k)")
                    did(v.tensor_scalar(selp[R, 0, :], flat, 4, None, ALU.logical_shift_right))
                    did(v.tensor_scalar(selp[R, 1, :], flat, 15, None, ALU.bitwise_and))
                    settle()
                    did(v.tensor_copy(selpf[R], selp[R]))
                    for a in range(2):
                        settle()
                        did(v.tensor_tensor(eq[R], selpf[R, a, :].unsqueeze(2).broadcast_to([np_, P, 16]),
                                            const[R, C_IOTA:C_IOTA + 16].unsqueeze(1).broadcast_to([np_, P, 16]), ALU.is_equal))
                        settle()
                        did(v.tensor_tensor(picked[R].rearrange("p (h k) i -> p h k i", h=PH),
                                            eq[R].rearrange("p (h k) i -> p h k i", h=PH),
                                            idxf[R, :, a, :].unsqueeze(2).broadcast_to([np_, PH, 16, 16]), ALU.mult))
                        settle()
                        did(v.tensor_reduce(pick[R, a, :], picked[R], AX.X, ALU.add))
                    settle()
                    did(v.scalar_tensor_tensor(eid_to, pick[R, 0, :], float(NK), pick[R, 1, :], ALU.mult, ALU.add))
                    v.wait_ge(s_gexp, turn_ + 1)
                    did(v.tensor_reduce(gsum[R], gexp[R], AX.X, ALU.add))
                    settle()
                    did(v.reciprocal(gsum[R], gsum[R]))
                    settle()
                    did(v.tensor_tensor(gate_to.rearrange("p (h k) -> p h k", h=PH), gexp[R],
                                        gsum[R].unsqueeze(2).broadcast_to([np_, PH, 16]), ALU.mult))
                    settle()

                per = 16 + 16 + 16 + 16 + 1 + 1 + 5 * PH + 3 + 6 + 1 + 3
                with steps_v.loop(TB, per) as i:
                    choose(P, i, eid[:, bass.ds(i * P, P)], gate[:, bass.ds(i * P, P)])
                choose(NS, TB, eidS[0:NS], gateS[0:NS])
                for g in range(4):
                    for src, dst in ((eidS, eid), (gateS, gate)):
                        steps_v.did(v.tensor_copy(dst[NS * g:NS * (g + 1), SEQ:T], src[0:NS, NS * g:NS * (g + 1)]))

        RING = 16
        ring = [at(s * D if s < 8 else 27968 + (s - 8) * D, D) for s in range(RING)]
        Xn = at(44352, D)
        g2b = at(46400, D)
        fgb = at(48448, D)
        dgr = at(50496, 4 * P, "p (s k) -> p s k", s=4)
        acts = at(51008, P)
        coef = at(51136, P)
        act16 = at(51264, RING)
        stage = at(51280, RING).bitcast(I32)
        fsq = at(51296, 1)
        frs = at(51297, 1)
        gl = at(51300, P)
        s_gb = sem("gains_in")
        s_ring = [sem(f"ring_slot{s}_in") for s in range(RING)]
        s_u, s_vv, s_st = sem("u_used"), sem("v_used"), sem("rows_staged")
        s_act, s_gelu, s_coef, s_dgr = sem("acts"), sem("gelu"), sem("coefs"), sem("diag_ready")
        s_ffn, s_fs, s_fm, s_fr, s_y = sem("ffn_psum"), sem("y_squares"), sem("y_mean_square"), sem("y_root"), sem("y_ready")
        s_rep = sem("x_replicated")
        s_x0 = sem("x_sample_scaled")
        U_ROWS, V_ROWS = io["peer_u"][0], io["peer_v"][0]
        TURNS = SLOTS // RING
        S_TURNS = SLOTS // 4 // RING
        V_BIAS = RING
        VP = PS[:, 4:8, :]

        with nc.Block() as block:
            @block.sync
            def _(sp_):
                sp_.dma_start(g2b, io["norm2_g"][0].partition_broadcast(P)).then_inc(s_gb, 16)
                sp_.dma_start(fgb, io["final_g"].partition_broadcast(P)).then_inc(s_gb, 16)
                yp = io["y_prompt"][0].rearrange("(b p) d -> p b d", p=P)
                with sp_.Fori(0, TB) as b:
                    wait_apart(sp_, s_y, b + 2)
                    sp_.dma_start(yp[:, bass.ds(b, 1), :], h[:, bass.ds(b, 1), :]).then_inc(out_done, 16)
                outs[0] += TB
                sp_.wait_ge(s_x0, 1)
                for g in range(1, 4):
                    sp_.dma_start(Xn[NS * g:NS * (g + 1), :], Xn[0:NS, :]).then_inc(s_rep, 16)
                sp_.wait_ge(s_y, TB + 2)
                store(sp_, io["y_sample"].rearrange("b t d -> (b t) d"), h[0:NS, TB, :])
                sp_.wait_ge(out_done, 16 * outs[0])

            @block.gpsimd
            def _(g_):
                g_.sem_inc(s_vv, V_BIAS)

                def gathers(table, first_col, count, freed, value):
                    for q in range(RING // 4):
                        wait_apart(g_, freed, value + 4 * q)
                        g_.tensor_copy(stage[:, 4 * q:4 * q + 4], eid[:, bass.ds(first_col + 4 * q, 4)]).then_inc(s_st, 1)
                        wait_apart(g_, s_st, count + (q + 1))
                        for s in range(4 * q, 4 * q + 4):
                            g_.indirect_dma_start(ring[s], None, table, bass.IndirectOffsetOnAxis(ap=stage[:, s:s + 1], axis=0)
                                                  ).then_inc(s_ring[s], 16)

                def phases(b, turns, inner):
                    n = turns * RING
                    gathers(U_ROWS, b * SLOTS, b * (2 * SLOTS // 4), s_vv, b * SLOTS + 4)
                    with g_.Fori(1, turns) as i:
                        gathers(U_ROWS, b * SLOTS + i * RING, b * (2 * SLOTS // 4) + i * 4, s_u, b * SLOTS + i * RING - (RING - 4))
                    gathers(V_ROWS, b * SLOTS, b * (2 * SLOTS // 4) + n // 4, s_u, b * SLOTS + (n - RING + 4))
                    with g_.Fori(1, turns) as i:
                        gathers(V_ROWS, b * SLOTS + i * RING, b * (2 * SLOTS // 4) + i * 4 + n // 4, s_vv,
                                b * SLOTS + i * RING + (V_BIAS - RING + 4))

                with g_.Fori(0, TB) as b:
                    phases(b, TURNS, None)
                phases(TB, S_TURNS, None)

            @block.vector
            def _(v):
                v.wait_ge(s_gb, 32)

                def u_phase(b, turns):
                    with steps_v.loop(turns, 1) as i:
                        for s in range(RING):
                            v.wait_ge(s_ring[s], (b * (2 * TURNS) + i) * 16 + 16)
                            v.tensor_tensor_reduce(ring[s], ring[s], Xn, 1.0, 0.0, ALU.mult, ALU.add,
                                                   act16[:, s:s + 1]).then_inc(s_u, 1)
                        wait_apart(v, s_u, b * SLOTS + i * RING + RING)
                        steps_v.did(v.tensor_copy(acts[:, bass.ds(i * RING, RING)], act16))
                        settle_apart(steps_v)

                def finish(b, np_, hb):
                    v.wait_ge(s_fs, b + 1)
                    v.tensor_scalar(frs[0:np_], fsq[0:np_], 1.0 / D, EPS, ALU.mult, ALU.add).then_inc(s_fm, 1)
                    v.wait_ge(s_fr, b + 1)
                    steps_v.did(v.reciprocal(frs[0:np_], frs[0:np_]))
                    steps_v.settle()
                    v.scalar_tensor_tensor(hb, VP[0:np_].rearrange("p a n -> p (a n)"), frs[0:np_], fgb[0:np_],
                                           ALU.mult, ALU.mult).then_inc(s_y, 1)

                v.sem_inc(s_y, 1)
                with v.Fori(0, TB) as b:
                    steps_v.n += 0
                    base = steps_v.base + steps_v.n
                    steps_v.base, steps_v.n = base + b * (TURNS + 2), 0
                    hb = h[:, bass.ds(b, 1), :].rearrange("p a n -> p (a n)")
                    steps_v.did(v.scalar_tensor_tensor(Xn, hb, rstd[:, bass.ds(b, 1)], g2b, ALU.mult, ALU.mult))
                    settle_apart(steps_v)
                    u_phase(b, TURNS)
                    v.sem_inc(s_act, 1)
                    v.wait_ge(s_gelu, b + 1)
                    v.wait_ge(s_vv, b * SLOTS + V_BIAS)
                    v.tensor_tensor(coef, gl, gate[:, bass.ds(b * SLOTS, SLOTS)], ALU.mult).then_inc(s_coef, 1)
                    finish(b, P, hb)
                steps_v.base, steps_v.n = base + TB * (TURNS + 2), 0
                v.scalar_tensor_tensor(Xn[0:NS], h[0:NS, TB, :], rstd[0:NS, 4:5], g2b[0:NS], ALU.mult, ALU.mult).then_inc(s_x0, 1)
                v.wait_ge(s_rep, 48)
                u_phase(TB, S_TURNS)
                v.sem_inc(s_act, 1)
                v.wait_ge(s_gelu, TB + 1)
                v.tensor_tensor(coef[:, 0:NS], gl[:, 0:NS], gate[:, SEQ:T], ALU.mult).then_inc(s_coef, 1)
                finish(TB, NS, h[0:NS, TB, :])

            @block.scalar
            def _(act):
                def v_phase(b, turns, np_, hb, table):
                    wait_apart(act, s_act, b + 1)
                    act.activation(gl[:, 0:turns * RING], acts[:, 0:turns * RING], ACT.Gelu).then_inc(s_gelu, 1)
                    act.wait_ge(s_coef, b + 1)
                    with act.Fori(0, turns) as i:
                        for s in range(RING):
                            wait_apart(act, s_vv, b * SLOTS + i * RING + (V_BIAS + s - 3))
                            act.activation(dgr[:, s % 4, 0:np_], table, ACT.Copy,
                                           scale=coef[:, bass.ds(i * RING + s, 1)]).then_inc(s_dgr, 1)
                    wait_apart(act, s_ffn, b + 1)
                    act.activation(hb, VP[0:np_].rearrange("p a n -> p (a n)"), ACT.Square,
                                   accum_out=fsq[0:np_]).then_inc(s_fs, 1)
                    act.wait_ge(s_fm, b + 1)
                    act.activation(frs[0:np_], frs[0:np_], ACT.Sqrt).then_inc(s_fr, 1)

                with act.Fori(0, TB) as b:
                    v_phase(b, TURNS, P, h[:, bass.ds(b, 1), :].rearrange("p a n -> p (a n)"), ident)
                v_phase(TB, S_TURNS, NS, h[0:NS, TB, :], const[:, C_REP:C_REP + NS])

            @block.tensor
            def _(pe):
                def v_phase(b, turns, np_, rhs):
                    pe.wait_ge(s_y, b + 1)

                    def turn_(i, first):
                        for s in range(RING):
                            pe.wait_ge(s_dgr, b * SLOTS + i * RING + (s + 1))
                            pe.wait_ge(s_ring[s], (b * (2 * TURNS) + i) * 16 + 16 * (turns + 1))
                            for n in range(4):
                                ins = pe.matmul(VP[0:np_, n, :], dgr[:, s % 4, 0:np_], ring[s][:, 512 * n:512 * (n + 1)],
                                                start=first and s == 0, stop=False)
                            ins.then_inc(s_vv, 1)

                    turn_(0, True)
                    with pe.Fori(1, turns) as i:
                        turn_(i, False)
                    for n in range(4):
                        ins = pe.matmul(VP[0:np_, n, :], ident[0:np_, 0:np_], rhs(n), start=False, stop=True)
                    ins.then_inc(s_ffn, 1)

                with pe.Fori(0, TB) as b:
                    v_phase(b, TURNS, P, lambda n: h[:, bass.ds(b, 1), 512 * n:512 * (n + 1)].rearrange("p a n -> p (a n)"))
                v_phase(TB, S_TURNS, NS, lambda n: h[0:NS, TB, 512 * n:512 * (n + 1)])


_INS = ['x_prompt', 'x_sample', 'cache_k', 'cache_v', 'state_conv', 'state_h', 'page_table', 'norm1_g', 'w_in',
        'lambda_q1', 'lambda_k1', 'lambda_q2', 'lambda_k2', 'subln_g', 'conv_w', 'conv_b', 'lru_wa', 'lru_ba',
        'lru_wx', 'lru_bx', 'lru_lambda', 'w_att_up', 'w_lru_up', 'w_out', 'norm2_g', 'peer_wq', 'peer_k1',
        'peer_k2', 'peer_u', 'peer_v', 'final_g']
_OUTS = {'y_prompt': (1, SEQ, D), 'y_sample': (NB, NT, D), 'k_prompt': (1, 1, SEQ, NG, P), 'v_prompt': (1, 1, SEQ, NG, P),
         'conv_prompt': (1, 1, CW - 1, LW), 'h_prompt': (1, 1, LW), 'k_sample': (1, NB, NT, NG, P),
         'v_sample': (1, NB, NT, NG, P), 'conv_sample': (1, NB, CW - 1, LW), 'h_sample': (1, NB, LW)}


def kernel(**inputs):
    import concourse.bacc as _bacc
    from concourse.bass_utils import run_bass_kernel_spmd as _run

    nc = _bacc.Bacc("TRN2", target_bir_lowering=False, num_devices=1)
    arrays, io = {}, {}
    for name in _INS + ['const']:
        a = np.ascontiguousarray(inputs[name]) if name != 'const' else shape_constants()
        arrays[f"in_{name}_dram"] = a
        io[name] = nc.dram_tensor(f"in_{name}_dram", a.shape, mybir.dt.from_np(a.dtype), kind="ExternalInput").ap()
    for name, shape in _OUTS.items():
        io[name] = nc.dram_tensor(f"out_{name}_dram", shape, F32, kind="ExternalOutput").ap()
    build_trunk(nc, io)
    r = _run(nc, [arrays], core_ids=[0])
    return tuple(r.results[0][f"out_{name}_dram"] for name in _OUTS)
```

```python
from contextlib import ExitStack, contextmanager

import numpy as np

import concourse.bass as bass
from concourse import mybir

F32 = mybir.dt.float32
I32 = mybir.dt.int32
U32 = mybir.dt.uint32
ALU = mybir.AluOpType
ACT = mybir.ActivationFunctionType
AX = mybir.AxisListType

P = 128
D = 2048
DC = D // P
SEQ, NB, NT = 512, 8, 4
TB = SEQ // P
NS = NB * NT
T = SEQ + NS
HALF = T // 2
NH, NG, HD = 8, 4, 64
AC = NH
LW, LB = 1024, 8
CW = 4
PAST, PAGE = 2048, 128
NK, PH, TOPK = 128, 8, 16
SLOTS = PH * TOPK
EPS = 1e-6
LAM_INIT = 0.8 - 0.6 * float(np.exp(-0.3 * 0))
HC = 256
COL_Q, COL_K, COL_V, COL_L, COL_GA, COL_GL = 0, 1024, 1536, 2048, 3072, 5120
NEG = -1e30

C_ID, C_CAUSAL, C_NEW, C_COMB, C_CS, C_ISC, C_REP, C_IOTA, C_ONE, C_PAGE, C_SEL = (
    0, 128, 256, 384, 448, 528, 530, 562, 578, 706, 707)
C_END = 723


def shape_constants():
    c = np.zeros((P, C_END), np.float32)
    p = np.arange(P)
    c[:, C_ID:C_ID + P] = np.eye(P)
    c[:, C_CAUSAL:C_CAUSAL + P] = np.where(p[None, :] <= p[:, None], 0.0, NEG)
    bb, g, comp, r, t = p // 64, p // 16 % 4, p // 8 % 2, p // 4 % 2, p % 4
    key = np.arange(NS)
    for pair in range(NB // 2):
        seen = (key[None, :] // NT == (2 * pair + bb)[:, None]) & (key[None, :] % NT <= t[:, None])
        c[:, C_NEW + NS * pair:C_NEW + NS * (pair + 1)] = np.where(seen, 0.0, NEG)
    c[p, C_COMB + bb * 32 + g * 8 + r * 4 + t] = 1.0
    inv = np.float32(500000.0) ** (-np.arange(8, dtype=np.float32) * np.float32(2.0) / np.float32(16))
    for tb in range(TB + 1):
        pos = (tb * P + p if tb < TB else PAST + p % NT).astype(np.float32)
        ang = (pos[:, None] * inv[None, :]).astype(np.float32)
        c[:, C_CS + 16 * tb:C_CS + 16 * tb + 8] = np.cos(ang)
        c[:, C_CS + 16 * tb + 8:C_CS + 16 * tb + 16] = np.sin(ang)
    c[:, C_ISC] = comp == 0
    c[:, C_ISC + 1] = comp == 1
    c[p, C_REP + p % NS] = 1.0
    c[:, C_IOTA:C_IOTA + 16] = np.arange(16)
    c[:, C_ONE:C_ONE + P] = 1.0
    c[:, C_PAGE] = 2 * (p % 8)
    c[p, C_SEL + p // 8] = 1.0
    return c


class Steps:

    def __init__(self, eng, sem):
        self.eng, self.sem, self.base, self.n = eng, sem, 0, 0

    def did(self, ins):
        ins.then_inc(self.sem, 1)
        self.n += 1
        return ins

    def settle(self):
        self.eng.wait_ge(self.sem, self.base + self.n)

    @contextmanager
    def loop(self, trips, per):
        start = self.base + self.n
        with self.eng.Fori(0, trips) as i:
            self.base, self.n = start + i * per, 0
            yield i
            assert self.n == per, (self.n, per)
        self.base, self.n = start + trips * per, 0


def build_trunk(nc, io):
    with ExitStack() as ctx:
        def sem(name):
            return ctx.enter_context(nc.semaphore(name))

        AREA = 53100
        area = ctx.enter_context(nc.sbuf_tensor("area", [P, AREA], F32))
        PS = ctx.enter_context(nc.psum_tensor("PS", [P, 8, 512], F32))

        def at(off, words, spec=None, **dims):
            assert off + words <= AREA
            v = area[:, off:off + words]
            return v.rearrange(spec, **dims) if spec else v

        W_AT, X_AT, A_AT, L_AT, M_AT = 0, 16384, 25088, 29440, 33792
        R_AT = M_AT + 8704
        K_AT = AREA - 1500
        W = at(W_AT, 16384, "p (s k n) -> p s k n", s=4, k=DC)
        xnT = at(X_AT, DC * T, "p (k t) -> p k t", k=DC)
        attT = at(A_AT, AC * T, "p (h t) -> p h t", h=AC)
        lruT = at(L_AT, LB * T, "p (n t) -> p n t", n=LB)
        mT = at(M_AT, DC * T, "p (k t) -> p k t", k=DC)

        const = at(K_AT, C_END)
        ident, causal = const[:, C_ID:C_ID + P], const[:, C_CAUSAL:C_CAUSAL + P]
        ones = const[:, C_ONE:C_ONE + P]
        small_at = [K_AT + C_END]

        def small(words, spec=None, **dims):
            small_at[0] += words
            return at(small_at[0] - words, words, spec, **dims)

        prmT = small(LB * 40, "p (n c) -> p n c", n=LB)
        gT = small(33)
        ssq = small(5)
        rstd = small(5)
        lam2 = small(2)
        neglam = small(1)
        csel = small(1)
        sp8 = small(LB)
        rowidx = small(2 * NB).bitcast(I32)
        stats = small(64)

        xs = at(M_AT, 5 * D, "p (b n) -> p b n", b=5)
        junk = at(L_AT, 2 * D, "p (b n) -> p b n", b=2)
        prm = at(44100, LW)
        gains = at(45200, P)
        lamq = at(45400, 4 * HD, "p (a d) -> p a d", a=4)
        lamp = at(45700, 2 * HD, "p (a d) -> p a d", a=2)
        pt = at(45900, 16 * NB).bitcast(I32)
        ptm = at(46130, 16 * NB)
        sp = at(46000, 8 * LB, "p (a n) -> p a n", a=8)
        ptf = at(46300, 3 * NB, "p (a n) -> p a n", a=3)

        def rows(tb):
            return P if tb < TB else NS

        steps_v = Steps(nc.vector, sem("vector_steps"))
        steps_g = Steps(nc.gpsimd, sem("pool_steps"))
        held = {e.engine: sem(f"held_{n}") for n, e in enumerate((nc.vector, nc.scalar, nc.gpsimd, nc.tensor, nc.sync))}

        def settle_apart(steps):
            wait_apart(steps.eng, steps.sem, steps.base + steps.n)

        def wait_apart(eng, s, value):
            eng.wait_ge(s, value)
            eng.sem_inc(held[eng.engine], 1)

        out_done = sem("out_done")
        outs = [0]

        def store(eng, dst, src):
            eng.dma_start(dst, src).then_inc(out_done, 16)
            outs[0] += 1

        w_in = io["w_in"][0].rearrange("(k p) n -> p k n", p=P)

        s_const, s_prm, s_lamq, s_pt = sem("const_in"), sem("prm_in"), sem("lamq_in"), sem("pages_in")
        s_x = [sem(f"x_in{tb}") for tb in range(5)]
        s_sq, s_ms, s_root = sem("squares"), sem("mean_squares"), sem("root")
        s_xs, s_tr, s_ev_a, s_ev_v = sem("x_scaled"), sem("x_transposed"), sem("evac_scalar"), sem("evac_vector")
        s_gT, s_gTe, s_pT, s_pTe = sem("gains_tr"), sem("gains_ready"), sem("prm_tr"), sem("prm_ready")
        w_in_sem = [sem(f"w_slot{s}_in") for s in range(4)]
        s_lamw = sem("lam_parts")
        s_lame = sem("lam_exp")
        s_spl = [sem(f"softplus_{k}") for k in range(4)]

        def transposed_norm(k, src, dstT, gcol):
            nbank = 4 * 5

            def squares(act):
                if k == 0:
                    act.wait_ge(s_spl[3], 1)
                for tb in range(5):
                    if k == 0:
                        act.wait_ge(s_x[tb], 16)
                    if tb >= 2:
                        act.wait_ge(s_sq, 5 * k + tb - 1)
                    act.activation(junk[:rows(tb), tb % 2, :], src[:rows(tb), tb, :], ACT.Square,
                                   accum_out=ssq[:rows(tb), tb:tb + 1]).then_inc(s_sq, 1)
                act.wait_ge(s_ms, k + 1)
                act.activation(rstd, rstd, ACT.Sqrt).then_inc(s_root, 1)

            def evac_scalar(act):
                act.wait_ge(s_gTe, 1)
                for n in range(0, nbank, 2):
                    tb, q, np_ = n // 4, n % 4, rows(n // 4)
                    act.wait_ge(s_tr, nbank * k + n + 1)
                    for j in range(4):
                        d = 4 * q + j
                        ins = act.activation(dstT[:, d, tb * P:tb * P + np_], PS[:, n % 4, j * P:j * P + np_],
                                             ACT.Copy, scale=gT[:, gcol + d:gcol + d + 1])
                    ins.then_inc(s_ev_a, 1)

            def scale(v):
                v.wait_ge(s_sq, 5 * (k + 1))
                v.tensor_scalar(rstd, ssq, 1.0 / D, EPS, ALU.mult, ALU.add).then_inc(s_ms, 1)
                v.wait_ge(s_root, k + 1)
                steps_v.did(v.reciprocal(rstd, rstd))
                steps_v.settle()

            def scale_block(v, tb, dst):
                v.tensor_scalar(dst, src[:rows(tb), tb, :], rstd[:rows(tb), tb:tb + 1], None,
                                ALU.mult).then_inc(s_xs, 1)

            def evac_vector(v, tb):
                for n in (4 * tb + 1, 4 * tb + 3):
                    q, np_ = n % 4, rows(tb)
                    v.wait_ge(s_tr, nbank * k + n + 1)
                    for j in range(4):
                        d = 4 * q + j
                        ins = v.tensor_scalar(dstT[:, d, tb * P:tb * P + np_], PS[:, n % 4, j * P:j * P + np_],
                                              gT[:, gcol + d:gcol + d + 1], None, ALU.mult)
                    ins.then_inc(s_ev_v, 1)

            def turn(pe, tb, block):
                pe.wait_ge(s_xs, 5 * k + tb + 1)
                for q in range(4):
                    n = 4 * tb + q
                    if n >= 4:
                        pe.wait_ge((s_ev_a, s_ev_v)[n % 2], (nbank // 2) * k + (n - 4) // 2 + 1)
                    for j in range(4):
                        d = 4 * q + j
                        ins = pe.transpose(PS[:, n % 4, j * P:j * P + rows(tb)], block[:, d * P:(d + 1) * P],
                                           ident[:rows(tb), :rows(tb)])
                    ins.then_inc(s_tr, 1)

            return squares, evac_scalar, scale, scale_block, evac_vector, turn

        wab = at(A_AT + 1088, 2 * 256, "p (a m j) -> p a m j", a=2, m=2)
        s_wab = [sem(f"lru_w{a}_in") for a in range(2)]
        landed = [0, 0, 0, 0]

        def load_w(sp_, a, src):
            sp_.dma_start(W[:, a], src).then_inc(w_in_sem[a], 16)

        def load_gates(sp_, a, n):
            for m, name in enumerate(("lru_wa", "lru_wx")):
                sp_.dma_start(wab[:, a, m, :], io[name].rearrange("l n i j -> (l n) i j")[n]).then_inc(s_wab[a], 16)

        squares, evac_scalar, scale, scale_block, evac_vector, turn = transposed_norm(0, xs, xnT, 0)
        xp = io["x_prompt"][0].rearrange("(b p) d -> b p d", p=P)
        xsm = io["x_sample"].rearrange("b t d -> (b t) d")

        with nc.Block() as block:
            @block.sync
            def _(sp_):
                for tb in range(5):
                    sp_.dma_start(xs[:rows(tb), tb, :], xp[tb] if tb < TB else xsm).then_inc(s_x[tb], 16)
                    if tb == 0:
                        sp_.dma_start(const, io["const"]).then_inc(s_const, 16)
                        sp_.dma_start(gains[0:16, :], io["norm1_g"][0].rearrange("(k p) -> k p", p=P)).then_inc(s_prm, 16)
                        sp_.dma_start(gains[16:32, :], io["norm2_g"][0].rearrange("(k p) -> k p", p=P)).then_inc(s_prm, 16)
                        sp_.dma_start(gains[32:33, :], io["subln_g"]).then_inc(s_prm, 16)
                for a in range(2):
                    load_w(sp_, a, w_in[:, :, COL_L + HC * a:COL_L + HC * (a + 1)])
                for a in range(2):
                    load_gates(sp_, a, a)

            @block.scalar
            def _(act):
                act.dma_start(prm[0:24, :], io["state_conv"][0].rearrange("b j c -> (b j) c")).then_inc(s_prm, 16)
                act.dma_start(prm[24:32, :], io["state_h"][0]).then_inc(s_prm, 16)
                act.dma_start(prm[32:36, :], io["conv_w"][0]).then_inc(s_prm, 16)
                for r, name in enumerate(("conv_b", "lru_ba", "lru_bx", "lru_lambda")):
                    act.dma_start(prm[36 + r:37 + r, :], io[name]).then_inc(s_prm, 16)
                for r, name in enumerate(("lambda_q1", "lambda_k1", "lambda_q2", "lambda_k2")):
                    act.dma_start(lamq[:, r, :], io[name][0].partition_broadcast(P)).then_inc(s_lamq, 16)
                pages = io["page_table"]
                act.dma_start(pt, pages.rearrange("b g -> (b g)").partition_broadcast(P)).then_inc(s_pt, 16)
                squares(act)
                act.wait_ge(s_lamw, 1)
                act.activation(lam2, stats[:, 0:2], ACT.Exp).then_inc(s_lame, 1)
                evac_scalar(act)
                act.wait_ge(s_spl[0], 1)
                act.activation(sp[:, 1, :], sp[:, 0, :], ACT.Exp, scale=-1.0).then_inc(s_spl[1], 1)

            @block.vector
            def _(v):
                v.memset(ssq, 1.0).then_inc(s_spl[3], 1)
                scale(v)
                v.wait_ge(s_lamq, 64)
                for a in range(2):
                    ins = v.tensor_tensor_reduce(lamp[:, a, :], lamq[:, 2 * a, :], lamq[:, 2 * a + 1, :], 1.0, 0.0,
                                                 ALU.mult, ALU.add, stats[:, a:a + 1])
                ins.then_inc(s_lamw, 1)
                for tb in range(5):
                    scale_block(v, tb, xs[:rows(tb), tb, :])
                v.wait_ge(s_gT, 1)
                v.tensor_copy(gT, PS[:, 7, 0:33]).then_inc(s_gTe, 1)
                v.wait_ge(s_pT, 1)
                v.tensor_copy(prmT, PS[:, 6, 0:320].rearrange("p (n c) -> p n c", n=LB)).then_inc(s_pTe, 1)
                v.wait_ge(s_pTe, 1)
                for tb in range(5):
                    evac_vector(v, tb)
                v.wait_ge(s_lame, 1)
                steps_v.did(v.tensor_tensor(neglam, lam2[:, 1:2], lam2[:, 0:1], ALU.subtract))
                steps_v.settle()
                steps_v.did(v.tensor_scalar(neglam, neglam, -LAM_INIT, None, ALU.add))
                steps_v.settle()
                steps_v.did(v.scalar_tensor_tensor(csel, const[:, C_ISC + 1:C_ISC + 2], neglam,
                                                   const[:, C_ISC:C_ISC + 1], ALU.mult, ALU.add))
                v.wait_ge(s_pt, 16)
                steps_v.did(v.tensor_tensor(ptm.rearrange("p (b g) -> p b g", b=NB), pt.rearrange("p (b g) -> p b g", b=NB),
                                            const[:, C_SEL:C_SEL + 16].unsqueeze(1).broadcast_to([P, NB, 16]), ALU.mult))
                steps_v.settle()
                steps_v.did(v.tensor_reduce(ptf[:, 0, :], ptm.rearrange("p (b g) -> p b g", b=NB), AX.X, ALU.add))
                steps_v.settle()
                steps_v.did(v.tensor_scalar(ptf[:, 1, :], ptf[:, 0, :], 16.0, const[:, C_PAGE:C_PAGE + 1],
                                            ALU.mult, ALU.add))
                steps_v.settle()
                steps_v.did(v.tensor_scalar(ptf[:, 2, :], ptf[:, 1, :], 1.0, None, ALU.add))
                steps_v.settle()
                steps_v.did(v.tensor_copy(rowidx[:, 0:NB], ptf[:, 1, :]))
                steps_v.did(v.tensor_copy(rowidx[:, NB:2 * NB], ptf[:, 2, :]))
                lam = prmT[:, :, 39]
                steps_v.did(v.tensor_scalar(sp[:, 0, :], lam, -1.0, None, ALU.mult))
                steps_v.settle()
                v.tensor_tensor(sp[:, 0, :], sp[:, 0, :], lam, ALU.max).then_inc(s_spl[0], 1)
                steps_v.did(v.tensor_scalar(sp[:, 7, :], lam, -1.0, 0.0, ALU.mult, ALU.max))
                v.wait_ge(s_spl[1], 1)
                steps_v.did(v.tensor_scalar(sp[:, 2, :], sp[:, 1, :], 2.0, None, ALU.add))
                steps_v.settle()
                steps_v.did(v.reciprocal(sp[:, 2, :], sp[:, 2, :]))
                steps_v.settle()
                steps_v.did(v.tensor_tensor(sp[:, 2, :], sp[:, 2, :], sp[:, 1, :], ALU.mult))
                steps_v.settle()
                steps_v.did(v.tensor_tensor(sp[:, 3, :], sp[:, 2, :], sp[:, 2, :], ALU.mult))
                steps_v.settle()
                steps_v.did(v.tensor_scalar(sp[:, 4, :], sp[:, 3, :], 1.0 / 17, 1.0 / 15, ALU.mult, ALU.add))
                for k in range(13, 0, -2):
                    steps_v.settle()
                    steps_v.did(v.tensor_tensor(sp[:, 4, :], sp[:, 4, :], sp[:, 3, :], ALU.mult))
                    steps_v.settle()
                    steps_v.did(v.tensor_scalar(sp[:, 4, :], sp[:, 4, :], 1.0 / k, None, ALU.add))
                steps_v.settle()
                steps_v.did(v.scalar_tensor_tensor(sp[:, 5, :], sp[:, 4, :], 2.0, sp[:, 2, :], ALU.mult, ALU.mult))
                steps_v.settle()
                steps_v.did(v.tensor_tensor(sp[:, 6, :], sp[:, 5, :], sp[:, 7, :], ALU.add))
                steps_v.settle()
                steps_v.did(v.tensor_scalar(sp8, sp[:, 6, :], -8.0, None, ALU.mult))

            @block.tensor
            def _(pe):
                pe.wait_ge(s_const, 16)
                pe.wait_ge(s_prm, 16 * 10)
                pe.transpose(PS[:, 7, 0:33], gains[0:33, :], ident[0:33, 0:33]).then_inc(s_gT, 1)
                for n in range(LB):
                    ins = pe.transpose(PS[:, 6, 40 * n:40 * n + 40], prm[0:40, n * P:(n + 1) * P], ident[0:40, 0:40])
                ins.then_inc(s_pT, 1)
                for tb in range(5):
                    turn(pe, tb, xs[:rows(tb), tb, :])

        qk = at(M_AT, 5 * 1536, "p (b n) -> p b n", b=5)
        vn = at(41472, 5 * 512, "p (b n) -> p b n", b=5)
        xlP = at(44032, LB * 515, "p (n t) -> p n t", n=LB)
        xlS = at(48152, LB * NB * 7, "p (n b j) -> p n b j", n=LB, b=NB)
        xc = at(A_AT, 2 * T, "p (a t) -> p a t", a=2)
        pnb = at(A_AT + 1600, 2 * 8, "p (a c) -> p a c", a=2)
        rg = at(48600, 2 * T, "p (a t) -> p a t", a=2)
        ig = at(49688, 2 * T, "p (a t) -> p a t", a=2)
        av = at(A_AT + 1616, T)
        th = at(A_AT + 2160, T)
        uu = at(A_AT + 2704, T)
        hx = at(A_AT + 3248, NB)
        s_xl, s_xle, s_pad = sem("xl_tile"), sem("xl_evac"), sem("conv_rows")
        s_xc, s_gate, s_sig, s_la = sem("xc_ready"), sem("gates_psum"), sem("gates"), sem("log_a")
        s_ab, s_tm, s_sr, s_lru = sem("a_and_tanh"), sem("one_minus_a2"), sem("root_u"), sem("lru_block")
        s_qkv, s_qkve = sem("qkv_tile"), sem("qkv_evac")
        XL0 = landed[0]

        def b_t(ap):
            return ap.rearrange("p (b t) -> p b t", b=NB)

        with nc.Block() as block:
            @block.sync
            def _(sp_):
                for a in range(2):
                    sp_.wait_ge(s_xl, 4 * (a + 1))
                    load_w(sp_, a, w_in[:, :, COL_L + HC * (2 + a):COL_L + HC * (3 + a)])
                for a in range(2):
                    sp_.wait_ge(s_xl, 4 * (a + 3))
                    load_w(sp_, a, w_in[:, :, HC * a:HC * (a + 1)])
                with sp_.Fori(1, 4) as i:
                    for a in range(2):
                        wait_apart(sp_, s_qkv, i * 10 + 5 * a - 5)
                        load_w(sp_, a, w_in[:, :, bass.ds(i * 512 + HC * a, HC)])
                        wait_apart(sp_, s_gate, i * 2 + a - 1)
                        for m, name in enumerate(("lru_wa", "lru_wx")):
                            sp_.dma_start(wab[:, a, m, :].unsqueeze(1),
                                          io[name][0].rearrange("n i j -> i n j")[:, bass.ds(i * 2 + a, 1), :]
                                          ).then_inc(s_wab[a], 16)

            @block.tensor
            def _(pe):
                for n in range(LB):
                    c, j = n // 2, n % 2
                    if j == 0:
                        pe.wait_ge(w_in_sem[c % 2], 16 * (c // 2 + 1))
                    for half in range(2):
                        k = 2 * n + half
                        if k >= 4:
                            pe.wait_ge(s_xle, k - 3)
                        for d in range(DC):
                            ins = pe.matmul(PS[:, k % 4, 0:HALF], W[:, c % 2, d, j * P:(j + 1) * P],
                                            xnT[:, d, half * HALF:(half + 1) * HALF], start=d == 0, stop=d == DC - 1)
                        ins.then_inc(s_xl, 1)
                pe.wait_ge(s_xle, 16)
                pe.sem_inc(s_qkve, 2)
                pe.sem_inc(s_sig, 1)
                with pe.Fori(0, 4) as i:
                    for a in range(2):
                        pe.wait_ge(w_in_sem[a], i * 16 + 48)
                        for tb in range(5):
                            k = 5 * a + tb
                            pe.wait_ge(s_qkve, i * 10 + k + 1)
                            for d in range(DC):
                                ins = pe.matmul(PS[:rows(tb), 4 + k % 2, 0:HC], xnT[:, d, tb * P:tb * P + rows(tb)],
                                                W[:, a, d, :], start=d == 0, stop=d == DC - 1)
                            ins.then_inc(s_qkv, 1)
                        pe.wait_ge(s_wab[a], i * 32 + 32)
                        pe.wait_ge(s_xc, i * 2 + a + 1)
                        pe.wait_ge(s_sig, i * 2 + a + 1)
                        for m in range(2):
                            pe.matmul(PS[:, 6 + m, :], wab[:, a, m, :], xc[:, a, 0:SEQ], start=True, stop=True)
                            ins = pe.matmul(PS[:, m, 0:NS], wab[:, a, m, :], xc[:, a, SEQ:T], start=True, stop=True)
                        ins.then_inc(s_gate, 1)

            @block.scalar
            def _(act):
                for n in range(LB):
                    act.wait_ge(s_xl, 2 * n + 1)
                    act.activation(xlP[:, n, 3:3 + HALF], PS[:, (2 * n) % 4, 0:HALF], ACT.Copy).then_inc(s_xle, 1)
                    act.wait_ge(s_xl, 2 * n + 2)
                    act.activation(xlP[:, n, 3 + HALF:515], PS[:, (2 * n + 1) % 4, 0:SEQ - HALF], ACT.Copy)
                    act.activation(xlS[:, n, :, 3:7], b_t(PS[:, (2 * n + 1) % 4, SEQ - HALF:HALF]),
                                   ACT.Copy).then_inc(s_xle, 1)

                def turn2(i, v_part):
                    for a in range(2):
                        for tb in range(5):
                            k = 5 * a + tb
                            wait_apart(act, s_qkv, i * 10 + k + 1)
                            if v_part:
                                dst = vn[:rows(tb), tb, HC * a:HC * (a + 1)]
                            else:
                                dst = qk[:rows(tb), tb, bass.ds(i * 512 + HC * a, HC)]
                            act.activation(dst, PS[:rows(tb), 4 + k % 2, 0:HC], ACT.Copy).then_inc(s_qkve, 1)
                        act.wait_ge(s_gate, i * 2 + a + 1)
                        for m, dst in ((0, rg), (1, ig)):
                            act.activation(dst[:, a, 0:SEQ], PS[:, 6 + m, :], ACT.Sigmoid, bias=pnb[:, a, 5 + m:6 + m])
                            ins = act.activation(dst[:, a, SEQ:T], PS[:, m, 0:NS], ACT.Sigmoid,
                                                 bias=pnb[:, a, 5 + m:6 + m])
                        ins.then_inc(s_sig, 1)
                        act.wait_ge(s_la, i * 2 + a + 1)
                        act.activation(av, rg[:, a, :], ACT.Exp)
                        act.activation(th, rg[:, a, :], ACT.Tanh, scale=-1.0).then_inc(s_ab, 1)
                        act.wait_ge(s_tm, i * 2 + a + 1)
                        act.activation(uu, th, ACT.Sqrt).then_inc(s_sr, 1)

                with act.Fori(0, 3) as i:
                    turn2(i, False)
                turn2(3, True)

            @block.vector
            def _(v):
                v.memset(xlP[:, :, 0:3], 0.0)
                v.tensor_copy(xlS[:, :, :, 0:3], prmT[:, :, 0:24].rearrange("p n (b j) -> p n b j", b=NB)).then_inc(s_pad, 1)
                v.wait_ge(s_pad, 1)
                v.wait_ge(s_xle, 16)
                with steps_v.loop(4, 2 * 19) as i:
                    for a in range(2):
                        n = i * 2 + a
                        steps_v.did(v.tensor_copy(pnb[:, a, 0:7].unsqueeze(1), prmT[:, bass.ds(n, 1), 32:39]))
                        steps_v.did(v.tensor_copy(pnb[:, a, 7:8], sp8[:, bass.ds(n, 1)]))
                        steps_v.settle()
                        xs_in = [xlP[:, bass.ds(n, 1), j:j + SEQ] for j in range(CW)]
                        xs_smp = [xlS[:, bass.ds(n, 1), :, j:j + NT].rearrange("p a b t -> p (a b) t") for j in range(CW)]
                        oP, oS = xc[:, a, 0:SEQ].unsqueeze(1), b_t(xc[:, a, SEQ:T])
                        steps_v.did(v.tensor_scalar(oP, xs_in[0], pnb[:, a, 0:1], pnb[:, a, 4:5], ALU.mult, ALU.add))
                        steps_v.did(v.tensor_scalar(oS, xs_smp[0], pnb[:, a, 0:1], pnb[:, a, 4:5], ALU.mult, ALU.add))
                        for j in range(1, CW):
                            steps_v.settle()
                            if j < CW - 1:
                                steps_v.did(v.scalar_tensor_tensor(oP, xs_in[j], pnb[:, a, j:j + 1], oP, ALU.mult, ALU.add))
                                steps_v.did(v.scalar_tensor_tensor(oS, xs_smp[j], pnb[:, a, j:j + 1], oS, ALU.mult, ALU.add))
                            else:
                                v.scalar_tensor_tensor(oP, xs_in[j], pnb[:, a, j:j + 1], oP, ALU.mult, ALU.add)
                                v.scalar_tensor_tensor(oS, xs_smp[j], pnb[:, a, j:j + 1], oS, ALU.mult,
                                                       ALU.add).then_inc(s_xc, 1)
                        v.wait_ge(s_sig, i * 2 + a + 2)
                        v.tensor_scalar(rg[:, a, :], rg[:, a, :], pnb[:, a, 7:8], None, ALU.mult).then_inc(s_la, 1)
                        steps_v.did(v.tensor_tensor(ig[:, a, :], ig[:, a, :], xc[:, a, :], ALU.mult))
                        v.wait_ge(s_ab, i * 2 + a + 1)
                        steps_v.did(v.tensor_tensor(uu, av, av, ALU.mult))
                        steps_v.settle()
                        v.scalar_tensor_tensor(th, uu, 1.0, th, ALU.add, ALU.mult).then_inc(s_tm, 1)
                        v.wait_ge(s_sr, i * 2 + a + 1)
                        steps_v.did(v.tensor_tensor(uu, uu, ig[:, a, :], ALU.mult))
                        steps_v.settle()
                        steps_v.did(v.tensor_tensor_scan(lruT[:, bass.ds(n, 1), 0:SEQ].rearrange("p a t -> p (a t)"),
                                                         av[:, 0:SEQ], uu[:, 0:SEQ], 0.0, ALU.mult, ALU.add))
                        hs = lruT[:, bass.ds(n, 1), SEQ:T].rearrange("p a (b t) -> p (a b) t", b=NB)
                        aS, uS = b_t(av[:, SEQ:T]), b_t(uu[:, SEQ:T])
                        prev = prmT[:, bass.ds(n, 1), 24:32].rearrange("p a b -> p (a b)").unsqueeze(2)
                        for t in range(NT):
                            steps_v.did(v.tensor_tensor(hx.unsqueeze(2), aS[:, :, t:t + 1], prev, ALU.mult))
                            steps_v.settle()
                            ins = v.tensor_tensor(hs[:, :, t:t + 1], hx.unsqueeze(2), uS[:, :, t:t + 1], ALU.add)
                            if t < NT - 1:
                                steps_v.did(ins)
                                steps_v.settle()
                            else:
                                ins.then_inc(s_lru, 1)
                            prev = hs[:, :, t:t + 1]
                        v.wait_ge(s_lru, i * 2 + a + 1)

        qT = at(0, NH * T, "p (h t) -> p h t", h=NH)
        kT = at(4352, NG * T, "p (g t) -> p g t", g=NG)
        rtmp = at(6528, 2 * 4 * 192, "p (b a g e) -> p b a g e", b=2, a=4, g=24)
        last = at(8064, LB * 36, "p (n c) -> p n c", n=LB)
        lastrows = at(8400, LW)
        s_rope, s_qkt, s_qke, s_last, s_lastT, s_lrow = (sem("rotated"), sem("qk_transposed"), sem("qk_evac"),
                                                        sem("last_cols"), sem("last_rows"), sem("last_rows_sbuf"))

        with nc.Block() as block:
            @block.vector
            def _(v):
                v.tensor_copy(last[:, :, 0:24].rearrange("p n (b j) -> p n b j", b=NB), xlS[:, :, :, 4:7])
                v.tensor_copy(last[:, :, 24:32], lruT[:, :, SEQ + NT - 1:T:NT])
                v.tensor_copy(last[:, :, 32:35], xlP[:, :, 512:515])
                v.tensor_copy(last[:, :, 35:36], lruT[:, :, SEQ - 1:SEQ]).then_inc(s_last, 1)
                for tb in range(5):
                    np_ = rows(tb)
                    t1 = qk[:np_, tb, :].rearrange("p (g e) -> p g e", g=24)[:, :, 0:8]
                    t2 = qk[:np_, tb, :].rearrange("p (g e) -> p g e", g=24)[:, :, 8:16]
                    cs = const[:np_, C_CS + 16 * tb:C_CS + 16 * tb + 8].unsqueeze(1).broadcast_to([np_, 24, 8])
                    sn = const[:np_, C_CS + 16 * tb + 8:C_CS + 16 * tb + 16].unsqueeze(1).broadcast_to([np_, 24, 8])
                    tmp = rtmp[:np_, tb % 2]
                    if tb >= 2:
                        v.wait_ge(s_rope, tb - 1)
                    for m, (x, y) in enumerate(((t1, cs), (t2, sn), (t2, cs), (t1, sn))):
                        steps_v.did(v.tensor_tensor(tmp[:, m], x, y, ALU.mult))
                    steps_v.settle()
                    v.tensor_tensor(t1, tmp[:, 0], tmp[:, 1], ALU.subtract)
                    v.tensor_tensor(t2, tmp[:, 2], tmp[:, 3], ALU.add).then_inc(s_rope, 1)
                v.wait_ge(s_lastT, 1)
                v.tensor_copy(lastrows[0:36, :].rearrange("p (a n) -> p a n", a=2), PS[0:36, 4:6, :]).then_inc(s_lrow, 1)

            @block.tensor
            def _(pe):
                pe.wait_ge(s_last, 1)
                for n in range(LB):
                    ins = pe.transpose(PS[0:36, 4 + n // 4, (n % 4) * P:(n % 4 + 1) * P], last[:, n, :], ident)
                ins.then_inc(s_lastT, 1)
                for tb in range(5):
                    pe.wait_ge(s_rope, tb + 1)
                    for q in range(3):
                        n = 3 * tb + q
                        if n >= 4:
                            pe.wait_ge(s_qke, n - 3)
                        for j in range(4):
                            ins = pe.transpose(PS[:, n % 4, j * P:j * P + rows(tb)],
                                               qk[:rows(tb), tb, (4 * q + j) * P:(4 * q + j + 1) * P], ident[:rows(tb), :rows(tb)])
                        ins.then_inc(s_qkt, 1)

            @block.scalar
            def _(act):
                for tb in range(5):
                    for q in range(3):
                        n = 3 * tb + q
                        dst = qT[:, 4 * q:4 * q + 4, tb * P:tb * P + rows(tb)] if q < 2 else kT[:, :, tb * P:tb * P + rows(tb)]
                        act.wait_ge(s_qkt, n + 1)
                        act.activation(dst, PS[:, n % 4, :].rearrange("p (j t) -> p j t", j=4)[:, :, 0:rows(tb)],
                                       ACT.Copy).then_inc(s_qke, 1)

            @block.sync
            def _(sp_):
                kp = io["k_prompt"][0, 0].rearrange("(b p) g c -> b p (g c)", p=P)
                vp = io["v_prompt"][0, 0].rearrange("(b p) g c -> b p (g c)", p=P)
                ks = io["k_sample"][0].rearrange("b t g c -> (b t) (g c)")
                vs = io["v_sample"][0].rearrange("b t g c -> (b t) (g c)")
                for tb in range(5):
                    store(sp_, vp[tb] if tb < TB else vs, vn[:rows(tb), tb, :])
                for tb in range(5):
                    sp_.wait_ge(s_rope, tb + 1)
                    store(sp_, kp[tb] if tb < TB else ks, qk[:rows(tb), tb, 1024:1536])
                sp_.wait_ge(s_lrow, 1)
                store(sp_, io["conv_sample"][0].rearrange("b j c -> (b j) c"), lastrows[0:24, :])
                store(sp_, io["h_sample"][0], lastrows[24:32, :])
                store(sp_, io["conv_prompt"][0, 0], lastrows[32:35, :])
                store(sp_, io["h_prompt"][0], lastrows[35:36, :])
                sp_.wait_ge(out_done, 16 * outs[0])

        pb = at(8064, 2 * 2 * SEQ, "p (b c k) -> p b c k", b=2, c=2)
        wTb = at(10112, 2 * SEQ, "p (b k) -> p b k", b=2)
        dg = at(11136, 2 * 2 * P, "p (b c k) -> p b c k", b=2, c=2)
        st = at(11648, 2 * 8, "p (b c) -> p b c", b=2)
        qbd = at(39008, NB * NG * 64, "p (b g c) -> p b g c", b=NB, g=NG)
        kTn = at(44032, NG * NS, "p (g t) -> p g t", g=NG)
        s_qbd = sem("q_blockdiag")
        s_S, s_nb, s_p, s_dg = sem("scores"), sem("neg_max"), sem("exp"), sem("diagonals")
        s_wt, s_wte, s_pv, s_att = sem("weights_T"), sem("weights_T_sbuf"), sem("values"), sem("att_sbuf")
        s_mk = sem("masked")
        its = [(h, qb) for h in range(NH) for qb in range(TB)]
        SC = HD ** -0.5

        with nc.Block() as block:
            @block.gpsimd
            def _(g_):
                steps_g.did(g_.memset(qbd, 0.0))
                for c in range(2):
                    for g in range(NG):
                        for r in range(2):
                            col = 16 * g + 8 * c + 4 * r
                            steps_g.settle()
                            steps_g.did(g_.tensor_copy(qbd[64 * c:64 * c + 64, :, g, col:col + 4],
                                           qT[64 * c:64 * c + 64, 2 * g + r, SEQ:T].rearrange("p (b t) -> p b t", b=NB)))
                steps_g.settle()
                g_.tensor_copy(kTn, kT[:, :, SEQ:T]).then_inc(s_qbd, 1)

            @block.tensor
            def _(pe):
                def scores(it):
                    h, qb = its[it]
                    if it >= 2:
                        pe.wait_ge(s_p, it - 1)
                    for c in range(2):
                        ins = pe.matmul(PS[:, c + 2 * (it % 2), 0:(qb + 1) * P], qT[64 * c:64 * c + 64, h, qb * P:(qb + 1) * P],
                                        kT[64 * c:64 * c + 64, h // 2, 0:(qb + 1) * P], start=True, stop=True)
                    ins.then_inc(s_S, 1)

                def weights(it):
                    h, qb = its[it]
                    pe.wait_ge(s_dg, it + 1)
                    if it >= 2:
                        pe.wait_ge(s_wte, it - 1)
                    for kb in range(qb + 1):
                        for c in range(2):
                            ins = pe.matmul(PS[:, 4 + it % 2, kb * P:(kb + 1) * P], pb[:, it % 2, c, kb * P:(kb + 1) * P],
                                            dg[:, it % 2, c, :], start=c == 0, stop=c == 1)
                    ins.then_inc(s_wt, 1)

                def values(it):
                    h, qb = its[it]
                    pe.wait_ge(s_wte, it + 1)
                    if it >= 2:
                        pe.wait_ge(s_att, it - 1)
                    for kb in range(qb + 1):
                        ins = pe.matmul(PS[:, 6 + it % 2, 0:P], vn[:, kb, (h // 2) * P:(h // 2 + 1) * P],
                                        wTb[:, it % 2, kb * P:(kb + 1) * P], start=kb == 0, stop=kb == qb)
                    ins.then_inc(s_pv, 1)

                scores(0)
                for it in range(len(its) + 1):
                    if it + 1 < len(its):
                        scores(it + 1)
                    if it < len(its):
                        weights(it)
                    if it >= 1:
                        values(it - 1)

            @block.vector
            def _(v):
                def front(it):
                    h, qb = its[it]
                    b0 = 2 * (it % 2)
                    v.wait_ge(s_S, it + 1)
                    dgl = PS[:, b0:b0 + 2, qb * P:(qb + 1) * P]
                    steps_v.did(v.tensor_tensor(dgl, dgl, causal.unsqueeze(1).broadcast_to([P, 2, P]), ALU.add))
                    steps_v.settle()
                    steps_v.did(v.tensor_reduce(st[:, it % 2, 0:2], PS[:, b0:b0 + 2, 0:(qb + 1) * P], AX.X, ALU.max))
                    steps_v.settle()
                    v.tensor_scalar(st[:, it % 2, 2:4], st[:, it % 2, 0:2], -SC, None, ALU.mult).then_inc(s_nb, 1)

                def back(it):
                    v.wait_ge(s_p, it + 1)
                    if it >= 2:
                        v.wait_ge(s_wt, it - 1)
                    steps_v.did(v.reciprocal(st[:, it % 2, 6:8], st[:, it % 2, 4:6]))
                    steps_v.settle()
                    steps_v.did(v.tensor_scalar(st[:, it % 2, 7:8], st[:, it % 2, 7:8], neglam, None, ALU.mult))
                    steps_v.settle()
                    for c in range(2):
                        ins = v.tensor_scalar(dg[:, it % 2, c, :], ident, st[:, it % 2, 6 + c:7 + c], None, ALU.mult)
                    ins.then_inc(s_dg, 1)

                def take(it):
                    h, qb = its[it]
                    v.wait_ge(s_pv, it + 1)
                    v.tensor_copy(attT[:, h, qb * P:(qb + 1) * P], PS[:, 6 + it % 2, 0:P]).then_inc(s_att, 1)

                front(0)
                for it in range(len(its) + 1):
                    if it + 1 < len(its):
                        front(it + 1)
                    if it < len(its):
                        back(it)
                    if it >= 1:
                        take(it - 1)

            @block.scalar
            def _(act):
                def exps(it):
                    h, qb = its[it]
                    act.wait_ge(s_nb, it + 1)
                    if it >= 2:
                        act.wait_ge(s_wt, it - 1)
                    for c in range(2):
                        ins = act.activation(pb[:, it % 2, c, 0:(qb + 1) * P], PS[:, c + 2 * (it % 2), 0:(qb + 1) * P],
                                             ACT.Exp, bias=st[:, it % 2, 2 + c:3 + c], scale=SC,
                                             accum_out=st[:, it % 2, 4 + c:5 + c])
                    ins.then_inc(s_p, 1)

                def take_weights(it):
                    h, qb = its[it]
                    act.wait_ge(s_wt, it + 1)
                    if it >= 2:
                        act.wait_ge(s_pv, it - 1)
                    act.activation(wTb[:, it % 2, 0:(qb + 1) * P], PS[:, 4 + it % 2, 0:(qb + 1) * P],
                                   ACT.Copy).then_inc(s_wte, 1)

                exps(0)
                for it in range(len(its)):
                    if it + 1 < len(its):
                        exps(it + 1)
                    take_weights(it)

        KTs = at(33792, 4 * 512, "p (s k) -> p s k", s=4)
        pS = at(35840, PAST + NS)
        wTs = at(37920, 17 * 64, "p (j c) -> p j c", j=17)
        snew = at(44160, NS)
        comb = at(44192, 64)
        sst = at(44256, 16)
        cache = [io[n].rearrange("l n (r k) g c -> (l n r) (k g c)", k=8) for n in ("cache_k", "cache_v")]
        slots = at(W_AT, 16384, "p (s m) -> p s m", s=4)
        kv = at(W_AT, 16384, "p (s j n) -> p s j n", s=4, j=8)
        s_cache = [sem(f"cache_slot{s}_in") for s in range(4)]
        s_T, s_evA, s_evB, s_sc = sem("k_transposed"), sem("kT_scalar"), sem("kT_vector"), sem("sample_scores")
        s_new, s_nbs, s_ps, s_c64 = sem("new_scores"), sem("sample_neg_max"), sem("sample_exp"), sem("sample_diag")
        s_w, s_wA, s_wB, s_v, s_pve = (sem("sample_weights_T"), sem("weights_T_scalar"), sem("weights_T_vector"),
                                      sem("sample_values"), sem("sample_att_sbuf"))
        PAIRS = NB // 2

        with nc.Block() as block:
            @block.gpsimd
            def _(g_):
                for pr in range(PAIRS):
                    for what in range(2):
                        for bb in range(2):
                            for hf in range(2):
                                b, slot = 2 * pr + bb, 2 * bb + hf
                                if what == 0 and pr >= 1:
                                    g_.wait_ge(s_v, 2 * (pr - 1) + bb + 1)
                                if what == 1:
                                    g_.wait_ge(s_T, 16 * b + 8 * (hf + 1))
                                g_.indirect_dma_start(
                                    slots[:, slot, :], None, cache[what],
                                    bass.IndirectOffsetOnAxis(ap=rowidx[:, hf * NB + b:hf * NB + b + 1], axis=0)
                                ).then_inc(s_cache[slot], 16)

            @block.tensor
            def _(pe):
                def turn_keys(pr, n):
                    bb, u = n // 16, n % 16
                    qd, g = u // 4, u % 4
                    U = 32 * pr + n
                    slot = 2 * bb + u // 8
                    if u % 8 == 0:
                        pe.wait_ge(s_cache[slot], 16 * (2 * pr + 1))
                    if n < 3 and pr:
                        pe.wait_ge(s_wA, pr)
                        pe.wait_ge(s_wB, 2 * pr)
                    elif U >= 3:
                        pe.wait_ge((s_evA, s_evB)[(U - 3) % 2], (U - 3) // 2 + 1)
                    for j in range(4):
                        ins = pe.transpose(PS[:, 5 + U % 3, j * P:(j + 1) * P],
                                           kv[:, slot, (qd % 2) * 4 + j, g * P:(g + 1) * P], ident)
                    ins.then_inc(s_T, 1)

                def score(pr, n):
                    bb, u = n // 16, n % 16
                    qd, g = u // 4, u % 4
                    U = 32 * pr + n
                    pe.wait_ge((s_evA, s_evB)[U % 2], U // 2 + 1)
                    if n == 0 and pr:
                        pe.wait_ge(s_ps, pr)
                    pe.matmul(PS[64 * bb:64 * bb + 64, qd, :], qbd[:, 2 * pr + bb, g, :], KTs[:, U % 4, :],
                              start=g == 0, stop=g == 3).then_inc(s_sc, 1)

                for pr in range(PAIRS):
                    for n in range(33):
                        if n < 32:
                            turn_keys(pr, n)
                        if n:
                            score(pr, n - 1)
                    if pr:
                        pe.wait_ge(s_pve, pr)
                    for bb in range(2):
                        for g in range(NG):
                            ins = pe.matmul(PS[64 * bb:64 * bb + 64, 4, 0:NS], qbd[:, 2 * pr + bb, g, :], kTn[:, g, :],
                                            start=g == 0, stop=g == 3)
                    ins.then_inc(s_new, 1)
                    pe.wait_ge(s_c64, pr + 1)
                    pe.wait_ge(s_evA, 16 * (pr + 1))
                    pe.wait_ge(s_evB, 16 * (pr + 1))
                    for j in range(16):
                        ins = pe.matmul(PS[:, 5 + j // 8, (j % 8) * 64:(j % 8 + 1) * 64], pS[:, j * P:(j + 1) * P], comb,
                                        start=True, stop=True)
                        if j % 8 == 7:
                            ins.then_inc(s_w, 1)
                    pe.matmul(PS[0:NS, 7, 0:64], pS[:, PAST:PAST + NS], comb, start=True, stop=True).then_inc(s_w, 1)
                    pe.wait_ge(s_wA, pr + 1)
                    pe.wait_ge(s_wB, 2 * (pr + 1))
                    for bb in range(2):
                        for hf in range(2):
                            pe.wait_ge(s_cache[2 * bb + hf], 16 * (2 * pr + 2))
                        for g in range(NG):
                            o = 32 * bb + 8 * g
                            dst = PS[:, 4, 64 + o:64 + o + 8]
                            for j in range(16):
                                pe.matmul(dst, kv[:, 2 * bb + j // 8, j % 8, g * P:(g + 1) * P], wTs[:, j, o:o + 8],
                                          start=j == 0, stop=False)
                            ins = pe.matmul(dst, vn[0:NS, TB, g * P:(g + 1) * P], wTs[0:NS, 16, o:o + 8],
                                            start=False, stop=True)
                        ins.then_inc(s_v, 1)

            def take_keys(eng, copy, pr, parity, s):
                for n in range(parity, 32, 2):
                    U = 32 * pr + n
                    eng.wait_ge(s_T, U + 1)
                    if U >= 4:
                        eng.wait_ge(s_sc, U - 3)
                    copy(KTs[:, U % 4, :], PS[:, 5 + U % 3, :]).then_inc(s, 1)

            @block.scalar
            def _(act):
                def copy(dst, src):
                    return act.activation(dst, src, ACT.Copy)
                for pr in range(PAIRS):
                    take_keys(act, copy, pr, 0, s_evA)
                    act.wait_ge(s_nbs, pr + 1)
                    act.activation(pS[:, 0:PAST].rearrange("p (a k) -> p a k", a=4), PS[:, 0:4, :], ACT.Exp, bias=sst[:, 3:4],
                                   scale=SC, accum_out=sst[:, 4:5])
                    act.activation(pS[:, PAST:PAST + NS], snew, ACT.Exp, bias=sst[:, 3:4], scale=SC,
                                   accum_out=sst[:, 5:6]).then_inc(s_ps, 1)
                    act.wait_ge(s_w, 3 * pr + 1)
                    copy(wTs[:, 0:8, :].rearrange("p j c -> p (j c)"), PS[:, 5, :]).then_inc(s_wA, 1)

            @block.vector
            def _(v):
                for pr in range(PAIRS):
                    take_keys(v, v.tensor_copy, pr, 1, s_evB)
                    v.wait_ge(s_new, pr + 1)
                    steps_v.did(v.tensor_tensor(snew, PS[:, 4, 0:NS], const[:, C_NEW + NS * pr:C_NEW + NS * (pr + 1)], ALU.add))
                    steps_v.did(v.tensor_reduce(sst[:, 0:1], PS[:, 0:4, :], AX.XY, ALU.max))
                    steps_v.settle()
                    steps_v.did(v.tensor_reduce(sst[:, 1:2], snew, AX.X, ALU.max))
                    steps_v.settle()
                    steps_v.did(v.tensor_tensor(sst[:, 2:3], sst[:, 0:1], sst[:, 1:2], ALU.max))
                    steps_v.settle()
                    v.tensor_scalar(sst[:, 3:4], sst[:, 2:3], -SC, None, ALU.mult).then_inc(s_nbs, 1)
                    v.wait_ge(s_ps, pr + 1)
                    steps_v.did(v.tensor_tensor(sst[:, 6:7], sst[:, 4:5], sst[:, 5:6], ALU.add))
                    steps_v.settle()
                    steps_v.did(v.reciprocal(sst[:, 7:8], sst[:, 6:7]))
                    steps_v.settle()
                    v.tensor_scalar(comb, const[:, C_COMB:C_COMB + 64], sst[:, 7:8], csel, ALU.mult,
                                    ALU.mult).then_inc(s_c64, 1)
                    v.wait_ge(s_w, 3 * pr + 2)
                    v.tensor_copy(wTs[:, 8:16, :].rearrange("p j c -> p (j c)"), PS[:, 6, :]).then_inc(s_wB, 1)
                    v.wait_ge(s_w, 3 * pr + 3)
                    v.tensor_copy(wTs[0:NS, 16, :], PS[0:NS, 7, 0:64]).then_inc(s_wB, 1)
                    v.wait_ge(s_v, 2 * (pr + 1))
                    cols = slice(SEQ + 2 * NT * pr, SEQ + 2 * NT * (pr + 1))
                    v.tensor_copy(attT[:, :, cols].rearrange("p h (b t) -> p h b t", b=2),
                                  PS[:, 4, 64:128].rearrange("p (b h t) -> p h b t", b=2, h=NH)).then_inc(s_pve, 1)

        w_att_up = io["w_att_up"][0].rearrange("(k p) n -> p k n", p=P)
        w_lru_up = io["w_lru_up"][0].rearrange("(k p) n -> p k n", p=P)
        w_out = io["w_out"][0].rearrange("(k p) n -> p k n", p=P)
        w_q = io["peer_wq"][0].rearrange("(k p) n -> p k n", p=P)

        def load_up(sp_, cols):
            sp_.dma_start(W[:, 2, 0:AC, :], w_att_up[:, :, cols]).then_inc(w_in_sem[2], 16)
            sp_.dma_start(W[:, 2, AC:DC, :], w_lru_up[:, :, cols]).then_inc(w_in_sem[2], 16)

        def stage7_first_loads(sp_):
            load_w(sp_, 0, w_in[:, :, COL_GA:COL_GA + HC])
            load_w(sp_, 1, w_in[:, :, COL_GL:COL_GL + HC])
            load_up(sp_, slice(0, HC))

        SQW = AC * T // 2
        asq = at(33792, AC * T)
        ars = at(38144, AC * T)
        af = at(A_AT, AC * T)
        g08 = at(44300, 1)
        s_asq, s_ams, s_art, s_aps = sem("att_squares"), sem("att_mean_squares"), sem("att_root"), sem("att_sums")

        with nc.Block() as block:
            @block.sync
            def _(sp_):
                stage7_first_loads(sp_)

            @block.vector
            def _(v):
                for r in range(2):
                    sl = slice(SQW * r, SQW * (r + 1))
                    v.tensor_tensor(asq[:, sl], af[:, sl], af[:, sl], ALU.mult).then_inc(s_asq, 1)
                steps_v.did(v.tensor_scalar(g08, gT[:, 32:33], 1.0 - LAM_INIT, None, ALU.mult))
                for r in range(2):
                    v.wait_ge(s_aps, 8 * (r + 1))
                    v.tensor_scalar(ars[:, SQW * r:SQW * (r + 1)].rearrange("p (k t) -> p k t", k=8), PS[:, :, 0:HALF],
                                    1.0 / P, EPS, ALU.mult, ALU.add).then_inc(s_ams, 1)
                for r in range(2):
                    sl = slice(SQW * r, SQW * (r + 1))
                    v.wait_ge(s_art, r + 1)
                    steps_v.did(v.reciprocal(ars[:, sl], ars[:, sl]))
                    steps_v.settle()
                    steps_v.did(v.scalar_tensor_tensor(af[:, sl], af[:, sl], g08, ars[:, sl], ALU.mult, ALU.mult))

            @block.scalar
            def _(act):
                for r in range(2):
                    sl = slice(SQW * r, SQW * (r + 1))
                    act.wait_ge(s_ams, r + 1)
                    act.activation(ars[:, sl], ars[:, sl], ACT.Sqrt).then_inc(s_art, 1)

            @block.tensor
            def _(pe):
                for r in range(2):
                    pe.wait_ge(s_asq, r + 1)
                    if r:
                        pe.wait_ge(s_ams, r)
                    for k in range(8):
                        o = SQW * r + HALF * k
                        pe.matmul(PS[:, k, 0:HALF], ones, asq[:, o:o + HALF], start=True, stop=True).then_inc(s_aps, 1)

        sga = at(44400, 4 * HALF, "p (x t) -> p x t", x=4)
        sgl = at(45500, 4 * HALF, "p (x t) -> p x t", x=4)
        s_ga, s_gl, s_up = sem("ga_tile"), sem("gl_tile"), sem("up_tiles")
        s_sga, s_sgl, s_mA, s_mB = sem("ga_sigmoid"), sem("gl_sigmoid"), sem("att_merged"), sem("lru_merged")
        NCH = D // HC
        L7 = 96

        with nc.Block() as block:
            @block.sync
            def _(sp_):
                with sp_.Fori(1, NCH) as i:
                    wait_apart(sp_, s_ga, i * 4)
                    load_w(sp_, 0, w_in[:, :, bass.ds(i * HC + COL_GA, HC)])
                    wait_apart(sp_, s_gl, i * 4)
                    load_w(sp_, 1, w_in[:, :, bass.ds(i * HC + COL_GL, HC)])
                    wait_apart(sp_, s_up, i * 4)
                    load_up(sp_, bass.ds(i * HC, HC))
                sp_.wait_ge(s_ga, 4 * NCH)
                load_w(sp_, 0, w_out[:, :, 0:HC])
                sp_.wait_ge(s_gl, 4 * NCH)
                load_w(sp_, 1, w_out[:, :, HC:2 * HC])

            @block.tensor
            def _(pe):
                with pe.Fori(0, NCH) as i:
                    for part, tile_done, merged in ((0, s_ga, s_mA), (1, s_gl, s_mB)):
                        pe.wait_ge(w_in_sem[part], i * 16 + (L7 + 16))
                        for x in range(4):
                            pe.wait_ge(merged, i * 4 + x + 1)
                            for d in range(DC):
                                ins = pe.matmul(PS[:, 4 * part + x, 0:HALF], W[:, part, d, (x // 2) * P:(x // 2 + 1) * P],
                                                xnT[:, d, (x % 2) * HALF:(x % 2 + 1) * HALF], start=d == 0, stop=d == DC - 1)
                            ins.then_inc(tile_done, 1)
                    pe.wait_ge(w_in_sem[2], i * 32 + 32)
                    for x in range(4):
                        for part, src, free in ((0, attT, s_sga), (1, lruT, s_sgl)):
                            pe.wait_ge(free, i * 4 + x + 1)
                            for d in range(AC):
                                ins = pe.matmul(PS[:, 4 * part + x, 0:HALF],
                                                W[:, 2, AC * part + d, (x // 2) * P:(x // 2 + 1) * P],
                                                src[:, d, (x % 2) * HALF:(x % 2 + 1) * HALF], start=d == 0, stop=d == AC - 1)
                        ins.then_inc(s_up, 1)

            @block.scalar
            def _(act):
                with act.Fori(0, NCH) as i:
                    for part, dst, tile_done, s, merged in ((0, sga, s_ga, s_sga, s_mA), (1, sgl, s_gl, s_sgl, s_mB)):
                        for x in range(4):
                            act.wait_ge(tile_done, i * 4 + x + 1)
                            act.wait_ge(merged, i * 4 + x + 1)
                            act.activation(dst[:, x, :], PS[:, 4 * part + x, 0:HALF], ACT.Sigmoid).then_inc(s, 1)

            @block.vector
            def _(v):
                v.sem_inc(s_mA, 4)
                v.sem_inc(s_mB, 4)
                with steps_v.loop(NCH, 4) as i:
                    for x in range(4):
                        dst = mT[:, bass.ds(i * 2 + x // 2, 1), (x % 2) * HALF:(x % 2 + 1) * HALF].rearrange("p a t -> p (a t)")
                        v.wait_ge(s_up, i * 4 + x + 1)
                        v.tensor_tensor(dst, sga[:, x, :], PS[:, x, 0:HALF], ALU.mult).then_inc(s_mA, 1)
                        steps_v.did(v.tensor_tensor(sgl[:, x, :], sgl[:, x, :], PS[:, 4 + x, 0:HALF], ALU.mult))
                        steps_v.settle()
                        v.tensor_tensor(dst, dst, sgl[:, x, :], ALU.add).then_inc(s_mB, 1)

        h = at(X_AT, 5 * D, "p (b n) -> p b n", b=5)
        s_xr, s_o, s_hadd = sem("x_again"), sem("out_tile"), sem("h_tile")
        L8 = L7 + 16 * NCH

        def stream_pairs(sp_, src, tile_done, per, upto=NCH):
            with sp_.Fori(1, upto // 2) as i:
                for a in range(2):
                    wait_apart(sp_, tile_done, i * (2 * per) + per * (a - 1))
                    load_w(sp_, a, src[:, :, bass.ds(i * (2 * HC) + HC * a, HC)])

        with nc.Block() as block:
            @block.sync
            def _(sp_):
                for tb in range(5):
                    sp_.dma_start(h[:rows(tb), tb, :], xp[tb] if tb < TB else xsm).then_inc(s_xr, 16)
                stream_pairs(sp_, w_out, s_o, 5)
                for a in range(2):
                    sp_.wait_ge(s_o, 5 * (NCH - 1 + a))
                    load_w(sp_, a, w_q[:, :, HC * a:HC * (a + 1)])

            @block.tensor
            def _(pe):
                with pe.Fori(0, NCH // 2) as i:
                    for a in range(2):
                        pe.wait_ge(w_in_sem[a], i * 16 + (L8 + 16))
                        for tb in range(5):
                            pe.wait_ge(s_hadd, i * 10 + 5 * a + tb + 1)
                            for d in range(DC):
                                ins = pe.matmul(PS[:rows(tb), tb, 0:HC], mT[:, d, tb * P:tb * P + rows(tb)], W[:, a, d, :],
                                                start=d == 0, stop=d == DC - 1)
                            ins.then_inc(s_o, 1)

            @block.vector
            def _(v):
                v.sem_inc(s_hadd, 5)
                v.wait_ge(s_xr, 16 * 5)
                with v.Fori(0, NCH // 2) as i:
                    for a in range(2):
                        for tb in range(5):
                            v.wait_ge(s_o, i * 10 + 5 * a + tb + 1)
                            dst = h[:rows(tb), tb, bass.ds(i * (2 * HC) + HC * a, HC)]
                            v.tensor_tensor(dst, dst, PS[:rows(tb), tb, 0:HC], ALU.add).then_inc(s_hadd, 1)

        xn2T = mT
        xsc = at(R_AT, 2 * D, "p (b n) -> p b n", b=2)
        kkT = at(26624, 2 * NK, "p (a n) -> p a n", a=2)
        kk = at(26880, 2 * P, "p (a n) -> p a n", a=2)
        s_kk, s_kkt, s_kke = sem("peer_keys_in"), sem("peer_keys_T"), sem("peer_keys_sbuf")
        squares, evac_scalar, scale, scale_block, evac_vector, turn = transposed_norm(1, h, xn2T, 16)

        with nc.Block() as block:
            @block.sync
            def _(sp_):
                for a in range(2):
                    sp_.dma_start(kk[:, a, :], io[f"peer_k{a + 1}"][0]).then_inc(s_kk, 16)

            @block.scalar
            def _(act):
                squares(act)
                act.wait_ge(s_kkt, 1)
                act.activation(kkT, PS[:, 4, 0:2 * NK].rearrange("p (a n) -> p a n", a=2), ACT.Copy).then_inc(s_kke, 1)
                evac_scalar(act)

            @block.vector
            def _(v):
                scale(v)
                scale_block(v, 0, xsc[:, 0, :])
                scale_block(v, 1, xsc[:, 1, :])
                for tb in range(5):
                    evac_vector(v, tb)
                    if tb + 2 < 5:
                        v.wait_ge(s_tr, 20 + 4 * (tb + 1))
                        scale_block(v, tb + 2, xsc[:rows(tb + 2), tb % 2, :])

            @block.tensor
            def _(pe):
                pe.wait_ge(s_kk, 32)
                for a in range(2):
                    ins = pe.transpose(PS[:, 4, a * NK:(a + 1) * NK], kk[:, a, :], ident)
                ins.then_inc(s_kkt, 1)
                for tb in range(5):
                    turn(pe, tb, xsc[:rows(tb), tb % 2, :])

        eid = at(26880, T).bitcast(I32)
        gate = at(27424, T)
        FR = 48600
        R0 = R_AT
        qc = at(R0, 2 * 2 * T, "p (a u t) -> p a u t", a=2, u=2)
        S2 = at(R0 + 2176, 5 * 2 * NK, "p (b u n) -> p b u n", b=5, u=2)
        cand = at(R0 + 3456, 5 * 256, "p (b m) -> p b m", b=5)
        cand2 = at(R0 + 4736, 5 * 256, "p (b m) -> p b m", b=5)
        eq = at(R0 + 6016, 5 * 256, "p (m i) -> p m i", i=16)
        picked = at(R0 + 7296, 5 * 256, "p (m i) -> p m i", i=16)
        vals = at(L_AT, 160, "p (b u k) -> p b u k", b=5, u=2)
        idx = at(L_AT + 160, 160, "p (b u k) -> p b u k", b=5, u=2).bitcast(U32)
        idxf = at(L_AT + 320, 160, "p (b u k) -> p b u k", b=5, u=2)
        best = at(L_AT + 480, 80, "p (b k) -> p b k", b=5)
        sel = at(L_AT + 560, 80, "p (b k) -> p b k", b=5).bitcast(U32)
        selp = at(L_AT + 640, 160, "p (a m) -> p a m", a=2).bitcast(U32)
        selpf = at(L_AT + 800, 160, "p (a m) -> p a m", a=2)
        pick = at(L_AT + 960, 160, "p (a m) -> p a m", a=2)
        rel = at(L_AT + 1120, 80, "p (b k) -> p b k", b=5)
        gexp = at(L_AT + 1200, 80, "p (b k) -> p b k", b=5)
        gsum = at(L_AT + 1280, 5)
        eidS = at(L_AT + 1300, P).bitcast(I32)
        gateS = at(L_AT + 1428, P)
        s_qp, s_qpe = sem("query_tile"), sem("query_evac")
        s_ks, s_l1, s_rel, s_gexp = sem("key_scores"), sem("key_scores_read"), sem("gate_logits"), sem("gate_exp")
        s_z4 = sem("spare_rows_set")
        L10 = L8 + 16 * NCH // 2

        def key_scores(tb, u=slice(0, 2)):
            return PS[:, 4 + tb // 2, (tb % 2) * 2 * NK:(tb % 2 + 1) * 2 * NK].rearrange("p (u n) -> p u n", u=2)[:, u]

        with nc.Block() as block:
            @block.sync
            def _(sp_):
                stream_pairs(sp_, w_q, s_qp, 4)

            @block.tensor
            def _(pe):
                pe.wait_ge(s_z4, 1)
                with pe.Fori(0, NCH // 2) as i:
                    for a in range(2):
                        pe.wait_ge(w_in_sem[a], i * 16 + (L10 + 16))
                        for x in range(4):
                            pe.wait_ge(s_qpe, i * 8 + 4 * a + x + 1)
                            for d in range(DC):
                                ins = pe.matmul(PS[:, x, 0:HALF], W[:, a, d, (x // 2) * P:(x // 2 + 1) * P],
                                                xn2T[:, d, (x % 2) * HALF:(x % 2 + 1) * HALF], start=d == 0, stop=d == DC - 1)
                            ins.then_inc(s_qp, 1)
                        pe.wait_ge(s_qpe, i * 8 + (4 * a + 8))
                        pe.wait_ge(s_l1, i * 2 + a + 1)
                        for tb in range(5):
                            for u in range(2):
                                ins = pe.matmul(key_scores(tb, u)[0:rows(tb)], qc[:, a, u, tb * P:tb * P + rows(tb)],
                                                kkT[:, u, :], start=True, stop=True)
                        ins.then_inc(s_ks, 1)

            @block.scalar
            def _(act):
                act.sem_inc(s_qpe, 4)
                with act.Fori(0, NCH // 2) as i:
                    for a in range(2):
                        for x in range(4):
                            act.wait_ge(s_qp, i * 8 + 4 * a + x + 1)
                            act.activation(qc[:, a, x // 2, (x % 2) * HALF:(x % 2 + 1) * HALF], PS[:, x, 0:HALF],
                                           ACT.Copy).then_inc(s_qpe, 1)
                        act.wait_ge(s_rel, i * 2 + a + 1)
                        act.activation(gexp, rel, ACT.Exp).then_inc(s_gexp, 1)

            @block.vector
            def _(v):
                did, settle = steps_v.did, lambda: settle_apart(steps_v)
                tiles = [(tb, u) for tb in range(5) for u in range(2)]
                for tb in range(5):
                    ins = v.memset(key_scores(tb), 0.0)
                ins.then_inc(s_z4, 1)
                v.sem_inc(s_l1, 1)
                per = 5 * 8 + 2 + 5 * 5 + 2 + 1 + 6 + 2 + 4
                with steps_v.loop(PH, per) as head:
                    wait_apart(v, s_ks, head + 1)
                    for tb, u in tiles:
                        did(v.max(vals[:, tb, u, 0:8], key_scores(tb, u)))
                    settle()
                    for tb, u in tiles:
                        did(v.max_index(idx[:, tb, u, 0:8], vals[:, tb, u, 0:8], key_scores(tb, u)))
                    for tb, u in tiles:
                        ins = v.match_replace(S2[:, tb, u, :], vals[:, tb, u, 0:8], key_scores(tb, u), -3e38)
                    ins.then_inc(s_l1, 1)
                    wait_apart(v, s_l1, head + 2)
                    for tb, u in tiles:
                        did(v.max(vals[:, tb, u, 8:16], S2[:, tb, u, :]))
                    settle()
                    for tb, u in tiles:
                        did(v.max_index(idx[:, tb, u, 8:16], vals[:, tb, u, 8:16], S2[:, tb, u, :]))
                    did(v.tensor_tensor(cand.rearrange("p b (i j) -> p b i j", i=16),
                                        vals[:, :, 0, :].unsqueeze(3).broadcast_to([P, 5, 16, 16]),
                                        vals[:, :, 1, :].unsqueeze(2).broadcast_to([P, 5, 16, 16]), ALU.add))
                    settle()
                    did(v.tensor_copy(idxf, idx))
                    for tb in range(5):
                        did(v.max(best[:, tb, 0:8], cand[:, tb]))
                    settle()
                    for tb in range(5):
                        did(v.max_index(sel[:, tb, 0:8], best[:, tb, 0:8], cand[:, tb]))
                    for tb in range(5):
                        did(v.match_replace(cand2[:, tb], best[:, tb, 0:8], cand[:, tb], -3e38))
                    settle()
                    for tb in range(5):
                        did(v.max(best[:, tb, 8:16], cand2[:, tb]))
                    settle()
                    for tb in range(5):
                        did(v.max_index(sel[:, tb, 8:16], best[:, tb, 8:16], cand2[:, tb]))
                    v.tensor_tensor(rel, best, best[:, :, 0:1].broadcast_to([P, 5, 16]), ALU.subtract).then_inc(s_rel, 1)
                    settle()
                    flat = sel.rearrange("p b k -> p (b k)")
                    did(v.tensor_scalar(selp[:, 0, :], flat, 4, None, ALU.logical_shift_right))
                    did(v.tensor_scalar(selp[:, 1, :], flat, 15, None, ALU.bitwise_and))
                    settle()
                    did(v.tensor_copy(selpf, selp))
                    for u in range(2):
                        settle()
                        did(v.tensor_tensor(eq, selpf[:, u, :].unsqueeze(2).broadcast_to([P, 80, 16]),
                                            const[:, C_IOTA:C_IOTA + 16].unsqueeze(1).broadcast_to([P, 80, 16]), ALU.is_equal))
                        settle()
                        did(v.tensor_tensor(picked.rearrange("p (b k) i -> p b k i", b=5),
                                            eq.rearrange("p (b k) i -> p b k i", b=5),
                                            idxf[:, :, u, :].unsqueeze(2).broadcast_to([P, 5, 16, 16]), ALU.mult))
                        settle()
                        did(v.tensor_reduce(pick[:, u, :], picked, AX.X, ALU.add))
                    settle()
                    pk = pick.rearrange("p u (b k) -> p u b k", b=5)
                    did(v.scalar_tensor_tensor(eid[:, 0:SEQ].rearrange("p (b m) -> p b m", b=TB)[:, :, bass.ds(head * 16, 16)],
                                               pk[:, 0, 0:TB], float(NK), pk[:, 1, 0:TB], ALU.mult, ALU.add))
                    did(v.scalar_tensor_tensor(eidS[0:NS, bass.ds(head * 16, 16)], pk[0:NS, 0, TB], float(NK),
                                               pk[0:NS, 1, TB], ALU.mult, ALU.add))
                    v.wait_ge(s_gexp, head + 1)
                    did(v.tensor_reduce(gsum, gexp, AX.X, ALU.add))
                    settle()
                    did(v.reciprocal(gsum, gsum))
                    settle()
                    did(v.tensor_tensor(gate[:, 0:SEQ].rearrange("p (b m) -> p b m", b=TB)[:, :, bass.ds(head * 16, 16)],
                                        gexp[:, 0:TB], gsum[:, 0:TB].unsqueeze(2).broadcast_to([P, TB, 16]), ALU.mult))
                    did(v.tensor_tensor(gateS[0:NS, bass.ds(head * 16, 16)], gexp[0:NS, TB],
                                        gsum[0:NS, TB:TB + 1].broadcast_to([NS, 16]), ALU.mult))
                    settle()
                for g in range(4):
                    for src, dst in ((eidS, eid), (gateS, gate)):
                        did(v.tensor_copy(dst[NS * g:NS * (g + 1), SEQ:T], src[0:NS, NS * g:NS * (g + 1)]))

        RING = 8
        ring_u = [at(s * D, D) for s in range(RING)]
        ring_v = [at(27968 + s * D, D) for s in range(RING)]
        Xn = at(44352, D)
        g2b = at(46400, D)
        fgb = at(48448, D)
        dgr = at(50496, 4 * P, "p (s k) -> p s k", s=4)
        acts = at(51008, P)
        coef = at(51136, P)
        act8 = at(51264, RING)
        stage_u = at(51272, RING).bitcast(I32)
        stage_v = at(51280, RING).bitcast(I32)
        fsq = at(51296, 1)
        frs = at(51297, 1)
        gl = at(51300, P)
        s_gb = sem("gains_in")
        s_ru = [sem(f"u_slot{s}_in") for s in range(RING)]
        s_rv = [sem(f"v_slot{s}_in") for s in range(RING)]
        s_u, s_vv, s_stu, s_stv = sem("u_used"), sem("v_used"), sem("u_rows_staged"), sem("v_rows_staged")
        s_act, s_gelu, s_coef, s_dgr = sem("acts"), sem("gelu"), sem("coefs"), sem("diag_ready")
        s_ffn, s_fs, s_fm, s_fr, s_y = sem("ffn_psum"), sem("y_squares"), sem("y_mean_square"), sem("y_root"), sem("y_ready")
        s_rep = sem("x_replicated")
        s_x0 = sem("x_sample_scaled")
        TURNS = SLOTS // RING
        S_TURNS = SLOTS // 4 // RING
        VP = PS[:, 4:8, :]

        with nc.Block() as block:
            @block.sync
            def _(sp_):
                sp_.dma_start(g2b, io["norm2_g"][0].partition_broadcast(P)).then_inc(s_gb, 16)
                sp_.dma_start(fgb, io["final_g"].partition_broadcast(P)).then_inc(s_gb, 16)
                yp = io["y_prompt"][0].rearrange("(b p) d -> p b d", p=P)
                with sp_.Fori(0, TB - 1) as b:
                    wait_apart(sp_, s_y, b + 2)
                    sp_.dma_start(yp[:, bass.ds(b, 1), :], h[:, bass.ds(b, 1), :]).then_inc(out_done, 16)
                outs[0] += TB - 1
                sp_.wait_ge(s_x0, 1)
                for g in range(1, 4):
                    sp_.dma_start(Xn[NS * g:NS * (g + 1), :], Xn[0:NS, :]).then_inc(s_rep, 16)
                sp_.wait_ge(s_y, TB + 1)
                store(sp_, yp[:, TB - 1, :], h[:, TB - 1, :])
                sp_.wait_ge(s_y, TB + 2)
                store(sp_, io["y_sample"].rearrange("b t d -> (b t) d"), h[0:NS, TB, :])
                sp_.wait_ge(out_done, 16 * outs[0])

            @block.gpsimd
            def _(g_):
                g_.sem_inc(s_u, RING)
                g_.sem_inc(s_vv, RING)
                kinds = {"u": (io["peer_u"][0], ring_u, s_ru, stage_u, s_stu, s_u),
                         "v": (io["peer_v"][0], ring_v, s_rv, stage_v, s_stv, s_vv)}

                def turn_(kinds_, turn_no, firsts):
                    for q in range(RING // 4):
                        for kind in kinds_:
                            table, ring, landed_, stage, staged, used = kinds[kind]
                            wait_apart(g_, used, firsts[kind] + (4 * q + 4))
                            g_.tensor_copy(stage[:, 4 * q:4 * q + 4],
                                           eid[:, bass.ds(firsts[kind] + 4 * q, 4)]).then_inc(staged, 1)
                            wait_apart(g_, staged, turn_no[kind] * 2 + (q + 1))
                            for s in range(4 * q, 4 * q + 4):
                                g_.indirect_dma_start(ring[s], None, table,
                                                      bass.IndirectOffsetOnAxis(ap=stage[:, s:s + 1], axis=0)
                                                      ).then_inc(landed_[s], 16)

                with g_.Fori(0, TURNS) as i:
                    turn_("u", {"u": i}, {"u": i * RING})
                with g_.Fori(0, (TB - 1) * TURNS) as i:
                    turn_("uv", {"u": i + TURNS, "v": i}, {"u": i * RING + SLOTS, "v": i * RING})
                u0, v0 = TB * TURNS, (TB - 1) * TURNS
                with g_.Fori(0, S_TURNS) as i:
                    for k in range(TURNS // S_TURNS):
                        n = i * (TURNS // S_TURNS) + (v0 + k)
                        if k == 0:
                            turn_("uv", {"u": i + u0, "v": n}, {"u": i * RING + u0 * RING, "v": n * RING})
                        else:
                            turn_("v", {"v": n}, {"v": n * RING})
                with g_.Fori(u0, u0 + S_TURNS) as i:
                    turn_("v", {"v": i}, {"v": i * RING})

            @block.vector
            def _(v):
                v.wait_ge(s_gb, 32)

                def u_phase(b, turns):
                    with steps_v.loop(turns, 1) as i:
                        for s in range(RING):
                            v.wait_ge(s_ru[s], (b * TURNS + i) * 16 + 16)
                            v.tensor_tensor_reduce(ring_u[s], ring_u[s], Xn, 1.0, 0.0, ALU.mult, ALU.add,
                                                   act8[:, s:s + 1]).then_inc(s_u, 1)
                        wait_apart(v, s_u, b * SLOTS + i * RING + 2 * RING)
                        steps_v.did(v.tensor_copy(acts[:, bass.ds(i * RING, RING)], act8))
                        settle_apart(steps_v)
                    v.sem_inc(s_act, 1)

                def coefs(b, gl_, coef_, gate_):
                    v.wait_ge(s_gelu, b + 1)
                    v.wait_ge(s_vv, b * SLOTS + RING)
                    v.tensor_tensor(coef_, gl_, gate_, ALU.mult).then_inc(s_coef, 1)

                def finish(b, np_, hb):
                    v.wait_ge(s_fs, b + 1)
                    v.tensor_scalar(frs[0:np_], fsq[0:np_], 1.0 / D, EPS, ALU.mult, ALU.add).then_inc(s_fm, 1)
                    v.wait_ge(s_fr, b + 1)
                    steps_v.did(v.reciprocal(frs[0:np_], frs[0:np_]))
                    steps_v.settle()
                    v.scalar_tensor_tensor(hb, VP[0:np_].rearrange("p a n -> p (a n)"), frs[0:np_], fgb[0:np_],
                                           ALU.mult, ALU.mult).then_inc(s_y, 1)

                def block_of(b):
                    return h[:, bass.ds(b, 1), :].rearrange("p a n -> p (a n)")

                def scaled(b):
                    steps_v.did(v.scalar_tensor_tensor(Xn, block_of(b), rstd[:, bass.ds(b, 1)], g2b, ALU.mult, ALU.mult))
                    settle_apart(steps_v)

                v.sem_inc(s_y, 1)
                scaled(0)
                u_phase(0, TURNS)
                coefs(0, gl, coef, gate[:, 0:SLOTS])
                with v.Fori(1, TB) as b:
                    start = steps_v.base + steps_v.n
                    steps_v.base, steps_v.n = start + (b - 1) * (TURNS + 2), 0
                    scaled(b)
                    u_phase(b, TURNS)
                    finish(b - 1, P, block_of(b - 1))
                    coefs(b, gl, coef, gate[:, bass.ds(b * SLOTS, SLOTS)])
                steps_v.base, steps_v.n = start + (TB - 1) * (TURNS + 2), 0
                v.scalar_tensor_tensor(Xn[0:NS], h[0:NS, TB, :], rstd[0:NS, 4:5], g2b[0:NS], ALU.mult, ALU.mult).then_inc(s_x0, 1)
                v.wait_ge(s_rep, 48)
                u_phase(TB, S_TURNS)
                finish(TB - 1, P, h[:, TB - 1, :])
                coefs(TB, gl[:, 0:NS], coef[:, 0:NS], gate[:, SEQ:T])
                finish(TB, NS, h[0:NS, TB, :])

            @block.scalar
            def _(act):
                def v_phase(b, turns, np_, hb, table):
                    wait_apart(act, s_act, b + 1)
                    act.activation(gl[:, 0:turns * RING], acts[:, 0:turns * RING], ACT.Gelu).then_inc(s_gelu, 1)
                    act.wait_ge(s_coef, b + 1)
                    with act.Fori(0, turns) as i:
                        for s in range(RING):
                            wait_apart(act, s_vv, b * SLOTS + i * RING + (RING + s - 3))
                            act.activation(dgr[:, s % 4, 0:np_], table, ACT.Copy,
                                           scale=coef[:, bass.ds(i * RING + s, 1)]).then_inc(s_dgr, 1)
                    wait_apart(act, s_ffn, b + 1)
                    act.activation(hb, VP[0:np_].rearrange("p a n -> p (a n)"), ACT.Square,
                                   accum_out=fsq[0:np_]).then_inc(s_fs, 1)
                    act.wait_ge(s_fm, b + 1)
                    act.activation(frs[0:np_], frs[0:np_], ACT.Sqrt).then_inc(s_fr, 1)

                with act.Fori(0, TB) as b:
                    v_phase(b, TURNS, P, h[:, bass.ds(b, 1), :].rearrange("p a n -> p (a n)"), ident)
                v_phase(TB, S_TURNS, NS, h[0:NS, TB, :], const[:, C_REP:C_REP + NS])

            @block.tensor
            def _(pe):
                def v_phase(b, turns, np_, rhs):
                    pe.wait_ge(s_y, b + 1)

                    def turn_(i, first):
                        for s in range(RING):
                            pe.wait_ge(s_dgr, b * SLOTS + i * RING + (s + 1))
                            pe.wait_ge(s_rv[s], (b * TURNS + i) * 16 + 16)
                            for n in range(4):
                                ins = pe.matmul(VP[0:np_, n, :], dgr[:, s % 4, 0:np_], ring_v[s][:, 512 * n:512 * (n + 1)],
                                                start=first and s == 0, stop=False)
                            ins.then_inc(s_vv, 1)

                    turn_(0, True)
                    with pe.Fori(1, turns) as i:
                        turn_(i, False)
                    for n in range(4):
                        ins = pe.matmul(VP[0:np_, n, :], ident[0:np_, 0:np_], rhs(n), start=False, stop=True)
                    ins.then_inc(s_ffn, 1)

                with pe.Fori(0, TB) as b:
                    v_phase(b, TURNS, P, lambda n: h[:, bass.ds(b, 1), 512 * n:512 * (n + 1)].rearrange("p a n -> p (a n)"))
                v_phase(TB, S_TURNS, NS, lambda n: h[0:NS, TB, 512 * n:512 * (n + 1)])


_INS = ['x_prompt', 'x_sample', 'cache_k', 'cache_v', 'state_conv', 'state_h', 'page_table', 'norm1_g', 'w_in',
        'lambda_q1', 'lambda_k1', 'lambda_q2', 'lambda_k2', 'subln_g', 'conv_w', 'conv_b', 'lru_wa', 'lru_ba',
        'lru_wx', 'lru_bx', 'lru_lambda', 'w_att_up', 'w_lru_up', 'w_out', 'norm2_g', 'peer_wq', 'peer_k1',
        'peer_k2', 'peer_u', 'peer_v', 'final_g']
_OUTS = {'y_prompt': (1, SEQ, D), 'y_sample': (NB, NT, D), 'k_prompt': (1, 1, SEQ, NG, P), 'v_prompt': (1, 1, SEQ, NG, P),
         'conv_prompt': (1, 1, CW - 1, LW), 'h_prompt': (1, 1, LW), 'k_sample': (1, NB, NT, NG, P),
         'v_sample': (1, NB, NT, NG, P), 'conv_sample': (1, NB, CW - 1, LW), 'h_sample': (1, NB, LW)}


def kernel(**inputs):
    import concourse.bacc as _bacc
    from concourse.bass_utils import run_bass_kernel_spmd as _run

    nc = _bacc.Bacc("TRN2", target_bir_lowering=False, num_devices=1)
    arrays, io = {}, {}
    for name in _INS + ['const']:
        a = np.ascontiguousarray(inputs[name]) if name != 'const' else shape_constants()
        arrays[f"in_{name}_dram"] = a
        io[name] = nc.dram_tensor(f"in_{name}_dram", a.shape, mybir.dt.from_np(a.dtype), kind="ExternalInput").ap()
    for name, shape in _OUTS.items():
        io[name] = nc.dram_tensor(f"out_{name}_dram", shape, F32, kind="ExternalOutput").ap()
    build_trunk(nc, io)
    r = _run(nc, [arrays], core_ids=[0])
    return tuple(r.results[0][f"out_{name}_dram"] for name in _OUTS)
```

```python
from contextlib import ExitStack, contextmanager

import numpy as np

import concourse.bass as bass
from concourse import mybir

F32 = mybir.dt.float32
I32 = mybir.dt.int32
U32 = mybir.dt.uint32
ALU = mybir.AluOpType
ACT = mybir.ActivationFunctionType
AX = mybir.AxisListType

P = 128
D = 2048
DC = D // P
SEQ, NB, NT = 512, 8, 4
TB = SEQ // P
NS = NB * NT
T = SEQ + NS
HALF = T // 2
NH, NG, HD = 8, 4, 64
AC = NH
LW, LB = 1024, 8
CW = 4
PAST, PAGE = 2048, 128
NK, PH, TOPK = 128, 8, 16
SLOTS = PH * TOPK
EPS = 1e-6
LAM_INIT = 0.8 - 0.6 * float(np.exp(-0.3 * 0))
HC = 256
COL_Q, COL_K, COL_V, COL_L, COL_GA, COL_GL = 0, 1024, 1536, 2048, 3072, 5120
NEG = -1e30

C_ID, C_CAUSAL, C_NEW, C_COMB, C_CS, C_ISC, C_REP, C_IOTA, C_ONE, C_PAGE, C_SEL, C_TOK = (
    0, 128, 256, 384, 448, 528, 530, 562, 578, 706, 707, 723)
C_END = 726


def shape_constants():
    c = np.zeros((P, C_END), np.float32)
    p = np.arange(P)
    c[:, C_ID:C_ID + P] = np.eye(P)
    c[:, C_CAUSAL:C_CAUSAL + P] = np.where(p[None, :] <= p[:, None], 0.0, NEG)
    bb, g, comp, r, t = p // 64, p // 16 % 4, p // 8 % 2, p // 4 % 2, p % 4
    key = np.arange(NS)
    for pair in range(NB // 2):
        seen = (key[None, :] // NT == (2 * pair + bb)[:, None]) & (key[None, :] % NT <= t[:, None])
        c[:, C_NEW + NS * pair:C_NEW + NS * (pair + 1)] = np.where(seen, 0.0, NEG)
    c[p, C_COMB + bb * 32 + g * 8 + r * 4 + t] = 1.0
    inv = np.float32(500000.0) ** (-np.arange(8, dtype=np.float32) * np.float32(2.0) / np.float32(16))
    for tb in range(TB + 1):
        pos = (tb * P + p if tb < TB else PAST + p % NT).astype(np.float32)
        ang = (pos[:, None] * inv[None, :]).astype(np.float32)
        c[:, C_CS + 16 * tb:C_CS + 16 * tb + 8] = np.cos(ang)
        c[:, C_CS + 16 * tb + 8:C_CS + 16 * tb + 16] = np.sin(ang)
    c[:, C_ISC] = comp == 0
    c[:, C_ISC + 1] = comp == 1
    c[p, C_REP + p % NS] = 1.0
    c[:, C_IOTA:C_IOTA + 16] = np.arange(16)
    c[:, C_ONE:C_ONE + P] = 1.0
    c[:, C_PAGE] = 2 * (p % 8)
    c[p, C_SEL + p // 8] = 1.0
    c[:, C_TOK], c[:, C_TOK + 1], c[:, C_TOK + 2] = p, P + p, 2 * P + p % NS
    return c


class Steps:

    def __init__(self, eng, sem):
        self.eng, self.sem, self.base, self.n = eng, sem, 0, 0

    def did(self, ins):
        ins.then_inc(self.sem, 1)
        self.n += 1
        return ins

    def settle(self):
        self.eng.wait_ge(self.sem, self.base + self.n)

    @contextmanager
    def loop(self, trips, per):
        start = self.base + self.n
        with self.eng.Fori(0, trips) as i:
            self.base, self.n = start + i * per, 0
            yield i
            assert self.n == per, (self.n, per)
        self.base, self.n = start + trips * per, 0


def build_trunk(nc, io):
    with ExitStack() as ctx:
        def sem(name):
            return ctx.enter_context(nc.semaphore(name))

        AREA = 53100
        area = ctx.enter_context(nc.sbuf_tensor("area", [P, AREA], F32))
        PS = ctx.enter_context(nc.psum_tensor("PS", [P, 8, 512], F32))

        def at(off, words, spec=None, **dims):
            assert off + words <= AREA
            v = area[:, off:off + words]
            return v.rearrange(spec, **dims) if spec else v

        W_AT, X_AT, A_AT, L_AT, M_AT = 0, 16384, 25088, 29440, 33792
        R_AT = M_AT + 8704
        K_AT = AREA - 1500
        W = at(W_AT, 16384, "p (s k n) -> p s k n", s=4, k=DC)
        xnT = at(X_AT, DC * T, "p (k t) -> p k t", k=DC)
        attT = at(A_AT, AC * T, "p (h t) -> p h t", h=AC)
        lruT = at(L_AT, LB * T, "p (n t) -> p n t", n=LB)
        mT = at(M_AT, DC * T, "p (k t) -> p k t", k=DC)

        const = at(K_AT, C_END)
        ident, causal = const[:, C_ID:C_ID + P], const[:, C_CAUSAL:C_CAUSAL + P]
        ones = const[:, C_ONE:C_ONE + P]
        small_at = [K_AT + C_END]

        def small(words, spec=None, **dims):
            small_at[0] += words
            return at(small_at[0] - words, words, spec, **dims)

        prmT = small(LB * 40, "p (n c) -> p n c", n=LB)
        gT = small(33)
        ssq = small(5)
        rstd = small(5)
        lam2 = small(2)
        neglam = small(1)
        csel = small(1)
        sp8 = small(LB)
        rowidx = small(2 * NB).bitcast(I32)
        stats = small(64)

        xs = at(M_AT, 5 * D, "p (b n) -> p b n", b=5)
        junk = at(L_AT, 2 * D, "p (b n) -> p b n", b=2)
        prm = at(44100, LW)
        gains = at(45200, P)
        lamq = at(45400, 4 * HD, "p (a d) -> p a d", a=4)
        lamp = at(45700, 2 * HD, "p (a d) -> p a d", a=2)
        pt = at(45900, 16 * NB).bitcast(I32)
        ptm = at(46130, 16 * NB)
        sp = at(46000, 8 * LB, "p (a n) -> p a n", a=8)
        ptf = at(46300, 3 * NB, "p (a n) -> p a n", a=3)

        def rows(tb):
            return P if tb < TB else NS

        steps_v = Steps(nc.vector, sem("vector_steps"))
        steps_g = Steps(nc.gpsimd, sem("pool_steps"))
        held = {e.engine: sem(f"held_{n}") for n, e in enumerate((nc.vector, nc.scalar, nc.gpsimd, nc.tensor, nc.sync))}

        def settle_apart(steps):
            wait_apart(steps.eng, steps.sem, steps.base + steps.n)

        def wait_apart(eng, s, value):
            eng.wait_ge(s, value)
            eng.sem_inc(held[eng.engine], 1)

        out_done = sem("out_done")
        outs = [0]

        def store(eng, dst, src):
            eng.dma_start(dst, src).then_inc(out_done, 16)
            outs[0] += 1

        w_in = io["w_in"][0].rearrange("(k p) n -> p k n", p=P)

        s_const, s_prm, s_lamq, s_pt = sem("const_in"), sem("prm_in"), sem("lamq_in"), sem("pages_in")
        s_x = [sem(f"x_in{tb}") for tb in range(5)]
        s_sq, s_ms, s_root = sem("squares"), sem("mean_squares"), sem("root")
        s_xs, s_tr, s_ev_a, s_ev_v = sem("x_scaled"), sem("x_transposed"), sem("evac_scalar"), sem("evac_vector")
        s_gT, s_gTe, s_pT, s_pTe = sem("gains_tr"), sem("gains_ready"), sem("prm_tr"), sem("prm_ready")
        w_in_sem = [sem(f"w_slot{s}_in") for s in range(4)]
        s_lamw = sem("lam_parts")
        s_lame = sem("lam_exp")
        s_spl = [sem(f"softplus_{k}") for k in range(4)]

        def transposed_norm(k, src, dstT, gcol):
            nbank = 4 * 5

            def squares(act):
                if k == 0:
                    act.wait_ge(s_spl[3], 1)
                for tb in range(5):
                    if k == 0:
                        act.wait_ge(s_x[tb], 16)
                    if tb >= 2:
                        act.wait_ge(s_sq, 5 * k + tb - 1)
                    act.activation(junk[:rows(tb), tb % 2, :], src[:rows(tb), tb, :], ACT.Square,
                                   accum_out=ssq[:rows(tb), tb:tb + 1]).then_inc(s_sq, 1)
                act.wait_ge(s_ms, k + 1)
                act.activation(rstd, rstd, ACT.Sqrt).then_inc(s_root, 1)

            def evac_scalar(act):
                act.wait_ge(s_gTe, 1)
                for n in range(0, nbank, 2):
                    tb, q, np_ = n // 4, n % 4, rows(n // 4)
                    act.wait_ge(s_tr, nbank * k + n + 1)
                    for j in range(4):
                        d = 4 * q + j
                        ins = act.activation(dstT[:, d, tb * P:tb * P + np_], PS[:, n % 4, j * P:j * P + np_],
                                             ACT.Copy, scale=gT[:, gcol + d:gcol + d + 1])
                    ins.then_inc(s_ev_a, 1)

            def scale(v):
                v.wait_ge(s_sq, 5 * (k + 1))
                v.tensor_scalar(rstd, ssq, 1.0 / D, EPS, ALU.mult, ALU.add).then_inc(s_ms, 1)
                v.wait_ge(s_root, k + 1)
                steps_v.did(v.reciprocal(rstd, rstd))
                steps_v.settle()

            def scale_block(v, tb, dst):
                v.tensor_scalar(dst, src[:rows(tb), tb, :], rstd[:rows(tb), tb:tb + 1], None,
                                ALU.mult).then_inc(s_xs, 1)

            def evac_vector(v, tb):
                for n in (4 * tb + 1, 4 * tb + 3):
                    q, np_ = n % 4, rows(tb)
                    v.wait_ge(s_tr, nbank * k + n + 1)
                    for j in range(4):
                        d = 4 * q + j
                        ins = v.tensor_scalar(dstT[:, d, tb * P:tb * P + np_], PS[:, n % 4, j * P:j * P + np_],
                                              gT[:, gcol + d:gcol + d + 1], None, ALU.mult)
                    ins.then_inc(s_ev_v, 1)

            def turn(pe, tb, block):
                pe.wait_ge(s_xs, 5 * k + tb + 1)
                for q in range(4):
                    n = 4 * tb + q
                    if n >= 4:
                        pe.wait_ge((s_ev_a, s_ev_v)[n % 2], (nbank // 2) * k + (n - 4) // 2 + 1)
                    for j in range(4):
                        d = 4 * q + j
                        ins = pe.transpose(PS[:, n % 4, j * P:j * P + rows(tb)], block[:, d * P:(d + 1) * P],
                                           ident[:rows(tb), :rows(tb)])
                    ins.then_inc(s_tr, 1)

            return squares, evac_scalar, scale, scale_block, evac_vector, turn

        wab = at(A_AT + 1088, 2 * 256, "p (a m j) -> p a m j", a=2, m=2)
        s_wab = [sem(f"lru_w{a}_in") for a in range(2)]
        landed = [0, 0, 0, 0]

        def load_w(sp_, a, src):
            sp_.dma_start(W[:, a], src).then_inc(w_in_sem[a], 16)

        def load_gates(sp_, a, n):
            for m, name in enumerate(("lru_wa", "lru_wx")):
                sp_.dma_start(wab[:, a, m, :], io[name].rearrange("l n i j -> (l n) i j")[n]).then_inc(s_wab[a], 16)

        squares, evac_scalar, scale, scale_block, evac_vector, turn = transposed_norm(0, xs, xnT, 0)
        xp = io["x_prompt"][0].rearrange("(b p) d -> b p d", p=P)
        xsm = io["x_sample"].rearrange("b t d -> (b t) d")

        with nc.Block() as block:
            @block.sync
            def _(sp_):
                for tb in range(5):
                    sp_.dma_start(xs[:rows(tb), tb, :], xp[tb] if tb < TB else xsm).then_inc(s_x[tb], 16)
                    if tb == 0:
                        sp_.dma_start(const, io["const"]).then_inc(s_const, 16)
                        sp_.dma_start(gains[0:16, :], io["norm1_g"][0].rearrange("(k p) -> k p", p=P)).then_inc(s_prm, 16)
                        sp_.dma_start(gains[16:32, :], io["norm2_g"][0].rearrange("(k p) -> k p", p=P)).then_inc(s_prm, 16)
                        sp_.dma_start(gains[32:33, :], io["subln_g"]).then_inc(s_prm, 16)
                for a in range(2):
                    load_w(sp_, a, w_in[:, :, COL_L + HC * a:COL_L + HC * (a + 1)])
                for a in range(2):
                    load_gates(sp_, a, a)

            @block.scalar
            def _(act):
                act.dma_start(prm[0:24, :], io["state_conv"][0].rearrange("b j c -> (b j) c")).then_inc(s_prm, 16)
                act.dma_start(prm[24:32, :], io["state_h"][0]).then_inc(s_prm, 16)
                act.dma_start(prm[32:36, :], io["conv_w"][0]).then_inc(s_prm, 16)
                for r, name in enumerate(("conv_b", "lru_ba", "lru_bx", "lru_lambda")):
                    act.dma_start(prm[36 + r:37 + r, :], io[name]).then_inc(s_prm, 16)
                for r, name in enumerate(("lambda_q1", "lambda_k1", "lambda_q2", "lambda_k2")):
                    act.dma_start(lamq[:, r, :], io[name][0].partition_broadcast(P)).then_inc(s_lamq, 16)
                pages = io["page_table"]
                act.dma_start(pt, pages.rearrange("b g -> (b g)").partition_broadcast(P)).then_inc(s_pt, 16)
                squares(act)
                act.wait_ge(s_lamw, 1)
                act.activation(lam2, stats[:, 0:2], ACT.Exp).then_inc(s_lame, 1)
                evac_scalar(act)
                act.wait_ge(s_spl[0], 1)
                act.activation(sp[:, 1, :], sp[:, 0, :], ACT.Exp, scale=-1.0).then_inc(s_spl[1], 1)

            @block.vector
            def _(v):
                v.memset(ssq, 1.0).then_inc(s_spl[3], 1)
                scale(v)
                v.wait_ge(s_lamq, 64)
                for a in range(2):
                    ins = v.tensor_tensor_reduce(lamp[:, a, :], lamq[:, 2 * a, :], lamq[:, 2 * a + 1, :], 1.0, 0.0,
                                                 ALU.mult, ALU.add, stats[:, a:a + 1])
                ins.then_inc(s_lamw, 1)
                for tb in range(5):
                    scale_block(v, tb, xs[:rows(tb), tb, :])
                v.wait_ge(s_gT, 1)
                v.tensor_copy(gT, PS[:, 7, 0:33]).then_inc(s_gTe, 1)
                v.wait_ge(s_pT, 1)
                v.tensor_copy(prmT, PS[:, 6, 0:320].rearrange("p (n c) -> p n c", n=LB)).then_inc(s_pTe, 1)
                v.wait_ge(s_pTe, 1)
                for tb in range(5):
                    evac_vector(v, tb)
                v.wait_ge(s_lame, 1)
                steps_v.did(v.tensor_tensor(neglam, lam2[:, 1:2], lam2[:, 0:1], ALU.subtract))
                steps_v.settle()
                steps_v.did(v.tensor_scalar(neglam, neglam, -LAM_INIT, None, ALU.add))
                steps_v.settle()
                steps_v.did(v.scalar_tensor_tensor(csel, const[:, C_ISC + 1:C_ISC + 2], neglam,
                                                   const[:, C_ISC:C_ISC + 1], ALU.mult, ALU.add))
                v.wait_ge(s_pt, 16)
                steps_v.did(v.tensor_tensor(ptm.rearrange("p (b g) -> p b g", b=NB), pt.rearrange("p (b g) -> p b g", b=NB),
                                            const[:, C_SEL:C_SEL + 16].unsqueeze(1).broadcast_to([P, NB, 16]), ALU.mult))
                steps_v.settle()
                steps_v.did(v.tensor_reduce(ptf[:, 0, :], ptm.rearrange("p (b g) -> p b g", b=NB), AX.X, ALU.add))
                steps_v.settle()
                steps_v.did(v.tensor_scalar(ptf[:, 1, :], ptf[:, 0, :], 16.0, const[:, C_PAGE:C_PAGE + 1],
                                            ALU.mult, ALU.add))
                steps_v.settle()
                steps_v.did(v.tensor_scalar(ptf[:, 2, :], ptf[:, 1, :], 1.0, None, ALU.add))
                steps_v.settle()
                steps_v.did(v.tensor_copy(rowidx[:, 0:NB], ptf[:, 1, :]))
                steps_v.did(v.tensor_copy(rowidx[:, NB:2 * NB], ptf[:, 2, :]))
                lam = prmT[:, :, 39]
                steps_v.did(v.tensor_scalar(sp[:, 0, :], lam, -1.0, None, ALU.mult))
                steps_v.settle()
                v.tensor_tensor(sp[:, 0, :], sp[:, 0, :], lam, ALU.max).then_inc(s_spl[0], 1)
                steps_v.did(v.tensor_scalar(sp[:, 7, :], lam, -1.0, 0.0, ALU.mult, ALU.max))
                v.wait_ge(s_spl[1], 1)
                steps_v.did(v.tensor_scalar(sp[:, 2, :], sp[:, 1, :], 2.0, None, ALU.add))
                steps_v.settle()
                steps_v.did(v.reciprocal(sp[:, 2, :], sp[:, 2, :]))
                steps_v.settle()
                steps_v.did(v.tensor_tensor(sp[:, 2, :], sp[:, 2, :], sp[:, 1, :], ALU.mult))
                steps_v.settle()
                steps_v.did(v.tensor_tensor(sp[:, 3, :], sp[:, 2, :], sp[:, 2, :], ALU.mult))
                steps_v.settle()
                steps_v.did(v.tensor_scalar(sp[:, 4, :], sp[:, 3, :], 1.0 / 17, 1.0 / 15, ALU.mult, ALU.add))
                for k in range(13, 0, -2):
                    steps_v.settle()
                    steps_v.did(v.tensor_tensor(sp[:, 4, :], sp[:, 4, :], sp[:, 3, :], ALU.mult))
                    steps_v.settle()
                    steps_v.did(v.tensor_scalar(sp[:, 4, :], sp[:, 4, :], 1.0 / k, None, ALU.add))
                steps_v.settle()
                steps_v.did(v.scalar_tensor_tensor(sp[:, 5, :], sp[:, 4, :], 2.0, sp[:, 2, :], ALU.mult, ALU.mult))
                steps_v.settle()
                steps_v.did(v.tensor_tensor(sp[:, 6, :], sp[:, 5, :], sp[:, 7, :], ALU.add))
                steps_v.settle()
                steps_v.did(v.tensor_scalar(sp8, sp[:, 6, :], -8.0, None, ALU.mult))

            @block.tensor
            def _(pe):
                pe.wait_ge(s_const, 16)
                pe.wait_ge(s_prm, 16 * 10)
                pe.transpose(PS[:, 7, 0:33], gains[0:33, :], ident[0:33, 0:33]).then_inc(s_gT, 1)
                for n in range(LB):
                    ins = pe.transpose(PS[:, 6, 40 * n:40 * n + 40], prm[0:40, n * P:(n + 1) * P], ident[0:40, 0:40])
                ins.then_inc(s_pT, 1)
                for tb in range(5):
                    turn(pe, tb, xs[:rows(tb), tb, :])

        qk = at(M_AT, 5 * 1536, "p (b n) -> p b n", b=5)
        vn = at(41472, 5 * 512, "p (b n) -> p b n", b=5)
        xlP = at(44032, LB * 515, "p (n t) -> p n t", n=LB)
        xlS = at(48152, LB * NB * 7, "p (n b j) -> p n b j", n=LB, b=NB)
        xc = at(A_AT, 2 * T, "p (a t) -> p a t", a=2)
        pnb = at(A_AT + 1600, 2 * 8, "p (a c) -> p a c", a=2)
        rg = at(48600, 2 * T, "p (a t) -> p a t", a=2)
        ig = at(49688, 2 * T, "p (a t) -> p a t", a=2)
        av = at(A_AT + 1616, T)
        th = at(A_AT + 2160, T)
        uu = at(A_AT + 2704, T)
        hx = at(A_AT + 3248, NB)
        s_xl, s_xle, s_pad = sem("xl_tile"), sem("xl_evac"), sem("conv_rows")
        s_xc, s_gate, s_sig, s_la = sem("xc_ready"), sem("gates_psum"), sem("gates"), sem("log_a")
        s_ab, s_tm, s_sr, s_lru = sem("a_and_tanh"), sem("one_minus_a2"), sem("root_u"), sem("lru_block")
        s_qkv, s_qkve = sem("qkv_tile"), sem("qkv_evac")
        XL0 = landed[0]

        def b_t(ap):
            return ap.rearrange("p (b t) -> p b t", b=NB)

        with nc.Block() as block:
            @block.sync
            def _(sp_):
                for a in range(2):
                    sp_.wait_ge(s_xl, 4 * (a + 1))
                    load_w(sp_, a, w_in[:, :, COL_L + HC * (2 + a):COL_L + HC * (3 + a)])
                for a in range(2):
                    sp_.wait_ge(s_xl, 4 * (a + 3))
                    load_w(sp_, a, w_in[:, :, HC * a:HC * (a + 1)])
                with sp_.Fori(1, 4) as i:
                    for a in range(2):
                        wait_apart(sp_, s_qkv, i * 10 + 5 * a - 5)
                        load_w(sp_, a, w_in[:, :, bass.ds(i * 512 + HC * a, HC)])
                        wait_apart(sp_, s_gate, i * 2 + a - 1)
                        for m, name in enumerate(("lru_wa", "lru_wx")):
                            sp_.dma_start(wab[:, a, m, :].unsqueeze(1),
                                          io[name][0].rearrange("n i j -> i n j")[:, bass.ds(i * 2 + a, 1), :]
                                          ).then_inc(s_wab[a], 16)

            @block.tensor
            def _(pe):
                for n in range(LB):
                    c, j = n // 2, n % 2
                    if j == 0:
                        pe.wait_ge(w_in_sem[c % 2], 16 * (c // 2 + 1))
                    for half in range(2):
                        k = 2 * n + half
                        if k >= 4:
                            pe.wait_ge(s_xle, k - 3)
                        for d in range(DC):
                            ins = pe.matmul(PS[:, k % 4, 0:HALF], W[:, c % 2, d, j * P:(j + 1) * P],
                                            xnT[:, d, half * HALF:(half + 1) * HALF], start=d == 0, stop=d == DC - 1)
                        ins.then_inc(s_xl, 1)
                pe.wait_ge(s_xle, 16)
                pe.sem_inc(s_qkve, 2)
                pe.sem_inc(s_sig, 1)
                with pe.Fori(0, 4) as i:
                    for a in range(2):
                        pe.wait_ge(w_in_sem[a], i * 16 + 48)
                        for tb in range(5):
                            k = 5 * a + tb
                            pe.wait_ge(s_qkve, i * 10 + k + 1)
                            for d in range(DC):
                                ins = pe.matmul(PS[:rows(tb), 4 + k % 2, 0:HC], xnT[:, d, tb * P:tb * P + rows(tb)],
                                                W[:, a, d, :], start=d == 0, stop=d == DC - 1)
                            ins.then_inc(s_qkv, 1)
                        pe.wait_ge(s_wab[a], i * 32 + 32)
                        pe.wait_ge(s_xc, i * 2 + a + 1)
                        pe.wait_ge(s_sig, i * 2 + a + 1)
                        for m in range(2):
                            pe.matmul(PS[:, 6 + m, :], wab[:, a, m, :], xc[:, a, 0:SEQ], start=True, stop=True)
                            ins = pe.matmul(PS[:, m, 0:NS], wab[:, a, m, :], xc[:, a, SEQ:T], start=True, stop=True)
                        ins.then_inc(s_gate, 1)

            @block.scalar
            def _(act):
                for n in range(LB):
                    act.wait_ge(s_xl, 2 * n + 1)
                    act.activation(xlP[:, n, 3:3 + HALF], PS[:, (2 * n) % 4, 0:HALF], ACT.Copy).then_inc(s_xle, 1)
                    act.wait_ge(s_xl, 2 * n + 2)
                    act.activation(xlP[:, n, 3 + HALF:515], PS[:, (2 * n + 1) % 4, 0:SEQ - HALF], ACT.Copy)
                    act.activation(xlS[:, n, :, 3:7], b_t(PS[:, (2 * n + 1) % 4, SEQ - HALF:HALF]),
                                   ACT.Copy).then_inc(s_xle, 1)

                def turn2(i, v_part):
                    for a in range(2):
                        for tb in range(5):
                            k = 5 * a + tb
                            wait_apart(act, s_qkv, i * 10 + k + 1)
                            if v_part:
                                dst = vn[:rows(tb), tb, HC * a:HC * (a + 1)]
                            else:
                                dst = qk[:rows(tb), tb, bass.ds(i * 512 + HC * a, HC)]
                            act.activation(dst, PS[:rows(tb), 4 + k % 2, 0:HC], ACT.Copy).then_inc(s_qkve, 1)
                        act.wait_ge(s_gate, i * 2 + a + 1)
                        for m, dst in ((0, rg), (1, ig)):
                            act.activation(dst[:, a, 0:SEQ], PS[:, 6 + m, :], ACT.Sigmoid, bias=pnb[:, a, 5 + m:6 + m])
                            ins = act.activation(dst[:, a, SEQ:T], PS[:, m, 0:NS], ACT.Sigmoid,
                                                 bias=pnb[:, a, 5 + m:6 + m])
                        ins.then_inc(s_sig, 1)
                        act.wait_ge(s_la, i * 2 + a + 1)
                        act.activation(av, rg[:, a, :], ACT.Exp)
                        act.activation(th, rg[:, a, :], ACT.Tanh, scale=-1.0).then_inc(s_ab, 1)
                        act.wait_ge(s_tm, i * 2 + a + 1)
                        act.activation(uu, th, ACT.Sqrt).then_inc(s_sr, 1)

                with act.Fori(0, 3) as i:
                    turn2(i, False)
                turn2(3, True)

            @block.vector
            def _(v):
                v.memset(xlP[:, :, 0:3], 0.0)
                v.tensor_copy(xlS[:, :, :, 0:3], prmT[:, :, 0:24].rearrange("p n (b j) -> p n b j", b=NB)).then_inc(s_pad, 1)
                v.wait_ge(s_pad, 1)
                v.wait_ge(s_xle, 16)
                with steps_v.loop(4, 2 * 19) as i:
                    for a in range(2):
                        n = i * 2 + a
                        steps_v.did(v.tensor_copy(pnb[:, a, 0:7].unsqueeze(1), prmT[:, bass.ds(n, 1), 32:39]))
                        steps_v.did(v.tensor_copy(pnb[:, a, 7:8], sp8[:, bass.ds(n, 1)]))
                        steps_v.settle()
                        xs_in = [xlP[:, bass.ds(n, 1), j:j + SEQ] for j in range(CW)]
                        xs_smp = [xlS[:, bass.ds(n, 1), :, j:j + NT].rearrange("p a b t -> p (a b) t") for j in range(CW)]
                        oP, oS = xc[:, a, 0:SEQ].unsqueeze(1), b_t(xc[:, a, SEQ:T])
                        steps_v.did(v.tensor_scalar(oP, xs_in[0], pnb[:, a, 0:1], pnb[:, a, 4:5], ALU.mult, ALU.add))
                        steps_v.did(v.tensor_scalar(oS, xs_smp[0], pnb[:, a, 0:1], pnb[:, a, 4:5], ALU.mult, ALU.add))
                        for j in range(1, CW):
                            steps_v.settle()
                            if j < CW - 1:
                                steps_v.did(v.scalar_tensor_tensor(oP, xs_in[j], pnb[:, a, j:j + 1], oP, ALU.mult, ALU.add))
                                steps_v.did(v.scalar_tensor_tensor(oS, xs_smp[j], pnb[:, a, j:j + 1], oS, ALU.mult, ALU.add))
                            else:
                                v.scalar_tensor_tensor(oP, xs_in[j], pnb[:, a, j:j + 1], oP, ALU.mult, ALU.add)
                                v.scalar_tensor_tensor(oS, xs_smp[j], pnb[:, a, j:j + 1], oS, ALU.mult,
                                                       ALU.add).then_inc(s_xc, 1)
                        v.wait_ge(s_sig, i * 2 + a + 2)
                        v.tensor_scalar(rg[:, a, :], rg[:, a, :], pnb[:, a, 7:8], None, ALU.mult).then_inc(s_la, 1)
                        steps_v.did(v.tensor_tensor(ig[:, a, :], ig[:, a, :], xc[:, a, :], ALU.mult))
                        v.wait_ge(s_ab, i * 2 + a + 1)
                        steps_v.did(v.tensor_tensor(uu, av, av, ALU.mult))
                        steps_v.settle()
                        v.scalar_tensor_tensor(th, uu, 1.0, th, ALU.add, ALU.mult).then_inc(s_tm, 1)
                        v.wait_ge(s_sr, i * 2 + a + 1)
                        steps_v.did(v.tensor_tensor(uu, uu, ig[:, a, :], ALU.mult))
                        steps_v.settle()
                        steps_v.did(v.tensor_tensor_scan(lruT[:, bass.ds(n, 1), 0:SEQ].rearrange("p a t -> p (a t)"),
                                                         av[:, 0:SEQ], uu[:, 0:SEQ], 0.0, ALU.mult, ALU.add))
                        hs = lruT[:, bass.ds(n, 1), SEQ:T].rearrange("p a (b t) -> p (a b) t", b=NB)
                        aS, uS = b_t(av[:, SEQ:T]), b_t(uu[:, SEQ:T])
                        prev = prmT[:, bass.ds(n, 1), 24:32].rearrange("p a b -> p (a b)").unsqueeze(2)
                        for t in range(NT):
                            steps_v.did(v.tensor_tensor(hx.unsqueeze(2), aS[:, :, t:t + 1], prev, ALU.mult))
                            steps_v.settle()
                            ins = v.tensor_tensor(hs[:, :, t:t + 1], hx.unsqueeze(2), uS[:, :, t:t + 1], ALU.add)
                            if t < NT - 1:
                                steps_v.did(ins)
                                steps_v.settle()
                            else:
                                ins.then_inc(s_lru, 1)
                            prev = hs[:, :, t:t + 1]
                        v.wait_ge(s_lru, i * 2 + a + 1)

        qT = at(0, NH * T, "p (h t) -> p h t", h=NH)
        kT = at(4352, NG * T, "p (g t) -> p g t", g=NG)
        rtmp = at(6528, 2 * 4 * 192, "p (b a g e) -> p b a g e", b=2, a=4, g=24)
        last = at(8064, LB * 36, "p (n c) -> p n c", n=LB)
        lastrows = at(8400, LW)
        s_rope, s_qkt, s_qke, s_last, s_lastT, s_lrow = (sem("rotated"), sem("qk_transposed"), sem("qk_evac"),
                                                        sem("last_cols"), sem("last_rows"), sem("last_rows_sbuf"))

        with nc.Block() as block:
            @block.vector
            def _(v):
                v.tensor_copy(last[:, :, 0:24].rearrange("p n (b j) -> p n b j", b=NB), xlS[:, :, :, 4:7])
                v.tensor_copy(last[:, :, 24:32], lruT[:, :, SEQ + NT - 1:T:NT])
                v.tensor_copy(last[:, :, 32:35], xlP[:, :, 512:515])
                v.tensor_copy(last[:, :, 35:36], lruT[:, :, SEQ - 1:SEQ]).then_inc(s_last, 1)
                for tb in range(5):
                    np_ = rows(tb)
                    t1 = qk[:np_, tb, :].rearrange("p (g e) -> p g e", g=24)[:, :, 0:8]
                    t2 = qk[:np_, tb, :].rearrange("p (g e) -> p g e", g=24)[:, :, 8:16]
                    cs = const[:np_, C_CS + 16 * tb:C_CS + 16 * tb + 8].unsqueeze(1).broadcast_to([np_, 24, 8])
                    sn = const[:np_, C_CS + 16 * tb + 8:C_CS + 16 * tb + 16].unsqueeze(1).broadcast_to([np_, 24, 8])
                    tmp = rtmp[:np_, tb % 2]
                    if tb >= 2:
                        v.wait_ge(s_rope, tb - 1)
                    for m, (x, y) in enumerate(((t1, cs), (t2, sn), (t2, cs), (t1, sn))):
                        steps_v.did(v.tensor_tensor(tmp[:, m], x, y, ALU.mult))
                    steps_v.settle()
                    v.tensor_tensor(t1, tmp[:, 0], tmp[:, 1], ALU.subtract)
                    v.tensor_tensor(t2, tmp[:, 2], tmp[:, 3], ALU.add).then_inc(s_rope, 1)
                v.wait_ge(s_lastT, 1)
                v.tensor_copy(lastrows[0:36, :].rearrange("p (a n) -> p a n", a=2), PS[0:36, 4:6, :]).then_inc(s_lrow, 1)

            @block.tensor
            def _(pe):
                pe.wait_ge(s_last, 1)
                for n in range(LB):
                    ins = pe.transpose(PS[0:36, 4 + n // 4, (n % 4) * P:(n % 4 + 1) * P], last[:, n, :], ident)
                ins.then_inc(s_lastT, 1)
                for tb in range(5):
                    pe.wait_ge(s_rope, tb + 1)
                    for q in range(3):
                        n = 3 * tb + q
                        if n >= 4:
                            pe.wait_ge(s_qke, n - 3)
                        for j in range(4):
                            ins = pe.transpose(PS[:, n % 4, j * P:j * P + rows(tb)],
                                               qk[:rows(tb), tb, (4 * q + j) * P:(4 * q + j + 1) * P], ident[:rows(tb), :rows(tb)])
                        ins.then_inc(s_qkt, 1)

            @block.scalar
            def _(act):
                for tb in range(5):
                    for q in range(3):
                        n = 3 * tb + q
                        dst = qT[:, 4 * q:4 * q + 4, tb * P:tb * P + rows(tb)] if q < 2 else kT[:, :, tb * P:tb * P + rows(tb)]
                        act.wait_ge(s_qkt, n + 1)
                        act.activation(dst, PS[:, n % 4, :].rearrange("p (j t) -> p j t", j=4)[:, :, 0:rows(tb)],
                                       ACT.Copy).then_inc(s_qke, 1)

            @block.sync
            def _(sp_):
                kp = io["k_prompt"][0, 0].rearrange("(b p) g c -> b p (g c)", p=P)
                vp = io["v_prompt"][0, 0].rearrange("(b p) g c -> b p (g c)", p=P)
                ks = io["k_sample"][0].rearrange("b t g c -> (b t) (g c)")
                vs = io["v_sample"][0].rearrange("b t g c -> (b t) (g c)")
                for tb in range(5):
                    store(sp_, vp[tb] if tb < TB else vs, vn[:rows(tb), tb, :])
                for tb in range(5):
                    sp_.wait_ge(s_rope, tb + 1)
                    store(sp_, kp[tb] if tb < TB else ks, qk[:rows(tb), tb, 1024:1536])
                sp_.wait_ge(s_lrow, 1)
                store(sp_, io["conv_sample"][0].rearrange("b j c -> (b j) c"), lastrows[0:24, :])
                store(sp_, io["h_sample"][0], lastrows[24:32, :])
                store(sp_, io["conv_prompt"][0, 0], lastrows[32:35, :])
                store(sp_, io["h_prompt"][0], lastrows[35:36, :])
                sp_.wait_ge(out_done, 16 * outs[0])

        pb = at(8064, 2 * 2 * SEQ, "p (b c k) -> p b c k", b=2, c=2)
        wTb = at(10112, 2 * SEQ, "p (b k) -> p b k", b=2)
        dg = at(11136, 2 * 2 * P, "p (b c k) -> p b c k", b=2, c=2)
        st = at(11648, 2 * 8, "p (b c) -> p b c", b=2)
        qbd = at(39008, NB * NG * 64, "p (b g c) -> p b g c", b=NB, g=NG)
        kTn = at(44032, NG * NS, "p (g t) -> p g t", g=NG)
        s_qbd = sem("q_blockdiag")
        s_S, s_nb, s_p, s_dg = sem("scores"), sem("neg_max"), sem("exp"), sem("diagonals")
        s_wt, s_wte, s_pv, s_att = sem("weights_T"), sem("weights_T_sbuf"), sem("values"), sem("att_sbuf")
        s_mk = sem("masked")
        its = [(h, qb) for h in range(NH) for qb in range(TB)]
        SC = HD ** -0.5

        with nc.Block() as block:
            @block.gpsimd
            def _(g_):
                steps_g.did(g_.memset(qbd, 0.0))
                for c in range(2):
                    for g in range(NG):
                        for r in range(2):
                            col = 16 * g + 8 * c + 4 * r
                            steps_g.settle()
                            steps_g.did(g_.tensor_copy(qbd[64 * c:64 * c + 64, :, g, col:col + 4],
                                           qT[64 * c:64 * c + 64, 2 * g + r, SEQ:T].rearrange("p (b t) -> p b t", b=NB)))
                steps_g.settle()
                g_.tensor_copy(kTn, kT[:, :, SEQ:T]).then_inc(s_qbd, 1)

            @block.tensor
            def _(pe):
                def scores(it):
                    h, qb = its[it]
                    if it >= 2:
                        pe.wait_ge(s_p, it - 1)
                    for c in range(2):
                        ins = pe.matmul(PS[:, c + 2 * (it % 2), 0:(qb + 1) * P], qT[64 * c:64 * c + 64, h, qb * P:(qb + 1) * P],
                                        kT[64 * c:64 * c + 64, h // 2, 0:(qb + 1) * P], start=True, stop=True)
                    ins.then_inc(s_S, 1)

                def weights(it):
                    h, qb = its[it]
                    pe.wait_ge(s_dg, it + 1)
                    if it >= 2:
                        pe.wait_ge(s_wte, it - 1)
                    for kb in range(qb + 1):
                        for c in range(2):
                            ins = pe.matmul(PS[:, 4 + it % 2, kb * P:(kb + 1) * P], pb[:, it % 2, c, kb * P:(kb + 1) * P],
                                            dg[:, it % 2, c, :], start=c == 0, stop=c == 1)
                    ins.then_inc(s_wt, 1)

                def values(it):
                    h, qb = its[it]
                    pe.wait_ge(s_wte, it + 1)
                    if it >= 2:
                        pe.wait_ge(s_att, it - 1)
                    for kb in range(qb + 1):
                        ins = pe.matmul(PS[:, 6 + it % 2, 0:P], vn[:, kb, (h // 2) * P:(h // 2 + 1) * P],
                                        wTb[:, it % 2, kb * P:(kb + 1) * P], start=kb == 0, stop=kb == qb)
                    ins.then_inc(s_pv, 1)

                scores(0)
                for it in range(len(its) + 1):
                    if it + 1 < len(its):
                        scores(it + 1)
                    if it < len(its):
                        weights(it)
                    if it >= 1:
                        values(it - 1)

            @block.vector
            def _(v):
                def front(it):
                    h, qb = its[it]
                    b0 = 2 * (it % 2)
                    v.wait_ge(s_S, it + 1)
                    dgl = PS[:, b0:b0 + 2, qb * P:(qb + 1) * P]
                    steps_v.did(v.tensor_tensor(dgl, dgl, causal.unsqueeze(1).broadcast_to([P, 2, P]), ALU.add))
                    steps_v.settle()
                    steps_v.did(v.tensor_reduce(st[:, it % 2, 0:2], PS[:, b0:b0 + 2, 0:(qb + 1) * P], AX.X, ALU.max))
                    steps_v.settle()
                    v.tensor_scalar(st[:, it % 2, 2:4], st[:, it % 2, 0:2], -SC, None, ALU.mult).then_inc(s_nb, 1)

                def back(it):
                    v.wait_ge(s_p, it + 1)
                    if it >= 2:
                        v.wait_ge(s_wt, it - 1)
                    steps_v.did(v.reciprocal(st[:, it % 2, 6:8], st[:, it % 2, 4:6]))
                    steps_v.settle()
                    steps_v.did(v.tensor_scalar(st[:, it % 2, 7:8], st[:, it % 2, 7:8], neglam, None, ALU.mult))
                    steps_v.settle()
                    for c in range(2):
                        ins = v.tensor_scalar(dg[:, it % 2, c, :], ident, st[:, it % 2, 6 + c:7 + c], None, ALU.mult)
                    ins.then_inc(s_dg, 1)

                def take(it):
                    h, qb = its[it]
                    v.wait_ge(s_pv, it + 1)
                    v.tensor_copy(attT[:, h, qb * P:(qb + 1) * P], PS[:, 6 + it % 2, 0:P]).then_inc(s_att, 1)

                front(0)
                for it in range(len(its) + 1):
                    if it + 1 < len(its):
                        front(it + 1)
                    if it < len(its):
                        back(it)
                    if it >= 1:
                        take(it - 1)

            @block.scalar
            def _(act):
                def exps(it):
                    h, qb = its[it]
                    act.wait_ge(s_nb, it + 1)
                    if it >= 2:
                        act.wait_ge(s_wt, it - 1)
                    for c in range(2):
                        ins = act.activation(pb[:, it % 2, c, 0:(qb + 1) * P], PS[:, c + 2 * (it % 2), 0:(qb + 1) * P],
                                             ACT.Exp, bias=st[:, it % 2, 2 + c:3 + c], scale=SC,
                                             accum_out=st[:, it % 2, 4 + c:5 + c])
                    ins.then_inc(s_p, 1)

                def take_weights(it):
                    h, qb = its[it]
                    act.wait_ge(s_wt, it + 1)
                    if it >= 2:
                        act.wait_ge(s_pv, it - 1)
                    act.activation(wTb[:, it % 2, 0:(qb + 1) * P], PS[:, 4 + it % 2, 0:(qb + 1) * P],
                                   ACT.Copy).then_inc(s_wte, 1)

                exps(0)
                for it in range(len(its)):
                    if it + 1 < len(its):
                        exps(it + 1)
                    take_weights(it)

        KTs = at(33792, 4 * 512, "p (s k) -> p s k", s=4)
        pS = at(35840, PAST + NS)
        wTs = at(37920, 17 * 64, "p (j c) -> p j c", j=17)
        snew = at(44160, NS)
        comb = at(44192, 64)
        sst = at(44256, 16)
        cache = [io[n].rearrange("l n (r k) g c -> (l n r) (k g c)", k=8) for n in ("cache_k", "cache_v")]
        slots = at(W_AT, 16384, "p (s m) -> p s m", s=4)
        kv = at(W_AT, 16384, "p (s j n) -> p s j n", s=4, j=8)
        s_cache = [sem(f"cache_slot{s}_in") for s in range(4)]
        s_T, s_evA, s_evB, s_sc = sem("k_transposed"), sem("kT_scalar"), sem("kT_vector"), sem("sample_scores")
        s_new, s_nbs, s_ps, s_c64 = sem("new_scores"), sem("sample_neg_max"), sem("sample_exp"), sem("sample_diag")
        s_w, s_wA, s_wB, s_v, s_pve = (sem("sample_weights_T"), sem("weights_T_scalar"), sem("weights_T_vector"),
                                      sem("sample_values"), sem("sample_att_sbuf"))
        PAIRS = NB // 2

        with nc.Block() as block:
            @block.gpsimd
            def _(g_):
                for pr in range(PAIRS):
                    for what in range(2):
                        for bb in range(2):
                            for hf in range(2):
                                b, slot = 2 * pr + bb, 2 * bb + hf
                                if what == 0 and pr >= 1:
                                    g_.wait_ge(s_v, 2 * (pr - 1) + bb + 1)
                                if what == 1:
                                    g_.wait_ge(s_T, 16 * b + 8 * (hf + 1))
                                g_.indirect_dma_start(
                                    slots[:, slot, :], None, cache[what],
                                    bass.IndirectOffsetOnAxis(ap=rowidx[:, hf * NB + b:hf * NB + b + 1], axis=0)
                                ).then_inc(s_cache[slot], 16)

            @block.tensor
            def _(pe):
                def turn_keys(pr, n):
                    bb, u = n // 16, n % 16
                    qd, g = u // 4, u % 4
                    U = 32 * pr + n
                    slot = 2 * bb + u // 8
                    if u % 8 == 0:
                        pe.wait_ge(s_cache[slot], 16 * (2 * pr + 1))
                    if n < 3 and pr:
                        pe.wait_ge(s_wA, pr)
                        pe.wait_ge(s_wB, 2 * pr)
                    elif U >= 3:
                        pe.wait_ge((s_evA, s_evB)[(U - 3) % 2], (U - 3) // 2 + 1)
                    for j in range(4):
                        ins = pe.transpose(PS[:, 5 + U % 3, j * P:(j + 1) * P],
                                           kv[:, slot, (qd % 2) * 4 + j, g * P:(g + 1) * P], ident)
                    ins.then_inc(s_T, 1)

                def score(pr, n):
                    bb, u = n // 16, n % 16
                    qd, g = u // 4, u % 4
                    U = 32 * pr + n
                    pe.wait_ge((s_evA, s_evB)[U % 2], U // 2 + 1)
                    if n == 0 and pr:
                        pe.wait_ge(s_ps, pr)
                    pe.matmul(PS[64 * bb:64 * bb + 64, qd, :], qbd[:, 2 * pr + bb, g, :], KTs[:, U % 4, :],
                              start=g == 0, stop=g == 3).then_inc(s_sc, 1)

                for pr in range(PAIRS):
                    for n in range(33):
                        if n < 32:
                            turn_keys(pr, n)
                        if n:
                            score(pr, n - 1)
                    if pr:
                        pe.wait_ge(s_pve, pr)
                    for bb in range(2):
                        for g in range(NG):
                            ins = pe.matmul(PS[64 * bb:64 * bb + 64, 4, 0:NS], qbd[:, 2 * pr + bb, g, :], kTn[:, g, :],
                                            start=g == 0, stop=g == 3)
                    ins.then_inc(s_new, 1)
                    pe.wait_ge(s_c64, pr + 1)
                    pe.wait_ge(s_evA, 16 * (pr + 1))
                    pe.wait_ge(s_evB, 16 * (pr + 1))
                    for j in range(16):
                        ins = pe.matmul(PS[:, 5 + j // 8, (j % 8) * 64:(j % 8 + 1) * 64], pS[:, j * P:(j + 1) * P], comb,
                                        start=True, stop=True)
                        if j % 8 == 7:
                            ins.then_inc(s_w, 1)
                    pe.matmul(PS[0:NS, 7, 0:64], pS[:, PAST:PAST + NS], comb, start=True, stop=True).then_inc(s_w, 1)
                    pe.wait_ge(s_wA, pr + 1)
                    pe.wait_ge(s_wB, 2 * (pr + 1))
                    for bb in range(2):
                        for hf in range(2):
                            pe.wait_ge(s_cache[2 * bb + hf], 16 * (2 * pr + 2))
                        for g in range(NG):
                            o = 32 * bb + 8 * g
                            dst = PS[:, 4, 64 + o:64 + o + 8]
                            for j in range(16):
                                pe.matmul(dst, kv[:, 2 * bb + j // 8, j % 8, g * P:(g + 1) * P], wTs[:, j, o:o + 8],
                                          start=j == 0, stop=False)
                            ins = pe.matmul(dst, vn[0:NS, TB, g * P:(g + 1) * P], wTs[0:NS, 16, o:o + 8],
                                            start=False, stop=True)
                        ins.then_inc(s_v, 1)

            def take_keys(eng, copy, pr, parity, s):
                for n in range(parity, 32, 2):
                    U = 32 * pr + n
                    eng.wait_ge(s_T, U + 1)
                    if U >= 4:
                        eng.wait_ge(s_sc, U - 3)
                    copy(KTs[:, U % 4, :], PS[:, 5 + U % 3, :]).then_inc(s, 1)

            @block.scalar
            def _(act):
                def copy(dst, src):
                    return act.activation(dst, src, ACT.Copy)
                for pr in range(PAIRS):
                    take_keys(act, copy, pr, 0, s_evA)
                    act.wait_ge(s_nbs, pr + 1)
                    act.activation(pS[:, 0:PAST].rearrange("p (a k) -> p a k", a=4), PS[:, 0:4, :], ACT.Exp, bias=sst[:, 3:4],
                                   scale=SC, accum_out=sst[:, 4:5])
                    act.activation(pS[:, PAST:PAST + NS], snew, ACT.Exp, bias=sst[:, 3:4], scale=SC,
                                   accum_out=sst[:, 5:6]).then_inc(s_ps, 1)
                    act.wait_ge(s_w, 3 * pr + 1)
                    copy(wTs[:, 0:8, :].rearrange("p j c -> p (j c)"), PS[:, 5, :]).then_inc(s_wA, 1)

            @block.vector
            def _(v):
                for pr in range(PAIRS):
                    take_keys(v, v.tensor_copy, pr, 1, s_evB)
                    v.wait_ge(s_new, pr + 1)
                    steps_v.did(v.tensor_tensor(snew, PS[:, 4, 0:NS], const[:, C_NEW + NS * pr:C_NEW + NS * (pr + 1)], ALU.add))
                    steps_v.did(v.tensor_reduce(sst[:, 0:1], PS[:, 0:4, :], AX.XY, ALU.max))
                    steps_v.settle()
                    steps_v.did(v.tensor_reduce(sst[:, 1:2], snew, AX.X, ALU.max))
                    steps_v.settle()
                    steps_v.did(v.tensor_tensor(sst[:, 2:3], sst[:, 0:1], sst[:, 1:2], ALU.max))
                    steps_v.settle()
                    v.tensor_scalar(sst[:, 3:4], sst[:, 2:3], -SC, None, ALU.mult).then_inc(s_nbs, 1)
                    v.wait_ge(s_ps, pr + 1)
                    steps_v.did(v.tensor_tensor(sst[:, 6:7], sst[:, 4:5], sst[:, 5:6], ALU.add))
                    steps_v.settle()
                    steps_v.did(v.reciprocal(sst[:, 7:8], sst[:, 6:7]))
                    steps_v.settle()
                    v.tensor_scalar(comb, const[:, C_COMB:C_COMB + 64], sst[:, 7:8], csel, ALU.mult,
                                    ALU.mult).then_inc(s_c64, 1)
                    v.wait_ge(s_w, 3 * pr + 2)
                    v.tensor_copy(wTs[:, 8:16, :].rearrange("p j c -> p (j c)"), PS[:, 6, :]).then_inc(s_wB, 1)
                    v.wait_ge(s_w, 3 * pr + 3)
                    v.tensor_copy(wTs[0:NS, 16, :], PS[0:NS, 7, 0:64]).then_inc(s_wB, 1)
                    v.wait_ge(s_v, 2 * (pr + 1))
                    cols = slice(SEQ + 2 * NT * pr, SEQ + 2 * NT * (pr + 1))
                    v.tensor_copy(attT[:, :, cols].rearrange("p h (b t) -> p h b t", b=2),
                                  PS[:, 4, 64:128].rearrange("p (b h t) -> p h b t", b=2, h=NH)).then_inc(s_pve, 1)

        w_att_up = io["w_att_up"][0].rearrange("(k p) n -> p k n", p=P)
        w_lru_up = io["w_lru_up"][0].rearrange("(k p) n -> p k n", p=P)
        w_out = io["w_out"][0].rearrange("(k p) n -> p k n", p=P)
        w_q = io["peer_wq"][0].rearrange("(k p) n -> p k n", p=P)

        def load_up(sp_, cols):
            sp_.dma_start(W[:, 2, 0:AC, :], w_att_up[:, :, cols]).then_inc(w_in_sem[2], 16)
            sp_.dma_start(W[:, 2, AC:DC, :], w_lru_up[:, :, cols]).then_inc(w_in_sem[2], 16)

        def stage7_first_loads(sp_):
            load_w(sp_, 0, w_in[:, :, COL_GA:COL_GA + HC])
            load_w(sp_, 1, w_in[:, :, COL_GL:COL_GL + HC])
            load_up(sp_, slice(0, HC))

        SQW = AC * T // 2
        asq = at(33792, AC * T)
        ars = at(38144, AC * T)
        af = at(A_AT, AC * T)
        g08 = at(44300, 1)
        s_asq, s_ams, s_art, s_aps = sem("att_squares"), sem("att_mean_squares"), sem("att_root"), sem("att_sums")

        with nc.Block() as block:
            @block.sync
            def _(sp_):
                stage7_first_loads(sp_)

            @block.vector
            def _(v):
                for r in range(2):
                    sl = slice(SQW * r, SQW * (r + 1))
                    v.tensor_tensor(asq[:, sl], af[:, sl], af[:, sl], ALU.mult).then_inc(s_asq, 1)
                steps_v.did(v.tensor_scalar(g08, gT[:, 32:33], 1.0 - LAM_INIT, None, ALU.mult))
                for r in range(2):
                    v.wait_ge(s_aps, 8 * (r + 1))
                    v.tensor_scalar(ars[:, SQW * r:SQW * (r + 1)].rearrange("p (k t) -> p k t", k=8), PS[:, :, 0:HALF],
                                    1.0 / P, EPS, ALU.mult, ALU.add).then_inc(s_ams, 1)
                for r in range(2):
                    sl = slice(SQW * r, SQW * (r + 1))
                    v.wait_ge(s_art, r + 1)
                    steps_v.did(v.reciprocal(ars[:, sl], ars[:, sl]))
                    steps_v.settle()
                    steps_v.did(v.scalar_tensor_tensor(af[:, sl], af[:, sl], g08, ars[:, sl], ALU.mult, ALU.mult))

            @block.scalar
            def _(act):
                for r in range(2):
                    sl = slice(SQW * r, SQW * (r + 1))
                    act.wait_ge(s_ams, r + 1)
                    act.activation(ars[:, sl], ars[:, sl], ACT.Sqrt).then_inc(s_art, 1)

            @block.tensor
            def _(pe):
                for r in range(2):
                    pe.wait_ge(s_asq, r + 1)
                    if r:
                        pe.wait_ge(s_ams, r)
                    for k in range(8):
                        o = SQW * r + HALF * k
                        pe.matmul(PS[:, k, 0:HALF], ones, asq[:, o:o + HALF], start=True, stop=True).then_inc(s_aps, 1)

        sga = at(44400, 4 * HALF, "p (x t) -> p x t", x=4)
        sgl = at(45500, 4 * HALF, "p (x t) -> p x t", x=4)
        s_ga, s_gl, s_up = sem("ga_tile"), sem("gl_tile"), sem("up_tiles")
        s_sga, s_sgl, s_mA, s_mB = sem("ga_sigmoid"), sem("gl_sigmoid"), sem("att_merged"), sem("lru_merged")
        NCH = D // HC
        L7 = 96

        with nc.Block() as block:
            @block.sync
            def _(sp_):
                with sp_.Fori(1, NCH) as i:
                    wait_apart(sp_, s_ga, i * 4)
                    load_w(sp_, 0, w_in[:, :, bass.ds(i * HC + COL_GA, HC)])
                    wait_apart(sp_, s_gl, i * 4)
                    load_w(sp_, 1, w_in[:, :, bass.ds(i * HC + COL_GL, HC)])
                    wait_apart(sp_, s_up, i * 4)
                    load_up(sp_, bass.ds(i * HC, HC))
                sp_.wait_ge(s_ga, 4 * NCH)
                load_w(sp_, 0, w_out[:, :, 0:HC])
                sp_.wait_ge(s_gl, 4 * NCH)
                load_w(sp_, 1, w_out[:, :, HC:2 * HC])

            @block.tensor
            def _(pe):
                with pe.Fori(0, NCH) as i:
                    for part, tile_done, merged in ((0, s_ga, s_mA), (1, s_gl, s_mB)):
                        pe.wait_ge(w_in_sem[part], i * 16 + (L7 + 16))
                        for x in range(4):
                            pe.wait_ge(merged, i * 4 + x + 1)
                            for d in range(DC):
                                ins = pe.matmul(PS[:, 4 * part + x, 0:HALF], W[:, part, d, (x // 2) * P:(x // 2 + 1) * P],
                                                xnT[:, d, (x % 2) * HALF:(x % 2 + 1) * HALF], start=d == 0, stop=d == DC - 1)
                            ins.then_inc(tile_done, 1)
                    pe.wait_ge(w_in_sem[2], i * 32 + 32)
                    for x in range(4):
                        for part, src, free in ((0, attT, s_sga), (1, lruT, s_sgl)):
                            pe.wait_ge(free, i * 4 + x + 1)
                            for d in range(AC):
                                ins = pe.matmul(PS[:, 4 * part + x, 0:HALF],
                                                W[:, 2, AC * part + d, (x // 2) * P:(x // 2 + 1) * P],
                                                src[:, d, (x % 2) * HALF:(x % 2 + 1) * HALF], start=d == 0, stop=d == AC - 1)
                        ins.then_inc(s_up, 1)

            @block.scalar
            def _(act):
                with act.Fori(0, NCH) as i:
                    for part, dst, tile_done, s, merged in ((0, sga, s_ga, s_sga, s_mA), (1, sgl, s_gl, s_sgl, s_mB)):
                        for x in range(4):
                            act.wait_ge(tile_done, i * 4 + x + 1)
                            act.wait_ge(merged, i * 4 + x + 1)
                            act.activation(dst[:, x, :], PS[:, 4 * part + x, 0:HALF], ACT.Sigmoid).then_inc(s, 1)

            @block.vector
            def _(v):
                v.sem_inc(s_mA, 4)
                v.sem_inc(s_mB, 4)
                with steps_v.loop(NCH, 4) as i:
                    for x in range(4):
                        dst = mT[:, bass.ds(i * 2 + x // 2, 1), (x % 2) * HALF:(x % 2 + 1) * HALF].rearrange("p a t -> p (a t)")
                        v.wait_ge(s_up, i * 4 + x + 1)
                        v.tensor_tensor(dst, sga[:, x, :], PS[:, x, 0:HALF], ALU.mult).then_inc(s_mA, 1)
                        steps_v.did(v.tensor_tensor(sgl[:, x, :], sgl[:, x, :], PS[:, 4 + x, 0:HALF], ALU.mult))
                        steps_v.settle()
                        v.tensor_tensor(dst, dst, sgl[:, x, :], ALU.add).then_inc(s_mB, 1)

        h = at(X_AT, 5 * D, "p (b n) -> p b n", b=5)
        s_xr, s_o, s_hadd = sem("x_again"), sem("out_tile"), sem("h_tile")
        L8 = L7 + 16 * NCH

        def stream_pairs(sp_, src, tile_done, per, upto=NCH):
            with sp_.Fori(1, upto // 2) as i:
                for a in range(2):
                    wait_apart(sp_, tile_done, i * (2 * per) + per * (a - 1))
                    load_w(sp_, a, src[:, :, bass.ds(i * (2 * HC) + HC * a, HC)])

        with nc.Block() as block:
            @block.sync
            def _(sp_):
                for tb in range(5):
                    sp_.dma_start(h[:rows(tb), tb, :], xp[tb] if tb < TB else xsm).then_inc(s_xr, 16)
                stream_pairs(sp_, w_out, s_o, 5)
                for a in range(2):
                    sp_.wait_ge(s_o, 5 * (NCH - 1 + a))
                    load_w(sp_, a, w_q[:, :, HC * a:HC * (a + 1)])

            @block.tensor
            def _(pe):
                with pe.Fori(0, NCH // 2) as i:
                    for a in range(2):
                        pe.wait_ge(w_in_sem[a], i * 16 + (L8 + 16))
                        for tb in range(5):
                            pe.wait_ge(s_hadd, i * 10 + 5 * a + tb + 1)
                            for d in range(DC):
                                ins = pe.matmul(PS[:rows(tb), tb, 0:HC], mT[:, d, tb * P:tb * P + rows(tb)], W[:, a, d, :],
                                                start=d == 0, stop=d == DC - 1)
                            ins.then_inc(s_o, 1)

            @block.vector
            def _(v):
                v.sem_inc(s_hadd, 5)
                v.wait_ge(s_xr, 16 * 5)
                with v.Fori(0, NCH // 2) as i:
                    for a in range(2):
                        for tb in range(5):
                            v.wait_ge(s_o, i * 10 + 5 * a + tb + 1)
                            dst = h[:rows(tb), tb, bass.ds(i * (2 * HC) + HC * a, HC)]
                            v.tensor_tensor(dst, dst, PS[:rows(tb), tb, 0:HC], ALU.add).then_inc(s_hadd, 1)

        xn2T = mT
        xsc = at(R_AT, 2 * D, "p (b n) -> p b n", b=2)
        kkT = at(26624, 2 * NK, "p (a n) -> p a n", a=2)
        kk = at(26880, 2 * P, "p (a n) -> p a n", a=2)
        s_kk, s_kkt, s_kke = sem("peer_keys_in"), sem("peer_keys_T"), sem("peer_keys_sbuf")
        squares, evac_scalar, scale, scale_block, evac_vector, turn = transposed_norm(1, h, xn2T, 16)

        with nc.Block() as block:
            @block.sync
            def _(sp_):
                for a in range(2):
                    sp_.dma_start(kk[:, a, :], io[f"peer_k{a + 1}"][0]).then_inc(s_kk, 16)

            @block.scalar
            def _(act):
                squares(act)
                act.wait_ge(s_kkt, 1)
                act.activation(kkT, PS[:, 4, 0:2 * NK].rearrange("p (a n) -> p a n", a=2), ACT.Copy).then_inc(s_kke, 1)
                evac_scalar(act)

            @block.vector
            def _(v):
                scale(v)
                scale_block(v, 0, xsc[:, 0, :])
                scale_block(v, 1, xsc[:, 1, :])
                for tb in range(5):
                    evac_vector(v, tb)
                    if tb + 2 < 5:
                        v.wait_ge(s_tr, 20 + 4 * (tb + 1))
                        scale_block(v, tb + 2, xsc[:rows(tb + 2), tb % 2, :])

            @block.tensor
            def _(pe):
                pe.wait_ge(s_kk, 32)
                for a in range(2):
                    ins = pe.transpose(PS[:, 4, a * NK:(a + 1) * NK], kk[:, a, :], ident)
                ins.then_inc(s_kkt, 1)
                for tb in range(5):
                    turn(pe, tb, xsc[:rows(tb), tb % 2, :])

        eid = at(26880, T).bitcast(I32)
        gate = at(27424, T)
        R0 = R_AT
        qc = at(R0, 2 * 2 * T, "p (a u t) -> p a u t", a=2, u=2)
        S2 = at(R0 + 2176, 5 * 2 * NK, "p (b u n) -> p b u n", b=5, u=2)
        cand = at(R0 + 3456, 5 * 256, "p (b m) -> p b m", b=5)
        cand2 = at(R0 + 4736, 5 * 256, "p (b m) -> p b m", b=5)
        eq = at(R0 + 6016, 5 * 256, "p (m i) -> p m i", i=16)
        picked = at(R0 + 7296, 5 * 256, "p (m i) -> p m i", i=16)
        vals = at(L_AT, 160, "p (b u k) -> p b u k", b=5, u=2)
        idx = at(L_AT + 160, 160, "p (b u k) -> p b u k", b=5, u=2).bitcast(U32)
        idxf = at(L_AT + 320, 160, "p (b u k) -> p b u k", b=5, u=2)
        best = at(L_AT + 480, 80, "p (b k) -> p b k", b=5)
        sel = at(L_AT + 560, 80, "p (b k) -> p b k", b=5).bitcast(U32)
        selp = at(L_AT + 640, 160, "p (a m) -> p a m", a=2).bitcast(U32)
        selpf = at(L_AT + 800, 160, "p (a m) -> p a m", a=2)
        pick = at(L_AT + 960, 160, "p (a m) -> p a m", a=2)
        rel = at(L_AT + 1120, 80, "p (b k) -> p b k", b=5)
        gexp = at(L_AT + 1200, 80, "p (b k) -> p b k", b=5)
        gsum = at(L_AT + 1280, 5)
        eidS = at(L_AT + 1300, P).bitcast(I32)
        gateS = at(L_AT + 1428, P)
        s_qp, s_qpe = sem("query_tile"), sem("query_evac")
        s_ks, s_l1, s_rel, s_gexp = sem("key_scores"), sem("key_scores_read"), sem("gate_logits"), sem("gate_exp")
        s_z4 = sem("spare_rows_set")
        L10 = L8 + 16 * NCH // 2

        def key_scores(tb, u=slice(0, 2)):
            return PS[:, 4 + tb // 2, (tb % 2) * 2 * NK:(tb % 2 + 1) * 2 * NK].rearrange("p (u n) -> p u n", u=2)[:, u]

        with nc.Block() as block:
            @block.sync
            def _(sp_):
                stream_pairs(sp_, w_q, s_qp, 4)

            @block.tensor
            def _(pe):
                pe.wait_ge(s_z4, 1)
                with pe.Fori(0, NCH // 2) as i:
                    for a in range(2):
                        pe.wait_ge(w_in_sem[a], i * 16 + (L10 + 16))
                        for x in range(4):
                            pe.wait_ge(s_qpe, i * 8 + 4 * a + x + 1)
                            for d in range(DC):
                                ins = pe.matmul(PS[:, x, 0:HALF], W[:, a, d, (x // 2) * P:(x // 2 + 1) * P],
                                                xn2T[:, d, (x % 2) * HALF:(x % 2 + 1) * HALF], start=d == 0, stop=d == DC - 1)
                            ins.then_inc(s_qp, 1)
                        pe.wait_ge(s_qpe, i * 8 + (4 * a + 8))
                        pe.wait_ge(s_l1, i * 2 + a + 1)
                        for tb in range(5):
                            for u in range(2):
                                ins = pe.matmul(key_scores(tb, u)[0:rows(tb)], qc[:, a, u, tb * P:tb * P + rows(tb)],
                                                kkT[:, u, :], start=True, stop=True)
                        ins.then_inc(s_ks, 1)

            @block.scalar
            def _(act):
                act.sem_inc(s_qpe, 4)
                with act.Fori(0, NCH // 2) as i:
                    for a in range(2):
                        for x in range(4):
                            act.wait_ge(s_qp, i * 8 + 4 * a + x + 1)
                            act.activation(qc[:, a, x // 2, (x % 2) * HALF:(x % 2 + 1) * HALF], PS[:, x, 0:HALF],
                                           ACT.Copy).then_inc(s_qpe, 1)
                        act.wait_ge(s_rel, i * 2 + a + 1)
                        act.activation(gexp, rel, ACT.Exp).then_inc(s_gexp, 1)

            @block.vector
            def _(v):
                did, settle = steps_v.did, lambda: settle_apart(steps_v)
                tiles = [(tb, u) for tb in range(5) for u in range(2)]
                for tb in range(5):
                    ins = v.memset(key_scores(tb), 0.0)
                ins.then_inc(s_z4, 1)
                v.sem_inc(s_l1, 1)
                per = 5 * 8 + 2 + 5 * 5 + 2 + 1 + 6 + 2 + 4
                with steps_v.loop(PH, per) as head:
                    wait_apart(v, s_ks, head + 1)
                    for tb, u in tiles:
                        did(v.max(vals[:, tb, u, 0:8], key_scores(tb, u)))
                    settle()
                    for tb, u in tiles:
                        did(v.max_index(idx[:, tb, u, 0:8], vals[:, tb, u, 0:8], key_scores(tb, u)))
                    for tb, u in tiles:
                        ins = v.match_replace(S2[:, tb, u, :], vals[:, tb, u, 0:8], key_scores(tb, u), -3e38)
                    ins.then_inc(s_l1, 1)
                    wait_apart(v, s_l1, head + 2)
                    for tb, u in tiles:
                        did(v.max(vals[:, tb, u, 8:16], S2[:, tb, u, :]))
                    settle()
                    for tb, u in tiles:
                        did(v.max_index(idx[:, tb, u, 8:16], vals[:, tb, u, 8:16], S2[:, tb, u, :]))
                    did(v.tensor_tensor(cand.rearrange("p b (i j) -> p b i j", i=16),
                                        vals[:, :, 0, :].unsqueeze(3).broadcast_to([P, 5, 16, 16]),
                                        vals[:, :, 1, :].unsqueeze(2).broadcast_to([P, 5, 16, 16]), ALU.add))
                    settle()
                    did(v.tensor_copy(idxf, idx))
                    for tb in range(5):
                        did(v.max(best[:, tb, 0:8], cand[:, tb]))
                    settle()
                    for tb in range(5):
                        did(v.max_index(sel[:, tb, 0:8], best[:, tb, 0:8], cand[:, tb]))
                    for tb in range(5):
                        did(v.match_replace(cand2[:, tb], best[:, tb, 0:8], cand[:, tb], -3e38))
                    settle()
                    for tb in range(5):
                        did(v.max(best[:, tb, 8:16], cand2[:, tb]))
                    settle()
                    for tb in range(5):
                        did(v.max_index(sel[:, tb, 8:16], best[:, tb, 8:16], cand2[:, tb]))
                    v.tensor_tensor(rel, best, best[:, :, 0:1].broadcast_to([P, 5, 16]), ALU.subtract).then_inc(s_rel, 1)
                    settle()
                    flat = sel.rearrange("p b k -> p (b k)")
                    did(v.tensor_scalar(selp[:, 0, :], flat, 4, None, ALU.logical_shift_right))
                    did(v.tensor_scalar(selp[:, 1, :], flat, 15, None, ALU.bitwise_and))
                    settle()
                    did(v.tensor_copy(selpf, selp))
                    for u in range(2):
                        settle()
                        did(v.tensor_tensor(eq, selpf[:, u, :].unsqueeze(2).broadcast_to([P, 80, 16]),
                                            const[:, C_IOTA:C_IOTA + 16].unsqueeze(1).broadcast_to([P, 80, 16]), ALU.is_equal))
                        settle()
                        did(v.tensor_tensor(picked.rearrange("p (b k) i -> p b k i", b=5),
                                            eq.rearrange("p (b k) i -> p b k i", b=5),
                                            idxf[:, :, u, :].unsqueeze(2).broadcast_to([P, 5, 16, 16]), ALU.mult))
                        settle()
                        did(v.tensor_reduce(pick[:, u, :], picked, AX.X, ALU.add))
                    settle()
                    pk = pick.rearrange("p u (b k) -> p u b k", b=5)
                    did(v.scalar_tensor_tensor(eid[:, 0:SEQ].rearrange("p (b m) -> p b m", b=TB)[:, :, bass.ds(head * 16, 16)],
                                               pk[:, 0, 0:TB], float(NK), pk[:, 1, 0:TB], ALU.mult, ALU.add))
                    did(v.scalar_tensor_tensor(eidS[0:NS, bass.ds(head * 16, 16)], pk[0:NS, 0, TB], float(NK),
                                               pk[0:NS, 1, TB], ALU.mult, ALU.add))
                    v.wait_ge(s_gexp, head + 1)
                    did(v.tensor_reduce(gsum, gexp, AX.X, ALU.add))
                    settle()
                    did(v.reciprocal(gsum, gsum))
                    settle()
                    did(v.tensor_tensor(gate[:, 0:SEQ].rearrange("p (b m) -> p b m", b=TB)[:, :, bass.ds(head * 16, 16)],
                                        gexp[:, 0:TB], gsum[:, 0:TB].unsqueeze(2).broadcast_to([P, TB, 16]), ALU.mult))
                    did(v.tensor_tensor(gateS[0:NS, bass.ds(head * 16, 16)], gexp[0:NS, TB],
                                        gsum[0:NS, TB:TB + 1].broadcast_to([NS, 16]), ALU.mult))
                    settle()
                for g in range(4):
                    for src, dst in ((eidS, eid), (gateS, gate)):
                        did(v.tensor_copy(dst[NS * g:NS * (g + 1), SEQ:T], src[0:NS, NS * g:NS * (g + 1)]))

        RING = 8
        TURNS = SLOTS // RING
        S_TURNS = SLOTS // 4 // RING
        EARLY = 2
        V0 = EARLY * TURNS
        LATE = T - EARLY * P
        NX = NK * NK
        CH = NX // P
        ring = [at(s * D, D) for s in range(RING)]
        gfb = at(27968, D)
        Xn = at(30016, D)
        Un = at(32064, 4 * D, "p (s n) -> p s n", s=4)
        Sb = at(40256, 2 * LATE, "p (s t) -> p s t", s=2)
        acts = at(40832, T)
        gl = at(41376, T)
        eidx = at(41920, LATE).bitcast(I32)
        xnB = at(42496, DC * LATE, "p (k t) -> p k t", k=DC)
        UT = at(47104, 2 * D, "p (s k e) -> p s k e", s=2, k=DC)
        junk2 = at(47104, D)
        stage = at(51200, RING).bitcast(I32)
        stage_e = at(51208, RING).bitcast(I32)
        el8 = at(51216, RING)
        act8 = at(51224, RING)
        fsq = at(51232, 5)
        frs = at(51240, 5)
        eps = at(51248, 1)
        products = nc.dram_tensor("late_products", (NX, LATE), F32, kind="Internal").ap()
        one_by_one = products.rearrange("e t -> (e t)").unsqueeze(1)
        s_g2, s_gf, s_xnB, s_eidx, s_eps = (sem("norm2_gain_in"), sem("final_gain_in"), sem("late_x_ready"),
                                            sem("product_places"), sem("eps_set"))
        s_in = [sem(f"row_slot{s}_in") for s in range(RING)]
        s_used, s_staged = sem("rows_used"), sem("rows_staged")
        s_un = [sem(f"u_chunk{s}_in") for s in range(4)]
        s_ut, s_ute, s_pr, s_pre = sem("u_transposed"), sem("u_T_sbuf"), sem("products"), sem("products_sbuf")
        s_st = [sem(f"products_stored{s}") for s in range(2)]
        s_all = sem("all_products_stored")
        s_es, s_el, s_elc = sem("places_staged"), sem("product_gathered"), sem("product_taken")
        s_act, s_gelu, s_coef = sem("acts"), sem("gelu"), sem("coefs")
        s_vd, s_root2, s_y, s_sum = sem("block_summed"), sem("y_root"), sem("y_ready"), sem("samples_summed")

        with nc.Block() as block:
            @block.sync
            def _(sp_):
                u_chunks = io["peer_u"][0].rearrange("(c p) n -> p c n", p=P)
                out_chunks = products.rearrange("(c p) t -> p c t", p=P)
                sp_.dma_start(gfb, io["norm2_g"][0].partition_broadcast(P)).then_inc(s_g2, 16)
                sp_.wait_ge(s_xnB, 1)
                for a in range(4):
                    sp_.dma_start(Un[:, a, :], u_chunks[:, a, :]).then_inc(s_un[a], 16)
                with sp_.Fori(0, CH // 4 - 1) as i:
                    for a in range(4):
                        wait_apart(sp_, s_ut, i * 16 + (4 * a + 4))
                        sp_.dma_start(Un[:, a:a + 1, :], u_chunks[:, bass.ds(i * 4 + (a + 4), 1), :]).then_inc(s_un[a], 16)
                        wait_apart(sp_, s_pre, i * 4 + (a + 3))
                        sp_.dma_start(out_chunks[:, bass.ds(i * 4 + a, 1), :], Sb[:, a % 2:a % 2 + 1, :]
                                      ).then_inc(s_st[a % 2], 16)
                for e in range(CH - 4, CH):
                    sp_.wait_ge(s_pre, e + 3)
                    sp_.dma_start(out_chunks[:, e, :], Sb[:, e % 2, :]).then_inc(s_st[e % 2], 16)
                for a in range(2):
                    sp_.wait_ge(s_st[a], 16 + 16 * CH // 2)
                sp_.sem_inc(s_all, 1)
                yp = io["y_prompt"][0].rearrange("(b p) d -> b p d", p=P)
                for b in range(TB + 1):
                    sp_.wait_ge(s_y, b + 1)
                    store(sp_, yp[b] if b < TB else io["y_sample"].rearrange("b t d -> (b t) d"), h[:rows(b), b, :])
                sp_.wait_ge(out_done, 16 * outs[0])

            @block.gpsimd
            def _(g_):
                g_.sem_inc(s_used, RING)

                def gather(table, turn_no, first):
                    for q in range(RING // 4):
                        wait_apart(g_, s_used, turn_no * RING + (4 * q + 4))
                        g_.tensor_copy(stage[:, 4 * q:4 * q + 4], eid[:, bass.ds(first + 4 * q, 4)]).then_inc(s_staged, 1)
                        wait_apart(g_, s_staged, turn_no * 2 + (q + 1))
                        for s in range(4 * q, 4 * q + 4):
                            g_.indirect_dma_start(ring[s], None, table,
                                                  bass.IndirectOffsetOnAxis(ap=stage[:, s:s + 1], axis=0)
                                                  ).then_inc(s_in[s], 16)

                def gather_products(j):
                    wait_apart(g_, s_elc, j + 1)
                    g_.tensor_copy(stage_e, eidx[:, bass.ds(j * RING, RING)]).then_inc(s_es, 1)
                    wait_apart(g_, s_es, j + 1)
                    for s in range(RING):
                        g_.indirect_dma_start(el8[:, s:s + 1], None, one_by_one,
                                              bass.IndirectOffsetOnAxis(ap=stage_e[:, s:s + 1], axis=0)).then_inc(s_el, 16)

                u_rows, v_rows = io["peer_u"][0], io["peer_v"][0]
                with g_.Fori(0, V0) as i:
                    gather(u_rows, i, i * RING)
                with g_.Fori(0, TURNS) as i:
                    gather(v_rows, i + V0, i * RING)
                g_.sem_inc(s_elc, 1)
                g_.wait_ge(s_eidx, 1)
                g_.wait_ge(s_all, 1)
                with g_.Fori(0, LATE // RING) as i:
                    gather(v_rows, i + (V0 + TURNS), (i + TURNS) * RING)
                    gather_products(i)
                with g_.Fori(LATE // RING + TURNS, TB * TURNS + S_TURNS) as i:
                    gather(v_rows, i + V0, i * RING)

            @block.vector
            def _(v):
                def dots(b):
                    steps_v.did(v.scalar_tensor_tensor(Xn, h[:, b, :], rstd[:, b:b + 1], gfb, ALU.mult, ALU.mult))
                    steps_v.settle()
                    with steps_v.loop(TURNS, 1) as i:
                        for s in range(RING):
                            v.wait_ge(s_in[s], i * 16 + (16 * TURNS * b + 16))
                            v.tensor_tensor_reduce(ring[s], ring[s], Xn, 1.0, 0.0, ALU.mult, ALU.add,
                                                   act8[:, s:s + 1]).then_inc(s_used, 1)
                        wait_apart(v, s_used, i * RING + (SLOTS * b + 2 * RING))
                        steps_v.did(v.tensor_copy(acts[:, bass.ds(i * RING + SLOTS * b, RING)], act8))
                        settle_apart(steps_v)
                    v.sem_inc(s_act, 1)

                def coefs(b):
                    cols = slice(SLOTS * b, SLOTS * b + SLOTS if b < TB else T)
                    v.wait_ge(s_gelu, b + 1)
                    steps_v.did(v.tensor_tensor(gl[:, cols], gl[:, cols], gate[:, cols], ALU.mult))
                    steps_v.settle()

                def weigh(dst, first, trips, products_too):
                    with v.Fori(first, first + trips) as i:
                        for s in range(RING):
                            v.wait_ge(s_in[s], i * 16 + (16 * V0 + 16))
                            v.wait_ge(s_used, i * RING + (RING * V0 + s + RING))
                            v.scalar_tensor_tensor(dst, ring[s], gl[:, bass.ds(i * RING + s, 1)], dst, ALU.mult,
                                                   ALU.add).then_inc(s_used, 1)
                        if products_too:
                            wait_apart(v, s_el, (i - TURNS) * (16 * RING) + 16 * RING)
                            v.tensor_copy(acts[:, bass.ds(i * RING + RING * TURNS, RING)], el8).then_inc(s_elc, 1)
                            wait_apart(v, s_elc, i - (TURNS - 2))
                    v.wait_ge(s_used, RING * (V0 + first + trips + 1))

                def finish(b):
                    np_ = rows(b)
                    v.wait_ge(s_root2, b + 1)
                    steps_v.did(v.reciprocal(frs[0:np_, b:b + 1], frs[0:np_, b:b + 1]))
                    steps_v.settle()
                    src = h[:, b, :] if b < TB else PS[0:np_, 0:4, :].rearrange("p a n -> p (a n)")
                    v.scalar_tensor_tensor(h[0:np_, b, :], src, frs[0:np_, b:b + 1], gfb[0:np_],
                                           ALU.mult, ALU.mult).then_inc(s_y, 1)

                v.memset(eps, EPS).then_inc(s_eps, 1)
                v.wait_ge(s_g2, 16)
                v.wait_ge(s_xnB, 1)
                for k in range(3):
                    cols = slice(SLOTS * k, min(SLOTS * (k + 1), LATE))
                    ins = v.tensor_scalar(eidx[:, cols], eid[:, EARLY * P:T][:, cols], float(LATE),
                                          const[:, C_TOK + k:C_TOK + k + 1], ALU.mult, ALU.add)
                ins.then_inc(s_eidx, 1)
                for b in range(EARLY):
                    dots(b)
                steps_v.did(v.memset(Xn, 0.0))
                coefs(0)
                coefs(1)
                weigh(h[:, 0, :], 0, TURNS, False)
                v.sem_inc(s_vd, 1)
                v.wait_ge(s_gf, 16)
                for b in range(1, TB):
                    if b == TB - 1:
                        weigh(h[:, b, :], b * TURNS, S_TURNS, True)
                        v.sem_inc(s_act, 1)
                        weigh(h[:, b, :], b * TURNS + S_TURNS, TURNS - S_TURNS, False)
                    else:
                        weigh(h[:, b, :], b * TURNS, TURNS, True)
                        v.sem_inc(s_act, 1)
                    v.sem_inc(s_vd, 1)
                    coefs(b + 1)
                    finish(b - 1)
                weigh(Xn, TB * TURNS, S_TURNS, False)
                v.sem_inc(s_vd, 1)
                finish(TB - 1)
                finish(TB)

            @block.scalar
            def _(act):
                def take_u(turn_no, a):
                    act.wait_ge(s_pr, turn_no * 4 + (a + 1))
                    for q in range(4):
                        act.wait_ge(s_ut, turn_no * 16 + (4 * a + q + 1))
                        act.activation(UT[:, a % 2, 4 * q:4 * q + 4, :],
                                       PS[:, q, :].rearrange("p (k e) -> p k e", k=4), ACT.Copy).then_inc(s_ute, 1)

                def take_products(turn_no, a):
                    act.wait_ge(s_pr, turn_no * 4 + (a + 3))
                    act.wait_ge(s_st[a % 2], turn_no * 32 + (16 * (a // 2) + 16))
                    act.activation(Sb[:, a % 2, :], PS[:, 4 + a % 2, 0:LATE], ACT.Copy).then_inc(s_pre, 1)

                def chunks(first, end):
                    with act.Fori(first, end) as i:
                        for a in range(4):
                            take_u(i, a + 1)
                            take_products(i, a)

                def gelu(b):
                    cols = slice(SLOTS * b, SLOTS * b + SLOTS if b < TB else T)
                    act.wait_ge(s_act, b + 1)
                    act.activation(gl[:, cols], acts[:, cols], ACT.Gelu).then_inc(s_gelu, 1)

                def root(b):
                    np_ = rows(b)
                    if b < TB:
                        act.wait_ge(s_vd, b + 1)
                        src = h[:, b, :]
                    else:
                        act.wait_ge(s_sum, 1)
                        src = PS[0:np_, 0:4, :].rearrange("p a n -> p (a n)")
                    if b:
                        act.wait_ge(s_root2, b)
                    act.activation(junk2[0:np_], src, ACT.Square, accum_out=fsq[0:np_, b:b + 1]).then_inc(s_coef, 1)
                    act.wait_ge(s_coef, b + 1)
                    act.activation(frs[0:np_, b:b + 1], fsq[0:np_, b:b + 1], ACT.Sqrt, bias=eps[0:np_],
                                   scale=1.0 / D).then_inc(s_root2, 1)

                act.activation(xnB, xn2T[:, :, EARLY * P:T], ACT.Copy).then_inc(s_xnB, 1)
                act.sem_inc(s_pr, 2)
                act.sem_inc(s_pre, 2)
                for a in range(2):
                    act.sem_inc(s_st[a], 16)
                take_u(0, 0)
                turns = CH // 4 - 1
                at_0, at_1 = turns * 14 // 31, turns * 28 // 31
                chunks(0, at_0)
                gelu(0)
                chunks(at_0, at_1)
                gelu(1)
                act.dma_start(gfb, io["final_g"].partition_broadcast(P)).then_inc(s_gf, 16)
                chunks(at_1, turns)
                for a in range(4):
                    if a < 3:
                        take_u(turns, a + 1)
                    take_products(turns, a)
                act.wait_ge(s_eps, 1)
                root(0)
                gelu(2)
                root(1)
                gelu(3)
                root(2)
                gelu(4)
                root(3)
                root(4)

            @block.tensor
            def _(pe):
                def turn_u(turn_no, a):
                    pe.wait_ge(s_un[a % 4], turn_no * 16 + (16 * (a // 4) + 16))
                    for q in range(4):
                        if not (isinstance(turn_no, int) and turn_no == 0 and a == 0):
                            pe.wait_ge(s_ute, turn_no * 16 + (4 * (a - 1) + q + 1))
                        for j in range(4):
                            ins = pe.transpose(PS[:, q, j * P:(j + 1) * P],
                                               Un[:, a % 4, (4 * q + j) * P:(4 * q + j + 1) * P], ident)
                        ins.then_inc(s_ut, 1)

                def multiply(turn_no, a):
                    pe.wait_ge(s_ute, turn_no * 16 + (4 * a + 4))
                    pe.wait_ge(s_pre, turn_no * 4 + (a + 1))
                    for d in range(DC):
                        ins = pe.matmul(PS[:, 4 + a % 2, 0:LATE], UT[:, a % 2, d, :], xnB[:, d, :],
                                        start=d == 0, stop=d == DC - 1)
                    ins.then_inc(s_pr, 1)

                pe.wait_ge(s_xnB, 1)
                turn_u(0, 0)
                with pe.Fori(0, CH // 4 - 1) as i:
                    for a in range(4):
                        turn_u(i, a + 1)
                        multiply(i, a)
                for a in range(4):
                    if a < 3:
                        turn_u(CH // 4 - 1, a + 1)
                    multiply(CH // 4 - 1, a)
                pe.wait_ge(s_vd, TB + 1)
                for n in range(4):
                    cols = slice(512 * n, 512 * (n + 1))
                    pe.matmul(PS[0:NS, n, :], const[:, C_REP:C_REP + NS], Xn[:, cols], start=True, stop=False)
                    ins = pe.matmul(PS[0:NS, n, :], ident[0:NS, 0:NS], h[0:NS, TB, cols], start=False, stop=True)
                ins.then_inc(s_sum, 1)


_INS = ['x_prompt', 'x_sample', 'cache_k', 'cache_v', 'state_conv', 'state_h', 'page_table', 'norm1_g', 'w_in',
        'lambda_q1', 'lambda_k1', 'lambda_q2', 'lambda_k2', 'subln_g', 'conv_w', 'conv_b', 'lru_wa', 'lru_ba',
        'lru_wx', 'lru_bx', 'lru_lambda', 'w_att_up', 'w_lru_up', 'w_out', 'norm2_g', 'peer_wq', 'peer_k1',
        'peer_k2', 'peer_u', 'peer_v', 'final_g']
_OUTS = {'y_prompt': (1, SEQ, D), 'y_sample': (NB, NT, D), 'k_prompt': (1, 1, SEQ, NG, P), 'v_prompt': (1, 1, SEQ, NG, P),
         'conv_prompt': (1, 1, CW - 1, LW), 'h_prompt': (1, 1, LW), 'k_sample': (1, NB, NT, NG, P),
         'v_sample': (1, NB, NT, NG, P), 'conv_sample': (1, NB, CW - 1, LW), 'h_sample': (1, NB, LW)}


def kernel(**inputs):
    import concourse.bacc as _bacc
    from concourse.bass_utils import run_bass_kernel_spmd as _run

    nc = _bacc.Bacc("TRN2", target_bir_lowering=False, num_devices=1)
    arrays, io = {}, {}
    for name in _INS + ['const']:
        a = np.ascontiguousarray(inputs[name]) if name != 'const' else shape_constants()
        arrays[f"in_{name}_dram"] = a
        io[name] = nc.dram_tensor(f"in_{name}_dram", a.shape, mybir.dt.from_np(a.dtype), kind="ExternalInput").ap()
    for name, shape in _OUTS.items():
        io[name] = nc.dram_tensor(f"out_{name}_dram", shape, F32, kind="ExternalOutput").ap()
    build_trunk(nc, io)
    r = _run(nc, [arrays], core_ids=[0])
    return tuple(r.results[0][f"out_{name}_dram"] for name in _OUTS)
```
